# Optimizing a Trainium2 kernel written in Bass

```python
import math
import jax
import jax.numpy as jnp
from jax import lax
import numpy as np

D_MODEL = 1024
BATCH = 1
SEQ = 1024
DEPTH = 2

ROPE_THETA = 500000.0
EPS = 1e-6
Q_BLOCK = 128
D_FF = 4 * D_MODEL
POS_OFFSET_MAX = 4096
NEG = -1e30
FORCED = 1e9
N_EVEN = (DEPTH + 1) // 2
N_ODD = DEPTH // 2

MLA_HEADS = 8
MLA_NOPE = 64
MLA_ROPE = 32
MLA_V = 64
MLA_Q_RANK = 256
MLA_KV_RANK = 256

NSA_HEADS = 8
NSA_GROUPS = 2
NSA_HPG = NSA_HEADS // NSA_GROUPS
NSA_DH = 64
NSA_ROT = NSA_DH // 4
NSA_CMP_LEN = 32
NSA_CMP_STRIDE = 16
NSA_CMP_HIDDEN = 128
NSA_SLC_LEN = 64
NSA_TOP_N = 16
NSA_WINDOW = 512
NSA_SLC_Q_BLOCK = 64

DIFF_HEADS = 8
DIFF_DH = 64
DIFF_ROT = DIFF_DH // 4

MLA_IN = MLA_Q_RANK + MLA_KV_RANK + MLA_ROPE
NSA_Q_W = NSA_HEADS * NSA_DH
NSA_KV_W = 3 * 2 * NSA_GROUPS * NSA_DH
NSA_GATE_W = 3 * NSA_HEADS
HY_IN = MLA_IN + NSA_Q_W + NSA_KV_W + NSA_GATE_W
HY_OUT = MLA_HEADS * MLA_V + NSA_HEADS * NSA_DH
HY_SPLITS = [MLA_Q_RANK, MLA_Q_RANK + MLA_KV_RANK, MLA_IN, MLA_IN + NSA_Q_W, MLA_IN + NSA_Q_W + NSA_KV_W]
DIFF_W = DIFF_HEADS * 2 * DIFF_DH

kernel_name = "hybrid_mla_nsa_diffattn_trunk"

def _rms(x, gain):
    xf = x.astype(jnp.float32)
    y = xf * lax.rsqrt(jnp.mean(xf * xf, axis=-1, keepdims=True) + EPS)
    return (y * gain.astype(jnp.float32)).astype(x.dtype)

def _rope(x, pos, rot):
    half = rot // 2
    inv_freq = ROPE_THETA ** (-jnp.arange(half, dtype=jnp.float32) / half)
    ang = pos.astype(jnp.float32)[..., None] * inv_freq
    cos, sin = jnp.cos(ang), jnp.sin(ang)
    xr = x[..., :rot].astype(jnp.float32)
    x1, x2 = xr[..., :half], xr[..., half:]
    xr = jnp.concatenate([x1 * cos - x2 * sin, x1 * sin + x2 * cos], axis=-1)
    return jnp.concatenate([xr.astype(x.dtype), x[..., rot:]], axis=-1)

def _causal_attention(q, k, v, map_w, scale):
    B, H, M, S, dk = q.shape
    dv = v.shape[-1]
    nb = S // Q_BLOCK
    qb = jnp.moveaxis(q.reshape(B, H, M, nb, Q_BLOCK, dk), 3, 0)
    kpos = jnp.arange(S)
    wf = map_w.astype(jnp.float32)

    def one(args):
        qblk, s0 = args
        s = jnp.einsum('bhmqd,bhmkd->bhmqk', qblk, k, preferred_element_type=jnp.float32) * scale
        mask = kpos[None, :] <= (s0 + jnp.arange(Q_BLOCK))[:, None]
        p = jax.nn.softmax(jnp.where(mask, s, NEG), axis=-1)
        a = jnp.einsum('m,bhmqk->bhqk', wf, p)
        return jnp.einsum('bhqk,bhkd->bhqd', a.astype(v.dtype), v)

    o = lax.map(one, (qb, jnp.arange(nb) * Q_BLOCK))
    return jnp.moveaxis(o, 0, 2).reshape(B, H, S, dv)

def _mla_mixer(cq_raw, ckv_raw, kpe_raw, pos, q_norm, w_uq, kv_norm, w_ukv, q_gain, k_gain):
    B, S, _ = cq_raw.shape
    H = MLA_HEADS
    q = (_rms(cq_raw, q_norm) @ w_uq).reshape(B, S, H, MLA_ROPE + MLA_NOPE).transpose(0, 2, 1, 3)
    kv = (_rms(ckv_raw, kv_norm) @ w_ukv).reshape(B, S, H, MLA_NOPE + MLA_V).transpose(0, 2, 1, 3)
    k_nope, v = kv[..., :MLA_NOPE], kv[..., MLA_NOPE:]
    k_pe = jnp.broadcast_to(kpe_raw[:, None], (B, H, S, MLA_ROPE))
    k = jnp.concatenate([k_pe, k_nope], axis=-1)
    p = pos[:, None, :]
    q = _rope(_rms(q, q_gain), p, MLA_ROPE)
    k = _rope(_rms(k, k_gain), p, MLA_ROPE)
    o = _causal_attention(q[:, :, None], k[:, :, None], v, jnp.ones((1,), jnp.float32),
                          (MLA_ROPE + MLA_NOPE) ** -0.5)
    return o.transpose(0, 2, 1, 3).reshape(B, S, H * MLA_V)

def _nsa_mixer(q_raw, kv_raw, gate_raw, pos, q_gain, k_gain, cmp_pos, cmp_w1, cmp_w2):
    B, S, _ = q_raw.shape
    G, HG, DH = NSA_GROUPS, NSA_HPG, NSA_DH
    scale = DH ** -0.5
    tpos = jnp.arange(S)
    q = q_raw.reshape(B, S, G, HG, DH).transpose(0, 2, 3, 1, 4)
    q = _rope(_rms(q, q_gain), pos[:, None, None, :], NSA_ROT)
    kv = kv_raw.reshape(B, S, 3, 2, G, DH).transpose(2, 3, 0, 4, 1, 5)

    nc = (S - NSA_CMP_LEN) // NSA_CMP_STRIDE + 1
    c_start = jnp.arange(nc) * NSA_CMP_STRIDE
    c_end = c_start + NSA_CMP_LEN - 1
    blk_idx = c_start[:, None] + jnp.arange(NSA_CMP_LEN)[None, :]

    def compress(tok, j):
        blocks = (tok[:, :, blk_idx] + cmp_pos[j]).reshape(B, G, nc, NSA_CMP_LEN * DH)
        return jax.nn.gelu(blocks @ cmp_w1[j]) @ cmp_w2[j]

    kc = _rope(_rms(compress(kv[0, 0], 0), k_gain[0]), pos[:, c_end][:, None, :], NSA_ROT)
    vc = compress(kv[0, 1], 1)
    s = jnp.einsum('bghqd,bgcd->bghqc', q, kc, preferred_element_type=jnp.float32) * scale
    cmask = c_end[None, :] <= tpos[:, None]
    p_cmp = jax.nn.softmax(jnp.where(cmask, s, NEG), axis=-1) * cmask
    o_cmp = jnp.einsum('bghqc,bgcd->bghqd', p_cmp.astype(vc.dtype), vc)

    ns = S // NSA_SLC_LEN
    n_sel = min(NSA_TOP_N, ns)
    j_start = jnp.arange(ns) * NSA_SLC_LEN
    cover = ((c_start[:, None] <= j_start[None, :] + NSA_SLC_LEN - 1)
             & (c_end[:, None] >= j_start[None, :])).astype(jnp.float32)
    imp = jnp.einsum('bghqc,cj->bgqj', p_cmp, cover)
    jt = tpos // NSA_SLC_LEN
    jj = jnp.arange(ns)
    allowed = jj[None, :] <= jt[:, None]
    forced = allowed & ((jj[None, :] == 0) | (jj[None, :] >= jt[:, None] - 1))
    imp = jnp.where(forced, FORCED, jnp.where(allowed, imp, NEG))
    top_val, top_idx = lax.top_k(imp, n_sel)
    top_ok = top_val > 0.5 * NEG
    ks = _rope(_rms(kv[1, 0], k_gain[1]), pos[:, None, :], NSA_ROT)
    k_blk = ks.reshape(B, G, ns, NSA_SLC_LEN, DH)
    v_blk = kv[1, 1].reshape(B, G, ns, NSA_SLC_LEN, DH)
    bi = jnp.arange(B)[:, None, None, None]
    gi = jnp.arange(G)[None, :, None, None]
    qb_n = NSA_SLC_Q_BLOCK

    def sel_block(args):
        qb, ib, okb, s0 = args
        kg = k_blk[bi, gi, ib]
        vg = v_blk[bi, gi, ib]
        sc = jnp.einsum('bghqd,bgqnld->bghqnl', qb, kg, preferred_element_type=jnp.float32) * scale
        qpos = s0 + jnp.arange(qb_n)
        kpos = ib[..., None] * NSA_SLC_LEN + jnp.arange(NSA_SLC_LEN)
        m = ((kpos <= qpos[:, None, None]) & okb[..., None])[:, :, None]
        sc = jnp.where(m, sc, NEG).reshape(B, G, HG, qb_n, n_sel * NSA_SLC_LEN)
        pr = jax.nn.softmax(sc, axis=-1).reshape(B, G, HG, qb_n, n_sel, NSA_SLC_LEN) * m
        return jnp.einsum('bghqnl,bgqnld->bghqd', pr.astype(vg.dtype), vg)

    nqb = S // qb_n
    o_slc = lax.map(sel_block, (
        jnp.moveaxis(q.reshape(B, G, HG, nqb, qb_n, DH), 3, 0),
        jnp.moveaxis(top_idx.reshape(B, G, nqb, qb_n, n_sel), 2, 0),
        jnp.moveaxis(top_ok.reshape(B, G, nqb, qb_n, n_sel), 2, 0),
        jnp.arange(nqb) * qb_n))
    o_slc = jnp.moveaxis(o_slc, 0, 3).reshape(B, G, HG, S, DH)

    kw = _rope(_rms(kv[2, 0], k_gain[2]), pos[:, None, :], NSA_ROT)
    pad = ((0, 0), (0, 0), (NSA_WINDOW, 0), (0, 0))
    kp, vp = jnp.pad(kw, pad), jnp.pad(kv[2, 1], pad)
    span = NSA_WINDOW + Q_BLOCK

    def win_block(args):
        qb, s0 = args
        kb = lax.dynamic_slice_in_dim(kp, s0, span, axis=2)
        vb = lax.dynamic_slice_in_dim(vp, s0, span, axis=2)
        sc = jnp.einsum('bghqd,bgkd->bghqk', qb, kb, preferred_element_type=jnp.float32) * scale
        qpos = (s0 + jnp.arange(Q_BLOCK))[:, None]
        kpos = (s0 - NSA_WINDOW + jnp.arange(span))[None, :]
        m = (kpos <= qpos) & (kpos > qpos - NSA_WINDOW) & (kpos >= 0)
        pr = jax.nn.softmax(jnp.where(m, sc, NEG), axis=-1)
        return jnp.einsum('bghqk,bgkd->bghqd', pr.astype(vb.dtype), vb)

    nb = S // Q_BLOCK
    o_win = lax.map(win_block, (jnp.moveaxis(q.reshape(B, G, HG, nb, Q_BLOCK, DH), 3, 0),
                                jnp.arange(nb) * Q_BLOCK))
    o_win = jnp.moveaxis(o_win, 0, 3).reshape(B, G, HG, S, DH)

    g = jax.nn.sigmoid(gate_raw).reshape(B, S, 3, G, HG).transpose(2, 0, 3, 4, 1)[..., None]
    o = g[0] * o_cmp.astype(g.dtype) + g[1] * o_slc.astype(g.dtype) + g[2] * o_win.astype(g.dtype)
    return o.transpose(0, 3, 1, 2, 4).reshape(B, S, NSA_HEADS * DH)

def _diff_mixer(h, w_qkv, w_out, q_gain, k_gain, lam, sub_gain, pos, lam_init):
    B, S, _ = h.shape
    H, d = DIFF_HEADS, DIFF_DH
    q, k, v = jnp.split(h @ w_qkv, 3, axis=-1)
    q = q.reshape(B, S, H, 2, d).transpose(0, 2, 3, 1, 4)
    k = k.reshape(B, S, H, 2, d).transpose(0, 2, 3, 1, 4)
    v = v.reshape(B, S, H, 2 * d).transpose(0, 2, 1, 3)
    p = pos[:, None, None, :]
    q = _rope(_rms(q, q_gain), p, DIFF_ROT)
    k = _rope(_rms(k, k_gain), p, DIFF_ROT)
    lf = lam.astype(jnp.float32)
    lmb = jnp.exp(jnp.sum(lf[0] * lf[1])) - jnp.exp(jnp.sum(lf[2] * lf[3])) + lam_init
    o = _causal_attention(q, k, v, jnp.stack([jnp.ones_like(lmb), -lmb]), d ** -0.5)
    o = _rms(o, sub_gain) * (1.0 - lam_init)
    return o.transpose(0, 2, 1, 3).reshape(B, S, DIFF_W) @ w_out

def setup_inputs(seed: int = 0) -> dict:
    key = jax.random.key(seed)
    ks = jax.random.split(key, 28)
    f32 = jnp.float32
    D = D_MODEL

    def nrm(k, shape, scale):
        return jax.random.normal(k, shape, f32) * scale

    def gain(k, shape):
        return 1.0 + 0.02 * jax.random.normal(k, shape, f32)

    positions = (jax.random.randint(ks[2], (BATCH, 1), 0, POS_OFFSET_MAX, dtype=jnp.int32)
                 + jnp.arange(SEQ, dtype=jnp.int32)[None, :])
    return {
        "x": nrm(ks[0], (BATCH, SEQ, D), 1.0),
        "c": nrm(ks[1], (BATCH, D), 1.0),
        "positions": positions,
        "ada_w": nrm(ks[3], (DEPTH, D, 6 * D), 0.5 * D ** -0.5),
        "ada_b": nrm(ks[4], (DEPTH, 6 * D), 0.02),
        "norm_mix": gain(ks[5], (DEPTH, D)),
        "norm_mlp": gain(ks[6], (DEPTH, D)),
        "mlp_w1": nrm(ks[7], (DEPTH, D, D_FF), D ** -0.5),
        "mlp_w2": nrm(ks[8], (DEPTH, D_FF, D), D_FF ** -0.5),
        "hy_w_in": nrm(ks[9], (N_EVEN, D, HY_IN), D ** -0.5),
        "hy_w_out": nrm(ks[10], (N_EVEN, HY_OUT, D), HY_OUT ** -0.5),
        "mla_q_norm": gain(ks[11], (N_EVEN, MLA_Q_RANK)),
        "mla_w_uq": nrm(ks[12], (N_EVEN, MLA_Q_RANK, MLA_HEADS * (MLA_ROPE + MLA_NOPE)), MLA_Q_RANK ** -0.5),
        "mla_kv_norm": gain(ks[13], (N_EVEN, MLA_KV_RANK)),
        "mla_w_ukv": nrm(ks[14], (N_EVEN, MLA_KV_RANK, MLA_HEADS * (MLA_NOPE + MLA_V)), MLA_KV_RANK ** -0.5),
        "mla_q_gain": gain(ks[15], (N_EVEN, MLA_ROPE + MLA_NOPE)),
        "mla_k_gain": gain(ks[16], (N_EVEN, MLA_ROPE + MLA_NOPE)),
        "nsa_q_gain": gain(ks[17], (N_EVEN, NSA_DH)),
        "nsa_k_gain": gain(ks[18], (N_EVEN, 3, NSA_DH)),
        "nsa_cmp_pos": nrm(ks[19], (N_EVEN, 2, NSA_CMP_LEN, NSA_DH), 0.1),
        "nsa_cmp_w1": nrm(ks[20], (N_EVEN, 2, NSA_CMP_LEN * NSA_DH, NSA_CMP_HIDDEN), (NSA_CMP_LEN * NSA_DH) ** -0.5),
        "nsa_cmp_w2": nrm(ks[21], (N_EVEN, 2, NSA_CMP_HIDDEN, NSA_DH), NSA_CMP_HIDDEN ** -0.5),
        "diff_w_qkv": nrm(ks[22], (N_ODD, D, 3 * DIFF_W), D ** -0.5),
        "diff_w_out": nrm(ks[23], (N_ODD, DIFF_W, D), DIFF_W ** -0.5),
        "diff_q_gain": gain(ks[24], (N_ODD, DIFF_DH)),
        "diff_k_gain": gain(ks[25], (N_ODD, DIFF_DH)),
        "diff_lambda": nrm(ks[26], (N_ODD, 4, DIFF_DH), 0.1),
        "diff_sub_gain": gain(ks[27], (N_ODD, 2 * DIFF_DH)),
    }

def reference(x, c, positions, ada_w, ada_b, norm_mix, norm_mlp, mlp_w1, mlp_w2,
              hy_w_in, hy_w_out, mla_q_norm, mla_w_uq, mla_kv_norm, mla_w_ukv, mla_q_gain, mla_k_gain,
              nsa_q_gain, nsa_k_gain, nsa_cmp_pos, nsa_cmp_w1, nsa_cmp_w2,
              diff_w_qkv, diff_w_out, diff_q_gain, diff_k_gain, diff_lambda, diff_sub_gain):
    cond = jax.nn.silu(c)
    for i in range(DEPTH):
        mod = (cond @ ada_w[i] + ada_b[i])[:, None, :]
        sh1, sc1, g1, sh2, sc2, g2 = jnp.split(mod, 6, axis=-1)
        h = _rms(x, norm_mix[i]) * (1 + sc1) + sh1
        j = i // 2
        if i % 2 == 0:
            u = h @ hy_w_in[j]
            cq, ckv, kpe, nq, nkv, ngate = jnp.split(u, HY_SPLITS, axis=-1)
            y_mla = _mla_mixer(cq, ckv, kpe, positions, mla_q_norm[j], mla_w_uq[j], mla_kv_norm[j],
                               mla_w_ukv[j], mla_q_gain[j], mla_k_gain[j])
            y_nsa = _nsa_mixer(nq, nkv, ngate, positions, nsa_q_gain[j], nsa_k_gain[j],
                               nsa_cmp_pos[j], nsa_cmp_w1[j], nsa_cmp_w2[j])
            y = jnp.concatenate([y_mla, y_nsa.astype(y_mla.dtype)], axis=-1) @ hy_w_out[j]
        else:
            lam_init = 0.8 - 0.6 * math.exp(-0.3 * i)
            y = _diff_mixer(h, diff_w_qkv[j], diff_w_out[j], diff_q_gain[j], diff_k_gain[j],
                            diff_lambda[j], diff_sub_gain[j], positions, lam_init)
        x = x + g1 * y
        h = _rms(x, norm_mlp[i]) * (1 + sc2) + sh2
        x = x + g2 * (jnp.square(jax.nn.relu(h @ mlp_w1[i])) @ mlp_w2[i])
    return x


_drawn_inputs = setup_inputs


def setup_inputs(seed=0):
    import zlib

    import numpy as np

    out = dict(_drawn_inputs(seed))
    spreads = {}
    factors = {'norm_mix': 8.0,
     'norm_mlp': 4.407,
     'mla_q_norm': 8.0,
     'mla_kv_norm': 8.0,
     'mla_q_gain': 8.0,
     'mla_k_gain': 8.0,
     'nsa_q_gain': 8.0,
     'nsa_k_gain': 8.0,
     'nsa_cmp_pos': 8.0,
     'diff_q_gain': 8.0,
     'diff_k_gain': 8.0,
     'diff_lambda': 4.634,
     'diff_sub_gain': 8.0}
    for name, (base, spread) in spreads.items():
        noise = np.random.default_rng([zlib.crc32(name.encode()), seed]).standard_normal(out[name].shape)
        drawn = base * np.exp(spread * noise) if base else spread * noise
        out[name] = jnp.asarray(drawn.astype(out[name].dtype))
    for name, factor in factors.items():
        out[name] = (out[name] * factor).astype(out[name].dtype)
    return out
```

```python
import math
from contextlib import ExitStack

import numpy as np

import concourse.bass as bass
from concourse import mybir

F32 = mybir.dt.float32
F32R = mybir.dt.float32r
I32 = mybir.dt.int32
ACT = mybir.ActivationFunctionType
ALU = mybir.AluOpType
AX = mybir.AxisListType

P = 128
SEQ = 1024
T = SEQ // P
D = 1024
KD = D // P
DFF = 4096
NEG = -1e30
EPS = 1e-6
THETA = 500000.0

HEADS = 8
DH = 64
MLA_DH, MLA_ROPE, MLA_NOPE, MLA_V, RANK = 96, 32, 64, 64, 256
GROUPS, PER_GROUP = 2, 4
WINDOW_TILES = 512 // P
CMP = 64
LATENT_W = 2 * RANK
NQ0 = LATENT_W + MLA_ROPE
NKV0 = NQ0 + HEADS * DH
GATE0 = NKV0 + 768
HY_IN = GATE0 + 24

WCH = 2048
FFG = 256
FF_GROUPS = DFF // FFG
LAM_INIT = 0.8 - 0.6 * math.exp(-0.3)


class Count:

    def __init__(self, eng, sem):
        self.eng, self.sem, self.base, self.k, self.off = eng, sem, 0, 0, 0

    def enter(self, turn, per):
        self.base, self.k, self.off = self.base + self.k, 0, turn * per

    def leave(self, per, times):
        assert self.k == per, (self.k, per)
        self.base, self.k, self.off = self.base + per * times, 0, 0

    def mark(self, ins):
        self.k += 1
        ins.then_inc(self.sem, 1)

    def sync(self):
        self.eng.wait_ge(self.sem, self.off + (self.base + self.k))

    def link(self, ins):
        self.mark(ins)
        self.sync()


def trunk(nc, x, c, positions, ada_w, ada_b, norm_mix, norm_mlp, mlp_w1, mlp_w2, hy_w_in, hy_w_out,
          mla_q_norm, mla_w_uq, mla_kv_norm, mla_w_ukv, mla_q_gain, mla_k_gain, nsa_q_gain,
          nsa_k_gain, nsa_cmp_pos, nsa_cmp_w1, nsa_cmp_w2, diff_w_qkv, diff_w_out, diff_q_gain,
          diff_k_gain, diff_lambda, diff_sub_gain, out):
    ctx = ExitStack()
    with ctx:
        ctx.enter_context(nc.allow_non_contiguous_dma(reason="small vectors are loaded transposed"))

        def sb(name, shape, dt=F32):
            return ctx.enter_context(nc.sbuf_tensor(name, shape, dt))

        def sem(name):
            return ctx.enter_context(nc.semaphore(name))

        actT = sb("actT", [P, 2 * KD * SEQ], F32R)
        wts = sb("wts", [P, 2, 2, WCH], F32R)
        gT = sb("gT", [P, 2, FFG // P, SEQ], F32R)
        xres = sb("xres", [P, T * D])
        stage = sb("stage", [P, 2, WCH])
        arena = sb("arena", [P, 11264])
        gates = sb("gates", [P, 2, D])
        ident = sb("ident", [P, P])
        identr = sb("identr", [P, P], F32R)
        masks = sb("masks", [P, 2, P], F32R)
        cmask = sb("cmask", [P, 184], F32R)
        ones = sb("ones", [P, P])
        rope = sb("rope", [P, 2, T + 1, 24])
        post = sb("post", [P, T + 1])
        posi = sb("posi", [P, T + 1], I32)
        cond = sb("cond", [P, 2, KD])
        normv = sb("normv", [P, 4, KD])
        latv = sb("latv", [P, 4])
        modv = sb("modv", [P, 4, KD])
        gainq = sb("gainq", [P, 2, 96])
        gainh = sb("gainh", [P, 6, DH])
        gsub = sb("gsub", [P, 2 * DH])
        lams = sb("lams", [P, 8])
        small = sb("small", [P, 3, T * 8])
        rows = sb("rows", [P, 4, 32])
        gate3 = sb("gate3", [P, T, 24])
        kpe = sb("kpe", [P, T, MLA_ROPE])
        lamt = kpe[:, :, :].rearrange("p t n -> p (t n)").rearrange("p (a n) -> p a n", a=4)
        kcv = arena[:, 7936:8192].rearrange("p (a n) -> p a n", a=4)
        xtra = gates[:, 1, :]
        valid = sb("valid", [P, 1])
        ps = ctx.enter_context(nc.psum_tensor("ps", [P, 8, 512], F32))
        psf = ps[:, :, :].rearrange("p b n -> p (b n)")

        xsave = nc.dram_tensor("xsave", (SEQ, D), F32).ap()
        nsad = nc.dram_tensor("nsad", (SEQ, 1280), F32).ap()
        mlad = nc.dram_tensor("mlad", (SEQ, 2048), F32).ap()
        difd = nc.dram_tensor("difd", (SEQ, 3072), F32).ap()

        aT = actT[:, :].rearrange("p (s k t) -> p s k t", s=2, k=KD)
        xr = xres[:, :].rearrange("p (t d) -> p t d", t=T)
        raw = xres[:, :].rearrange("p (s t n) -> p s t n", s=2, t=T)
        x_in = x.rearrange("b (t p) d -> p (b t) d", p=P)
        x_sv = xsave.rearrange("(t p) d -> p t d", p=P)
        x_out = out.rearrange("b (t p) d -> p (b t) d", p=P)
        nsav = nsad.rearrange("(t p) n -> p t n", p=P)
        mlav = mlad.rearrange("(t p) n -> p t n", p=P)
        difv = difd.rearrange("(t p) n -> p t n", p=P)

        s_const = sem("s_const")
        s_posz = sem("s_posz")
        s_made = sem("s_made")
        s_stage = [sem("s_stage0"), sem("s_stage1")]
        s_wready = sem("s_wready")
        s_wused = sem("s_wused")
        s_tick = sem("s_tick")
        s_pool = sem("s_pool")
        s_dve = sem("s_dve")
        s_act = sem("s_act")
        s_bar = sem("s_bar")
        s_adal = [sem("s_adal0"), sem("s_adal1")]
        s_adau = sem("s_adau")
        s_adaacc = sem("s_adaacc")
        s_adamm = sem("s_adamm")
        s_adaev = sem("s_adaev")
        s_x = sem("s_x")
        s_ss = sem("s_ss")
        s_var = sem("s_var")
        s_std = sem("s_std")
        s_xn = sem("s_xn")
        s_tr = sem("s_tr")
        s_trh = sem("s_trh")
        s_trl = sem("s_trl")
        s_mm = sem("s_mm")
        s_raw = sem("s_raw")
        s_proc = sem("s_proc")
        s_spill = [sem("s_spill0"), sem("s_spill1")]
        s_cmp = sem("s_cmp")
        s_cpe = sem("s_cpe")
        s_cact = sem("s_cact")
        s_cdve = sem("s_cdve")
        s_out = sem("s_out")
        s_xs = sem("s_xs")

        s_cond = sem("s_cond")
        s_lam = sem("s_lam")
        s_ang = sem("s_ang")
        s_sin = sem("s_sin")
        s_g1 = sem("s_g1")
        s_gr = sem("s_gr")
        s_gt = sem("s_gt")
        s_gh = sem("s_gh")
        s_gl = sem("s_gl")
        s_y = sem("s_y")
        s_ya = sem("s_ya")

        pexp = arena[:, 9216:11264].rearrange("p (s n) -> p s n", s=2)
        pT = actT[:, 12288:16384].rearrange("p (u s n) -> p u s n", u=2, s=2)
        relu = arena[:, 0:1024].rearrange("p (s n) -> p s n", s=2)
        sq = arena[:, 1024:2048].rearrange("p (s n) -> p s n", s=2)
        upq = [xres[:, 0:3072].rearrange("p (t n) -> p t n", t=4),
               arena[:, 0:3072].rearrange("p (t n) -> p t n", t=4)]
        upk = [xres[:, 3072:8192].rearrange("p (t h n) -> p t h n", t=4, h=HEADS),
               arena[:, 3072:8192].rearrange("p (t h n) -> p t h n", t=4, h=HEADS)]
        ang = xtra[:, 0:216].rearrange("p (t n) -> p t n", t=T + 1)
        turns = xtra[:, 216:432].rearrange("p (t n) -> p t n", t=T + 1)
        half_ang = xtra[:, 432:648].rearrange("p (t n) -> p t n", t=T + 1)
        invf = xtra[:, 648:672]
        NCONST = 22
        ORDER = [(k, half) for half in range(2) for k in range(KD)]

        block = ctx.enter_context(nc.Block())

        STAGES = ["norm0", "proj0", "latent", "up", "cmp", "mla", "nsa", "otr0", "out0", "norm1", "mlp0",
                  "ada1", "norm2", "proj1", "dif", "sub", "otr1", "out1", "norm3", "mlp1", "end"]
        BAR = {name: n + 1 for n, name in enumerate(STAGES)}

        def barrier(eng, q, stage):
            q.drain().then_inc(s_bar, 1)
            eng.wait_ge(s_bar, 3 * BAR[stage])

        TR = {"norm0": 0, "latent": 16, "otr0": 24, "norm1": 40, "norm2": 56, "otr1": 72, "norm3": 88}
        MM = {"proj0": 0, "up": 28, "out0": 42, "proj1": 56, "out1": 98}
        RAW = {"proj0": 0, "up": 32, "out0": 48, "proj1": 64, "out1": 112}

        def unit(t, kind, k0, nblk, add, factor):
            return dict(t=t, kind=kind, k0=k0, n=nblk, add=add, factor=factor, halves=(nblk + 3) // 4)

        UNITS = {"mla": [unit(t, "full", 0, t + 1, False, None) for t in range(T)],
                 "nsa": [u for t in range(T) for u in (
                     unit(t, "slc", 0, t + 1, False, 1),
                     unit(t, "win", max(0, t - WINDOW_TILES), min(t, WINDOW_TILES) + 1, True, 2),
                     unit(t, "cmp", 0, 1, True, 0))],
                 "dif": [unit(t, f"map{m}", 0, t + 1, m == 1, m) for t in range(T) for m in range(2)]}
        ATT = {}
        for name in UNITS:
            ATT[name] = {k: sem(f"{name}_{k}") for k in (
                "s_load",
                "s_fhi",
                "s_fmt",
                "s_ftr",
                "s_feva",
                "s_fevd",
                "s_qk",
                "s_mx",
                "s_ex",
                "s_t",
                "s_ph",
                "s_pl",
                "s_pv",
                "s_o",
                "s_own",
                )}
            ATT[name]["U"] = len(UNITS[name])
            ATT[name]["H"] = sum(u["halves"] for u in UNITS[name])
        nsag = {k: sem(f"nsag_{k}") for k in ("s_load", "s_fhi", "s_fmt", "s_ftr", "s_feva", "s_fevd")}
        ATT["mla"]["nfmt"], ATT["nsa"]["nfmt"], ATT["dif"]["nfmt"] = 3, 1, 5

        def wview(a, row0, nk, c0, n):
            return a[row0:row0 + nk * P, c0:c0 + n].rearrange("(k p) n -> p k n", p=P)

        HYC = [[(NQ0, 512)], [(NKV0, 512)], [(NKV0 + 512, 280), (LATENT_W, 32)], [(0, 512)]]
        PROJ0 = []
        for cols in HYC:
            for kh in range(2):
                PROJ0.append(("cols", hy_w_in[0], kh * 512, 4, cols, None))
        PROJ0.append(("cols", mla_w_uq[0], 0, 2, [(0, 768)], None))
        PROJ0.append(("cols", mla_w_ukv[0], 0, 2, [(0, 1024)], None))
        OUT0 = [("cols", hy_w_out[0], kh * 512, 4, [(n * 512, 512)], (0, n * 512, 512))
                for n in range(2) for kh in range(2)]
        PROJ1 = [("cols", diff_w_qkv[0], kh * 512, 4, [(n * 512, 512)], None)
                 for n in range(6) for kh in range(2)]
        OUT1 = [("cols", diff_w_out[0], kh * 512, 4, [(n * 512, 512)], (0, n * 512, 512))
                for n in range(2) for kh in range(2)]
        FIRST = {"proj0": 0}
        FIRST["out0"] = len(PROJ0)
        FIRST["mlp0"] = FIRST["out0"] + len(OUT0)
        FIRST["proj1"] = FIRST["mlp0"] + 2 * FF_GROUPS
        FIRST["out1"] = FIRST["proj1"] + len(PROJ1)
        FIRST["mlp1"] = FIRST["out1"] + len(OUT1)
        assert all(v % 2 == 0 for v in FIRST.values())

        def mlp_views(layer, g):
            w1 = mlp_w1[layer].rearrange("(k p) n -> p k n", p=P)[:, :, bass.ds(g * FFG, FFG)]
            w2 = mlp_w2[layer].rearrange("(q p) n -> p q n", p=P)[:, bass.ds(g * 2, 2), :]
            return w1, w2

        @block.sync
        def _(sp):
            def load(dst, src, s):
                sp.dma_start(dst, src).then_inc(s, 16)

            sp.wait_ge(s_posz, 1)
            load(posi[:, 0:T], positions.rearrange("b (t p) -> p (b t)", p=P), s_const)
            load(posi[0:CMP - 1, T:T + 1], positions[0:1, 31:SEQ:16].rearrange("b c -> c b"), s_const)
            load(cond[:, 0, :], c.rearrange("b (p k) -> p (b k)", p=P), s_const)
            for i in range(2):
                load(normv[:, 2 * i, :], norm_mix[i:i + 1, :].rearrange("b (k p) -> p (b k)", p=P), s_const)
                load(normv[:, 2 * i + 1, :], norm_mlp[i:i + 1, :].rearrange("b (k p) -> p (b k)", p=P), s_const)
            load(latv[:, 0:2], mla_q_norm.rearrange("b (k p) -> p (b k)", p=P), s_const)
            load(latv[:, 2:4], mla_kv_norm.rearrange("b (k p) -> p (b k)", p=P), s_const)
            load(gainq[:, 0, :], mla_q_gain.broadcast_to([P, 96]), s_const)
            load(gainq[:, 1, :], mla_k_gain.broadcast_to([P, 96]), s_const)
            load(gainh[:, 0, :], nsa_q_gain.broadcast_to([P, DH]), s_const)
            for b in range(3):
                load(gainh[:, 1 + b, :], nsa_k_gain[0, b:b + 1, :].broadcast_to([P, DH]), s_const)
            load(gainh[:, 4, :], diff_q_gain.broadcast_to([P, DH]), s_const)
            load(gainh[:, 5, :], diff_k_gain.broadcast_to([P, DH]), s_const)
            load(gsub[:, :], diff_sub_gain.broadcast_to([P, 2 * DH]), s_const)
            for b in range(4):
                load(lamt[:, b, :], diff_lambda[0, b:b + 1, :].broadcast_to([P, DH]), s_const)

            def chunk(n, kind):
                _, w, row0, nk, cols, _ = kind
                if n >= 2:
                    sp.wait_ge(s_wready, n - 1)
                width = sum(m for _, m in cols)
                dst = stage[:, n % 2, 0:nk * width].rearrange("p (k n) -> p k n", k=nk)
                at = 0
                for c0, m in cols:
                    load(dst[:, :, at:at + m], wview(w, row0, nk, c0, m), s_stage[n % 2])
                    at += m

            def ada(layer):
                w = ada_w[layer].rearrange("(p k) n -> p k n", k=KD)
                for g in range(6):
                    for half in range(2):
                        n = layer * 12 + g * 2 + half
                        if n >= 2:
                            sp.wait_ge(s_adaacc if half else s_adau, n // 2)
                        dst = arena[:, (n % 2) * 4096:(n % 2) * 4096 + 4096].rearrange("p (k n) -> p k n", k=4)
                        load(dst, w[:, 4 * half:4 * half + 4, g * 1024:(g + 1) * 1024], s_adal[n % 2])
                        if half == 0:
                            load(arena[0:1, 9216 + (g % 2) * 1024:10240 + (g % 2) * 1024],
                                 ada_b[layer:layer + 1, g * 1024:(g + 1) * 1024], s_adal[n % 2])

            def mlp(layer):
                with sp.Fori(0, FF_GROUPS) as g:
                    w1, w2 = mlp_views(layer, g)
                    first = FIRST[f"mlp{layer}"]
                    sp.wait_ge(s_wready, g * 2 + first - 1)
                    load(stage[:, 0, :].rearrange("p (k n) -> p k n", k=KD), w1, s_stage[0])
                    sp.wait_ge(s_wready, g * 2 + first)
                    load(stage[:, 1, :].rearrange("p (k n) -> p k n", k=2), w2, s_stage[1])

            load(xr, x_in, s_x)
            chunk(0, PROJ0[0])
            chunk(1, PROJ0[1])
            ada(0)
            for n in range(2, len(PROJ0)):
                chunk(n, PROJ0[n])
            for n, kind in enumerate(OUT0):
                chunk(FIRST["out0"] + n, kind)
            sp.wait_ge(s_bar, 3 * BAR["cmp"])
            for a in range(4):
                load(xres[0:CMP, a * 1024:(a + 1) * 1024].rearrange("p (l n) -> p l n", l=16),
                     nsad[:, 512 + a * DH:512 + (a + 1) * DH].rearrange("(m l) n -> m l n", l=16), s_cmp)
            for j in range(2):
                load(arena[:, j * 2048:(j + 1) * 2048].rearrange("p (i n) -> p i n", i=16),
                     nsa_cmp_w1[0, j].rearrange("(i q) n -> q i n", q=P), s_cmp)
                load(arena[:, 10240 + j * 64:10304 + j * 64], nsa_cmp_w2[0, j], s_cmp)
                for par in range(2):
                    load(arena[64 * par:64 * par + 64, 10368 + j * 16:10384 + j * 16],
                         nsa_cmp_pos[0, j].rearrange("(i r) d -> r d i", r=2)[par], s_cmp)
            sp.wait_ge(s_bar, 3 * BAR["mla"])
            mla = ATT["mla"]
            with sp.Fori(0, HEADS) as h:
                sp.wait_ge(mla["s_fmt"], h * mla["nfmt"])
                src = [mlav[:, :, bass.ds(h * 96, 96)], mlav[:, :, bass.ds(h * 96 + 768, 96)],
                       mlav[:, :, bass.ds(h * 64 + 1536, 64)]]
                hb = arena[:, 0:T * 256].rearrange("p (t n) -> p t n", t=T)
                load(hb[:, :, 0:96], src[0], mla["s_load"])
                load(hb[:, :, 96:192], src[1], mla["s_load"])
                load(hb[:, :, 192:256], src[2], mla["s_load"])
            sp.wait_ge(s_bar, 3 * BAR["nsa"])
            nsa = ATT["nsa"]
            with sp.Fori(0, GROUPS) as g:
                sp.wait_ge(nsa["s_fmt"], g * PER_GROUP * nsa["nfmt"])
                sp.sem_inc(s_tick, 1)
                sp.wait_ge(nsag["s_fmt"], g * 6)
                sp.sem_inc(s_tick, 1)
                kb = arena[:, 0:T * 256].rearrange("p (t n) -> p t n", t=T)
                for m, col in enumerate([768, 768 + 128, 1024, 1024 + 128]):
                    load(kb[:, :, m * 64:(m + 1) * 64], nsav[:, :, bass.ds(g * 64 + col, 64)], nsag["s_load"])
                with sp.Fori(0, PER_GROUP) as hh:
                    sp.wait_ge(nsa["s_fmt"], (g * PER_GROUP + hh) * nsa["nfmt"])
                    sp.sem_inc(s_tick, 1)
                    load(arena[:, 2048:2560].rearrange("p (t n) -> p t n", t=T),
                         nsav[:, :, bass.ds((g * PER_GROUP + hh) * 64, 64)], nsa["s_load"])
            sp.wait_ge(s_bar, 3 * BAR["out0"])
            load(xr, x_in, s_x)
            mlp(0)
            sp.wait_ge(s_bar, 3 * BAR["ada1"])
            load(x_sv, xr, s_xs)
            n0 = FIRST["proj1"]
            chunk(n0, PROJ1[0])
            chunk(n0 + 1, PROJ1[1])
            ada(1)
            for n in range(2, len(PROJ1)):
                chunk(n0 + n, PROJ1[n])
            for n, kind in enumerate(OUT1):
                chunk(FIRST["out1"] + n, kind)
            sp.wait_ge(s_bar, 3 * BAR["dif"])
            dif = ATT["dif"]
            with sp.Fori(0, HEADS) as h:
                sp.wait_ge(dif["s_fmt"], h * dif["nfmt"])
                hb = arena[:, 0:T * 384].rearrange("p (t n) -> p t n", t=T)
                for m in range(3):
                    load(hb[:, :, m * 128:(m + 1) * 128], difv[:, :, bass.ds(h * 128 + m * 1024, 128)],
                         dif["s_load"])
            sp.wait_ge(s_bar, 3 * BAR["out1"])
            load(xr, x_sv, s_x)
            mlp(1)
            sp.wait_ge(s_bar, 3 * BAR["end"])
            load(x_out, xr, s_out)
            sp.wait_ge(s_out, 16)
            sp.wait_ge(s_xs, 16)

        @block.gpsimd
        def _(pool):
            own = Count(pool, s_pool)
            q = nc.gpsimd
            own.mark(q.memset(ones[:, :], 1.0))
            own.mark(q.memset(gates[:, 0, 0:184], 0.0))
            q.memset(posi[:, :], 0).then_inc(s_posz, 1)
            own.sync()
            own.link(q.affine_select(out=ident[:, :], in_=gates[:, 0, 0:P], compare_op=ALU.not_equal, fill=1.0,
                                     base=0, pattern=[[-1, P]], channel_multiplier=1))
            own.mark(q.affine_select(out=masks[:, 0, :], in_=gates[:, 0, 0:P], compare_op=ALU.is_ge, fill=NEG,
                                     base=0, pattern=[[-1, P]], channel_multiplier=1))
            own.mark(q.affine_select(out=masks[:, 1, :], in_=gates[:, 0, 0:P], compare_op=ALU.is_gt, fill=NEG,
                                     base=0, pattern=[[1, P]], channel_multiplier=-1))
            own.mark(q.affine_select(out=cmask[:, :], in_=gates[:, 0, 0:184], compare_op=ALU.is_ge,
                                     fill=NEG, base=16 * 56 - 31, pattern=[[-16, 184]], channel_multiplier=1))
            own.mark(q.affine_select(out=valid[:, :], in_=ones[:, 0:1], compare_op=ALU.is_ge, fill=0.0,
                                     base=-31, pattern=[[0, 1]], channel_multiplier=1))
            own.mark(q.tensor_copy(identr[:, :], ident[:, :]))
            own.sync()
            q.drain().then_inc(s_made, 1)

            def split(n, slot, length, staged, gate):
                w = stage[:, slot, 0:length]
                pool.wait_ge(s_stage[slot], staged)
                if gate is not None:
                    nk, g, c0, m = gate
                    v = w.rearrange("p (k n) -> p k n", k=nk)
                    own.link(q.tensor_tensor(v, v, gates[:, g:g + 1, c0:c0 + m].broadcast_to([P, nk, m]), ALU.mult))
                hi, lo = wts[:, slot, 0, 0:length], wts[:, slot, 1, 0:length]
                if not (isinstance(n, int) and n < 2):
                    pool.wait_ge(s_wused, n - 1)
                own.link(q.tensor_tensor(hi, w, ones[:, 0:1].broadcast_to([P, length]), ALU.mult))
                q.tensor_tensor(lo, w, hi.bitcast(F32), ALU.subtract).then_inc(s_wready, 1)

            staged = [0, 0]

            def straight(first, kinds):
                for m, (_, _, _, nk, cols, gate) in enumerate(kinds):
                    n = first + m
                    staged[n % 2] += 16 * len(cols)
                    width = sum(w for _, w in cols)
                    split(n, n % 2, nk * width, staged[n % 2], None if gate is None else (nk, *gate))

            def mlp(layer):
                first = FIRST[f"mlp{layer}"]
                with pool.Fori(0, FF_GROUPS) as g:
                    own.enter(g, 3)
                    split(g * 2 + first, 0, WCH, g * 16 + (staged[0] + 16), None)
                    split(g * 2 + (first + 1), 1, WCH, g * 16 + (staged[1] + 16), (2, 1, 0, D))
                own.leave(3, FF_GROUPS)
                staged[0] += 16 * FF_GROUPS
                staged[1] += 16 * FF_GROUPS

            straight(FIRST["proj0"], PROJ0)
            pool.wait_ge(s_adaev, 6)
            straight(FIRST["out0"], OUT0)
            mlp(0)
            straight(FIRST["proj1"], PROJ1)
            pool.wait_ge(s_adaev, 12)
            straight(FIRST["out1"], OUT1)
            mlp(1)


        @block.tensor
        def _(pe):
            q = nc.tensor

            def product(dst, passes, last):
                ins = None
                for n, (a, b) in enumerate(passes):
                    ins = q.matmul(dst, a, b, start=(n == 0), stop=(n == len(passes) - 1 and last))
                return ins

            def ada(layer):
                for g in range(6):
                    n = layer * 6 + g
                    pe.wait_ge(s_adaacc, n + 1)
                    if n >= 1:
                        pe.wait_ge(s_adaev, n)
                    acc = arena[:, 8192:9216]
                    bias = arena[0:1, 9216 + (g % 2) * 1024:10240 + (g % 2) * 1024]
                    if g in (2, 5):
                        for h in range(2):
                            q.matmul(ps[:, h, :], ones[:, :], acc[:, h * 512:(h + 1) * 512], start=True, stop=False)
                            ins = q.matmul(ps[:, h, :], ones[0:1, :], bias[:, h * 512:(h + 1) * 512],
                                           start=False, stop=True)
                    else:
                        for k in range(KD):
                            q.matmul(ps[:, 0, k:k + 1], acc[:, k * P:(k + 1) * P], ones[:, 0:1], start=True, stop=False)
                            ins = q.matmul(ps[:, 0, k:k + 1], bias[:, k * P:(k + 1) * P], ones[0:1, 0:1],
                                           start=False, stop=True)
                    ins.then_inc(s_adamm, 1)

            def transposes(name, src, order):
                for idx, (k, half) in enumerate(order):
                    if idx >= 8:
                        pe.wait_ge(s_trl, TR[name] + idx - 7)
                    for m in range(4):
                        ins = q.transpose(ps[:, idx % 8, m * P:(m + 1) * P], src(4 * half + m, k), ident[:, :])
                    ins.then_inc(s_tr, 1)

            def norm_banks(name, n):
                for idx, (k, half) in enumerate(ORDER):
                    pe.wait_ge(s_xn, 8 * n + 4 * half + 4)
                    if idx >= 8:
                        pe.wait_ge(s_trl, TR[name] + idx - 7)
                    for m in range(4):
                        t = 4 * half + m
                        ins = q.transpose(ps[:, idx % 8, m * P:(m + 1) * P],
                                          arena[:, t * D + k * P:t * D + (k + 1) * P], ident[:, :])
                    ins.then_inc(s_tr, 1)

            def splits(a, b, n):
                return [(a[0], b[0]), (a[0], b[1]), (a[1], b[0])]

            def project(chunk, width, raw_free):
                for kh in range(2):
                    pe.wait_ge(s_wready, chunk + (kh + 1))
                    w = [wts[:, kh, s, 0:4 * width].rearrange("p (k n) -> p k n", k=4) for s in range(2)]
                    for t in range(T):
                        if kh == 0 and raw_free is not None:
                            pe.wait_ge(s_raw, raw_free + (t + 1))
                        passes = []
                        for k in range(4):
                            a = [aT[:, s, kh * 4 + k, t * P:(t + 1) * P] for s in range(2)]
                            passes += splits(a, [w[s][:, k, :] for s in range(2)], t)
                        for n, (a, b) in enumerate(passes):
                            ins = q.matmul(ps[:, t, 0:width], a, b, start=(kh == 0 and n == 0),
                                           stop=(kh == 1 and n == len(passes) - 1))
                        if t == T - 1:
                            ins.then_inc(s_wused, 1)
                        elif kh == 1:
                            ins.then_inc(s_mm, 1)

            def up():
                for which, (k0, halfw) in enumerate(((0, 384), (2, 512))):
                    n = FIRST["proj0"] + 8 + which
                    pe.wait_ge(s_wready, n + 1)
                    w = [wts[:, which, s, 0:4 * halfw].rearrange("p (k n) -> p k n", k=2) for s in range(2)]
                    for t in range(T):
                        u = which * T + t
                        if u >= 4:
                            pe.wait_ge(s_raw, RAW["up"] + u - 3)
                        for h in range(2):
                            passes = []
                            for k in range(2):
                                a = [aT[:, s, k0 + k, t * P:(t + 1) * P] for s in range(2)]
                                passes += splits(a, [w[s][:, k, h * halfw:(h + 1) * halfw] for s in range(2)], t)
                            ins = product(ps[:, (u % 4) * 2 + h, 0:halfw], passes, True)
                        ins.then_inc(s_wused if t == T - 1 else s_mm, 1)

            def compress():
                pe.wait_ge(s_cmp, 16 * 12)
                cb = xres[0:CMP, 0:4096].rearrange("p (a n) -> p a n", a=4)
                for a in range(4):
                    for i in range(8):
                        ins = q.transpose(ps[:, a, i * CMP:(i + 1) * CMP],
                                          cb[:, a, i * P:(i + 1) * P], ident[0:CMP, 0:CMP])
                    ins.then_inc(s_cpe, 1)
                w1 = arena[:, 0:4096].rearrange("p (j i n) -> p j i n", j=2, i=16)
                blk = arena[:, 4096:8192].rearrange("p (i a m) -> p i a m", i=16, a=4)
                pe.wait_ge(s_cdve, 2)
                for j in range(2):
                    ins = product(ps[:, 4 + j, 0:P], [(w1[:, j, i, :], blk[:, i, 2 * j:2 * j + 2, :])
                                                      for i in range(16)], True)
                    ins.then_inc(s_cpe, 1)
                hid = arena[:, 8192:8448].rearrange("p (j g m) -> p j g m", j=2, g=2)
                w2 = arena[:, 10240:10368].rearrange("p (j n) -> p j n", j=2)
                pe.wait_ge(s_cact, 2)
                for j in range(2):
                    for g in range(2):
                        ins = q.matmul(ps[0:CMP, 6, (2 * j + g) * DH:(2 * j + g + 1) * DH], hid[:, j, g, :],
                                       w2[:, j, :], start=True, stop=True)
                ins.then_inc(s_cpe, 1)

            def stacks(tiles, width, done, ready):
                for n, tile in enumerate(tiles):
                    for half in range(2):
                        if ready is not None:
                            ready(2 * n + half)
                        for m in range(4):
                            ins = q.transpose(ps[0:width, (2 * n + half) % 8, m * P:(m + 1) * P],
                                              tile[:, 4 * half + m, 0:width], ident[:, :])
                        ins.then_inc(done, 1)

            def attend(name, head, scores, values, dv):
                S, units, U, H = ATT[name], UNITS[name], ATT[name]["U"], ATT[name]["H"]
                before = [sum(u["halves"] for u in units[:n]) for n in range(U + 1)]

                def qk(n):
                    u = units[n]
                    pe.wait_ge(S["s_ex"], head * U + max(n - 1, 0))
                    base = (n % 2) * 1024
                    for b in range(0, u["n"], 4):
                        w = min(4, u["n"] - b) * P
                        dst = psf[:, base + b * P:base + b * P + w]
                        passes = scores(u, (u["k0"] + b) * P, w)
                        for m, (a, c2) in enumerate(passes):
                            ins = q.matmul(dst, a, c2, start=(m == 0), stop=False, skip_group_check=True)
                        if u["kind"] == "cmp":
                            wanted = [(0, cmask[:, 56 - 8 * u["t"]:184 - 8 * u["t"]])]
                        else:
                            wanted = [(u["t"] - u["k0"], masks[:, 0, :])]
                            if u["kind"] == "win" and u["t"] >= WINDOW_TILES:
                                wanted.append((0, masks[:, 1, :]))
                        for at, mask in wanted:
                            if b <= at < b + 4:
                                ins = q.matmul(psf[:, base + at * P:base + (at + 1) * P], identr[:, :],
                                               mask, start=False, stop=False, skip_group_check=True)
                    ins.then_inc(S["s_qk"], 1)

                def tr(n):
                    u = units[n]
                    pe.wait_ge(S["s_ex"], head * U + (n + 1))
                    for half in range(u["halves"]):
                        k = before[n] + half
                        pe.wait_ge(S["s_pl"], head * H + max(k - 1, 0))
                        for m in range(4 * half, min(4 * half + 4, u["n"])):
                            ins = q.transpose(ps[:, 4 + k % 2, (m % 4) * P:(m % 4 + 1) * P],
                                              pexp[:, n % 2, m * P:(m + 1) * P], ident[:, :])
                        ins.then_inc(S["s_t"], 1)

                def pv(n):
                    u = units[n]
                    pe.wait_ge(S["s_pl"], head * H + before[n + 1])
                    pe.wait_ge(S["s_o"], head * U + max(n - 1, 0))
                    passes = []
                    for m in range(u["n"]):
                        p = [pT[:, n % 2, s, m * P:(m + 1) * P] for s in range(2)]
                        passes += splits(p, [values(u, u["k0"] + m, s) for s in range(2)], m)
                    product(ps[:, 6 + n % 2, 0:dv], passes, True).then_inc(S["s_pv"], 1)

                qk(0)
                qk(1)
                for n in range(U):
                    tr(n)
                    if n >= 1:
                        pv(n - 1)
                    if n + 2 < U:
                        qk(n + 2)
                pv(U - 1)

            def drained(name, head):
                S = ATT[name]
                pe.wait_ge(S["s_o"], head * S["U"])
                pe.wait_ge(S["s_pl"], head * S["H"])
                pe.wait_ge(S["s_ex"], head * S["U"])

            def mla():
                S = ATT["mla"]
                st = [actT[0:MLA_DH, n * 1024:(n + 1) * 1024] for n in range(4)]
                v = actT[:, 4096:5120].rearrange("p (t s n) -> p t s n", t=T, s=2)
                fm = arena[:, 2048:6144].rearrange("p (a t n) -> p a t n", a=4, t=T)
                with pe.Fori(0, HEADS) as h:
                    drained("mla", h)
                    pe.wait_ge(S["s_fmt"], h * 3 + 3)
                    stacks([fm[:, n, :, :] for n in range(4)], MLA_DH, S["s_ftr"], None)
                    pe.wait_ge(S["s_feva"], h * 4 + 4)
                    pe.wait_ge(S["s_fevd"], h * 4 + 4)

                    def scores(u, c0, w):
                        qt = [st[s][:, u["t"] * P:(u["t"] + 1) * P] for s in range(2)]
                        return splits(qt, [st[2 + s][:, c0:c0 + w] for s in range(2)], 0)

                    attend("mla", h, scores, lambda u, kb, s: v[:, kb, s, :], MLA_V)

            def nsa():
                S = ATT["nsa"]
                st = {"slc": [actT[:, 0:1024], actT[:, 1024:2048]], "win": [actT[:, 2048:3072], actT[:, 3072:4096]],
                      "cmp": [actT[:, 7168:7296], actT[:, 7296:7424]]}
                qs = actT[:, 4096:5120]
                v = {"slc": actT[:, 5120:6144].rearrange("p (t s n) -> p t s n", t=T, s=2),
                     "win": actT[:, 6144:7168].rearrange("p (t s n) -> p t s n", t=T, s=2),
                     "cmp": actT[:, 7424:7552].rearrange("p (t s n) -> p t s n", t=1, s=2)}
                fm = arena[:, 2560:6656].rearrange("p (a t n) -> p a t n", a=4, t=T)
                fq = arena[:, 6656:7680].rearrange("p (t n) -> p t n", t=T)
                fc = arena[:, 7680:7936].rearrange("p (s n) -> p s n", s=2)
                with pe.Fori(0, GROUPS) as g:
                    drained("nsa", g * PER_GROUP)
                    pe.wait_ge(nsag["s_fmt"], g * 6 + 6)
                    for n in range(4):
                        for half in range(2):
                            for m in range(4):
                                ins = q.transpose(ps[:, 2 * n + half, m * P:(m + 1) * P],
                                                  fm[:, n, 4 * half + m, :], ident[:, :])
                            ins.then_inc(nsag["s_ftr"], 1)
                    pe.wait_ge(nsag["s_feva"], g * 5 + 1)
                    for s in range(2):
                        ins = q.transpose(ps[:, 0, s * P:(s + 1) * P], fc[:, s, :], ident[:, :])
                    ins.then_inc(nsag["s_ftr"], 1)
                    pe.wait_ge(nsag["s_feva"], g * 5 + 5)
                    pe.wait_ge(nsag["s_fevd"], g * 4 + 4)
                    pe.sem_inc(s_tick, 1)
                    with pe.Fori(0, PER_GROUP) as hh:
                        h = g * PER_GROUP + hh
                        drained("nsa", h)
                        pe.wait_ge(S["s_fmt"], h + 1)
                        stacks([fq], P, S["s_ftr"], None)
                        pe.wait_ge(S["s_feva"], h + 1)
                        pe.wait_ge(S["s_fevd"], h + 1)

                        def scores(u, c0, w):
                            qt = qs[:, u["t"] * P:(u["t"] + 1) * P]
                            return [(qt, st[u["kind"]][s][:, c0:c0 + w]) for s in range(2)]

                        attend("nsa", h, scores, lambda u, kb, s: v[u["kind"]][:, kb, s, :], DH)

            def dif():
                S = ATT["dif"]
                v = actT[:, 6144:8192].rearrange("p (t s n) -> p t s n", t=T, s=2)
                fm = arena[:, 3072:9216].rearrange("p (a t n) -> p a t n", a=6, t=T)
                with pe.Fori(0, HEADS) as h:
                    drained("dif", h)
                    pe.wait_ge(S["s_fmt"], h * 5 + 5)

                    def taken(b):
                        if b >= 8:
                            pe.wait_ge(S["s_feva"] if b % 2 == 0 else S["s_fevd"], h * 6 + ((b - 8) // 2 + 1))

                    stacks([fm[:, n, :, :] for n in range(6)], P, S["s_ftr"], taken)
                    pe.wait_ge(S["s_feva"], h * 6 + 6)
                    pe.wait_ge(S["s_fevd"], h * 6 + 6)

                    def scores(u, c0, w):
                        o = 3072 * u["factor"]
                        qt = actT[:, o + u["t"] * P:o + (u["t"] + 1) * P]
                        return [(qt, actT[:, o + (1 + s) * 1024 + c0:o + (1 + s) * 1024 + c0 + w]) for s in range(2)]

                    attend("dif", h, scores, lambda u, kb, s: v[:, kb, s, :], 2 * DH)

            def mlp(layer):
                first = FIRST[f"mlp{layer}"]
                w1 = [wts[:, 0, s, :].rearrange("p (k n) -> p k n", k=KD) for s in range(2)]
                w2 = [wts[:, 1, s, :].rearrange("p (k n) -> p k n", k=2) for s in range(2)]
                with pe.Fori(0, FF_GROUPS) as g:
                    pe.wait_ge(s_wready, g * 2 + (first + 1))
                    for idx, (half, f) in enumerate(((0, 0), (0, 1), (1, 0), (1, 1))):
                        pe.wait_ge(s_gl, g * 4 + (layer * 64 + max(idx - 3, 0)))
                        passes = []
                        for k in range(KD):
                            passes += splits([w1[s][:, k, f * P:(f + 1) * P] for s in range(2)],
                                             [aT[:, s, k, half * 512:(half + 1) * 512] for s in range(2)], 0)
                        product(ps[:, idx, :], passes, True).then_inc(s_wused if idx == 3 else s_g1, 1)
                    pe.wait_ge(s_wready, g * 2 + (first + 2))
                    for idx in range(16):
                        t, n = idx // 2, idx % 2
                        if idx == 0:
                            pe.wait_ge(s_gl, g * 4 + (layer * 64 + 2))
                        if idx == 8:
                            pe.wait_ge(s_gl, g * 4 + (layer * 64 + 4))
                        pe.wait_ge(s_ya, g * 16 + (layer * 256 + max(idx - 3, 0)))
                        passes = []
                        for f in range(2):
                            passes += splits([gT[:, s, f, t * P:(t + 1) * P] for s in range(2)],
                                             [w2[s][:, f, n * 512:(n + 1) * 512] for s in range(2)], 0)
                        product(ps[:, 4 + idx % 4, :], passes, True).then_inc(s_wused if idx == 15 else s_y, 1)

            pe.wait_ge(s_made, 1)
            ada(0)
            barrier(pe, q, "norm0")
            norm_banks("norm0", 0)
            barrier(pe, q, "proj0")
            for j, cols in enumerate(HYC):
                project(2 * j, sum(w for _, w in cols), None if j == 0 else 8 * (j - 1))
            barrier(pe, q, "latent")
            latents = xres[:, 4096:8192].rearrange("p (t n) -> p t n", t=T)
            pe.wait_ge(s_proc, 3)
            transposes("latent", lambda t, k: latents[:, t, k * P:(k + 1) * P],
                       [(k, h) for h in range(2) for k in range(4)])
            barrier(pe, q, "up")
            up()
            barrier(pe, q, "cmp")
            compress()
            barrier(pe, q, "mla")
            mla()
            barrier(pe, q, "nsa")
            nsa()
            barrier(pe, q, "otr0")
            transposes("otr0", lambda t, k: xr[:, t, k * P:(k + 1) * P], ORDER)
            barrier(pe, q, "out0")
            for j in range(2):
                project(FIRST["out0"] + 2 * j, 512, None if j == 0 else RAW["out0"])
            barrier(pe, q, "norm1")
            norm_banks("norm1", 1)
            barrier(pe, q, "mlp0")
            mlp(0)
            barrier(pe, q, "ada1")
            ada(1)
            barrier(pe, q, "norm2")
            norm_banks("norm2", 2)
            barrier(pe, q, "proj1")
            project(FIRST["proj1"], 512, None)
            with pe.Fori(0, 5) as j:
                project(j * 2 + (FIRST["proj1"] + 2), 512, j * 8 + RAW["proj1"])
            barrier(pe, q, "dif")
            dif()
            barrier(pe, q, "sub")
            barrier(pe, q, "otr1")
            transposes("otr1", lambda t, k: xr[:, t, k * P:(k + 1) * P], ORDER)
            barrier(pe, q, "out1")
            for j in range(2):
                project(FIRST["out1"] + 2 * j, 512, None if j == 0 else RAW["out1"])
            barrier(pe, q, "norm3")
            norm_banks("norm3", 3)
            barrier(pe, q, "mlp1")
            mlp(1)
            barrier(pe, q, "end")

        @block.scalar
        def _(act):
            q = nc.scalar
            own = Count(act, s_act)
            std = [0]
            spills = [0, 0]

            def sqrt(n):
                std[0] += 1
                act.wait_ge(s_var, std[0])
                q.activation(small[:, 2, 0:n], small[:, 1, 0:n], ACT.Sqrt).then_inc(s_std, 1)

            def sumsq(n):
                for t in range(T):
                    if t >= 1:
                        act.wait_ge(s_ss, 8 * n + t)
                    q.activation(arena[:, 8192:9216], xr[:, t, :], ACT.Square,
                                 accum_out=small[:, 0, t:t + 1]).then_inc(s_ss, 1)

            def take_hi(name, order, scale, shift):
                for idx, (k, half) in enumerate(order):
                    act.wait_ge(s_tr, TR[name] + idx + 1)
                    dst = aT[:, 0, k, half * 512:(half + 1) * 512]
                    src = ps[:, idx % 8, :]
                    if scale is not None:
                        act.wait_ge(s_trl, TR[name] + max(idx - 1, 0))
                        tmp = arena[:, 8192 + (idx % 2) * 512:8704 + (idx % 2) * 512]
                        if shift is not None:
                            own.link(q.activation(tmp, src, ACT.Identity, bias=shift(k), scale=scale(k)))
                        else:
                            own.link(q.activation(tmp, src, ACT.Copy, scale=scale(k)))
                        src = tmp
                    q.activation(dst, src, ACT.Copy).then_inc(s_trh, 1)

            def norm(name, n):
                sumsq(n)
                sqrt(T)
                w = n % 2
                take_hi(name, ORDER, lambda k: modv[:, 2 * w, k:k + 1], lambda k: modv[:, 2 * w + 1, k:k + 1])

            def spill(slot, ready, pairs):
                if ready is not None:
                    act.wait_ge(s_proc, ready)
                for dst, src in pairs:
                    act.dma_start(dst, src).then_inc(s_spill[slot], 16)
                    spills[slot] += 16

            def stored(*slots):
                for slot in slots:
                    act.wait_ge(s_spill[slot], spills[slot])

            def take(mm, wused, name, t, dst, src):
                if t == T - 1:
                    act.wait_ge(s_wused, wused)
                else:
                    act.wait_ge(s_mm, mm + t + 1)
                q.activation(dst, src, ACT.Copy).then_inc(s_raw, 1)

            act.wait_ge(s_const, 16 * NCONST)
            q.activation(cond[:, 1, :], cond[:, 0, :], ACT.Exp, scale=-1.0).then_inc(s_cond, 1)
            act.wait_ge(s_ang, 1)
            q.activation(rope[:, 1, :, :], ang, ACT.Sin).then_inc(s_sin, 1)
            q.activation(half_ang, ang, ACT.Sin, scale=0.5).then_inc(s_sin, 1)
            act.wait_ge(s_lam, 1)
            q.activation(lams[:, 2:4], lams[:, 0:2], ACT.Exp).then_inc(s_cond, 1)
            barrier(act, q, "norm0")
            act.wait_ge(s_x, 16)
            norm("norm0", 0)
            barrier(act, q, "proj0")
            for j in range(4):
                width = sum(w for _, w in HYC[j])
                stored(j % 2)
                for t in range(T):
                    take(7 * j, 2 * j + 2, "proj0", t, raw[:, j % 2, t, 0:width], ps[:, t, 0:width])
                if j != 2:
                    sqrt({0: 64, 1: 16, 3: 16}[j])
                else:
                    sqrt(16)
                    act.wait_ge(s_raw, 24)
                    q.activation(gate3[:, :, :], raw[:, 0, :, 256:280], ACT.Exp, scale=-1.0).then_inc(s_cond, 1)
                    q.activation(kpe[:, :, :], raw[:, 0, :, 280:312], ACT.Copy).then_inc(s_cond, 1)
                if j == 0:
                    spill(0, 1, [(nsav[:, :, 0:512], raw[:, 0, :, :])])
                if j == 1:
                    spill(1, 2, [(nsav[:, :, 512:1024], raw[:, 1, :, :])])
                if j == 2:
                    spill(0, 3, [(nsav[:, :, 1024:1280], raw[:, 0, :, 0:256])])
            stored(0, 1)
            barrier(act, q, "latent")
            take_hi("latent", [(k, h) for h in range(2) for k in range(4)], lambda k: latv[:, k:k + 1], None)
            barrier(act, q, "up")
            for t in range(T):
                take(MM["up"], 9, "up", t, upq[t // 4][:, t % 4, :].rearrange("p (h n) -> p h n", h=2),
                     ps[:, (t % 4) * 2:(t % 4) * 2 + 2, 0:384])
            for t in range(T):
                take(MM["up"] + 7, 10, "up", t, upk[t // 4][:, t % 4, :, 32:160],
                     psf[:, (t % 4) * 1024:(t % 4) * 1024 + 1024].rearrange("p (h n) -> p h n", h=HEADS))
            for n in range(4):
                sqrt(32)
            for hf in range(2):
                rowsd = mlav[:, 4 * hf:4 * hf + 4, :]
                spill(hf, 5 + hf, [(rowsd[:, :, 0:768], upq[hf])])
            for hf in range(2):
                rowsd = mlav[:, 4 * hf:4 * hf + 4, :]
                spill(hf, 7 + hf, [(rowsd[:, t, 768:1536].rearrange("p (h n) -> p h n", h=HEADS),
                                 upk[hf][:, t, :, 0:96]) for t in range(4)] +
                      [(rowsd[:, t, 1536:2048].rearrange("p (h n) -> p h n", h=HEADS),
                        upk[hf][:, t, :, 96:160]) for t in range(4)])
            stored(0, 1)
            barrier(act, q, "cmp")
            for j in range(2):
                act.wait_ge(s_cpe, 5 + j)
                q.activation(arena[:, 8192 + j * P:8320 + j * P], ps[:, 4 + j, 0:P],
                             ACT.Gelu_apprx_tanh).then_inc(s_cact, 1)
            sqrt(2)
            barrier(act, q, "mla")

            def round_hi(dst, src, done):
                q.activation(dst, src, ACT.Copy).then_inc(done, 1)

            def attend(name, head):
                S, units, U, H = ATT[name], UNITS[name], ATT[name]["U"], ATT[name]["H"]
                before = [sum(u["halves"] for u in units[:n]) for n in range(U + 1)]

                def exps(n):
                    u = units[n]
                    act.wait_ge(S["s_mx"], head * U + (n + 1))
                    act.wait_ge(S["s_t"], head * H + before[max(n - 1, 0)])
                    base = (n % 2) * 1024
                    q.activation(pexp[:, n % 2, 0:u["n"] * P], psf[:, base:base + u["n"] * P], ACT.Exp,
                                 bias=rows[:, 0, n:n + 1], accum_out=rows[:, 1, n:n + 1]).then_inc(S["s_ex"], 1)

                def take_p(n):
                    u = units[n]
                    for half in range(u["halves"]):
                        k = before[n] + half
                        w = min(4, u["n"] - 4 * half) * P
                        act.wait_ge(S["s_t"], head * H + (k + 1))
                        act.wait_ge(S["s_pv"], head * U + max(n - 1, 0))
                        q.activation(pT[:, n % 2, 0, 512 * half:512 * half + w], ps[:, 4 + k % 2, 0:w],
                                     ACT.Copy).then_inc(S["s_ph"], 1)

                exps(0)
                exps(1)
                for n in range(U):
                    take_p(n)
                    if n + 2 < U:
                        exps(n + 2)

            def take_stacks(head, ftr, per, feva, stack_list, width):
                for n, dst in enumerate(stack_list):
                    act.wait_ge(ftr, head * per + (2 * n + 1))
                    q.activation(dst[:, 0:512], ps[0:width, (2 * n) % 8, :], ACT.Copy).then_inc(feva, 1)

            S = ATT["mla"]
            with act.Fori(0, HEADS) as h:
                fm = arena[:, 2048:6144].rearrange("p (a t n) -> p a t n", a=4, t=T)
                hb = arena[:, 0:2048].rearrange("p (t n) -> p t n", t=T)
                act.wait_ge(S["s_load"], h * 48 + 48)
                act.wait_ge(S["s_pv"], h * 8)
                round_hi(fm[:, 0, :, 0:96].bitcast(F32R), hb[:, :, 0:96], S["s_fhi"])
                round_hi(fm[:, 2, :, 0:96].bitcast(F32R), hb[:, :, 96:192], S["s_fhi"])
                round_hi(actT[:, 4096:5120].rearrange("p (t s n) -> p t s n", t=T, s=2)[:, :, 0, :],
                         hb[:, :, 192:256], S["s_fhi"])
                take_stacks(h, S["s_ftr"], 8, S["s_feva"],
                            [actT[0:MLA_DH, n * 1024:(n + 1) * 1024] for n in range(4)], MLA_DH)
                attend("mla", h)
            barrier(act, q, "nsa")
            S = ATT["nsa"]
            with act.Fori(0, GROUPS) as g:
                kb = arena[:, 0:2048].rearrange("p (t b n) -> p t b n", t=T, b=4)
                fm = arena[:, 2560:6656].rearrange("p (a t r n) -> p a t r n", a=4, t=T, r=2)
                fc = arena[:, 7680:7936].rearrange("p (s r n) -> p s r n", s=2, r=2)
                act.wait_ge(nsag["s_load"], g * 64 + 64)
                act.wait_ge(S["s_pv"], g * (4 * S["U"]))
                for b in range(2):
                    for r in range(2):
                        round_hi(fm[:, 2 * b, :, r, :].bitcast(F32R), kb[:, :, 2 * b, :], nsag["s_fhi"])
                    v = actT[:, 5120 + b * 1024:6144 + b * 1024].rearrange("p (t s n) -> p t s n", t=T, s=2)
                    round_hi(v[:, :, 0, :], kb[:, :, 2 * b + 1, :], nsag["s_fhi"])
                for r in range(2):
                    round_hi(fc[0:CMP, 0, r, :].bitcast(F32R), kcv[0:CMP, bass.ds(g, 1), :].rearrange("p a n -> p (a n)"),
                             nsag["s_fhi"])
                round_hi(actT[0:CMP, 7424:7488], kcv[0:CMP, bass.ds(g + 2, 1), :].rearrange("p a n -> p (a n)"),
                         nsag["s_fhi"])
                take_stacks(g, nsag["s_ftr"], 9, nsag["s_feva"], [actT[:, n * 1024:(n + 1) * 1024] for n in range(4)], P)
                act.wait_ge(nsag["s_ftr"], g * 9 + 9)
                q.activation(actT[:, 7168:7424], ps[:, 0, 0:256], ACT.Copy).then_inc(nsag["s_feva"], 1)
                with act.Fori(0, PER_GROUP) as hh:
                    h = g * PER_GROUP + hh
                    hb = arena[:, 2048:2560].rearrange("p (t n) -> p t n", t=T)
                    fq = arena[:, 6656:7680].rearrange("p (t r n) -> p t r n", t=T, r=2)
                    act.wait_ge(S["s_load"], h * 16 + 16)
                    act.wait_ge(S["s_pv"], h * S["U"])
                    round_hi(fq[:, :, 0, :].bitcast(F32R), hb, S["s_fhi"])
                    take_stacks(h, S["s_ftr"], 2, S["s_feva"], [actT[:, 4096:5120]], P)
                    attend("nsa", h)
            barrier(act, q, "otr0")
            take_hi("otr0", ORDER, None, None)
            barrier(act, q, "out0")
            barrier(act, q, "norm1")
            norm("norm1", 1)

            def mlp(layer):
                first = FIRST[f"mlp{layer}"]
                with act.Fori(0, FF_GROUPS) as g:
                    for idx, (half, f) in enumerate(((0, 0), (0, 1), (1, 0), (1, 1))):
                        if idx == 3:
                            act.wait_ge(s_wused, g * 2 + (first + 1))
                        else:
                            act.wait_ge(s_g1, g * 3 + (layer * 48 + idx + 1))
                        act.wait_ge(s_gt, g * 4 + (layer * 64 + max(idx - 1, 0)))
                        q.activation(relu[:, idx % 2, :], ps[:, idx, :], ACT.Relu).then_inc(s_gr, 1)
                        act.wait_ge(s_gt, g * 4 + (layer * 64 + idx + 1))
                        act.wait_ge(s_y, g * 15 + (layer * 240))
                        q.activation(gT[:, 0, f, half * 512:(half + 1) * 512], sq[:, idx % 2, :],
                                     ACT.Copy).then_inc(s_gh, 1)

            barrier(act, q, "mlp0")
            mlp(0)
            barrier(act, q, "ada1")
            barrier(act, q, "norm2")
            norm("norm2", 2)
            barrier(act, q, "proj1")
            for j in range(6):
                stored(j % 2)
                for t in range(T):
                    take(MM["proj1"] + 7 * j, FIRST["proj1"] + 2 * j + 2, "proj1", t, raw[:, j % 2, t, :], ps[:, t, :])
                if j < 4:
                    sqrt(64)
                    spill(j % 2, 10 + j, [(difv[:, :, j * 512:(j + 1) * 512], raw[:, j % 2, :, :])])
                else:
                    act.wait_ge(s_raw, RAW["proj1"] + 8 * (j + 1))
                    spill(j % 2, None, [(difv[:, :, j * 512:(j + 1) * 512], raw[:, j % 2, :, :])])
            stored(0, 1)
            barrier(act, q, "dif")
            S = ATT["dif"]
            with act.Fori(0, HEADS) as h:
                hb = arena[:, 0:3072].rearrange("p (t w m n) -> p t w m n", t=T, w=3, m=2)
                fm = arena[:, 3072:9216].rearrange("p (m a t r n) -> p m a t r n", m=2, a=3, t=T, r=2)
                v = actT[:, 6144:8192].rearrange("p (t s n) -> p t s n", t=T, s=2)
                act.wait_ge(S["s_load"], h * 48 + 48)
                act.wait_ge(S["s_pv"], h * S["U"])
                for m in range(2):
                    round_hi(fm[:, m, 0, :, 0, :].bitcast(F32R), hb[:, :, 0, m, :], S["s_fhi"])
                    for r in range(2):
                        round_hi(fm[:, m, 1, :, r, :].bitcast(F32R), hb[:, :, 1, m, :], S["s_fhi"])
                round_hi(v[:, :, 0, :], arena[:, 0:3072].rearrange("p (t n) -> p t n", t=T)[:, :, 256:384], S["s_fhi"])
                take_stacks(h, S["s_ftr"], 12, S["s_feva"], [actT[:, n * 1024:(n + 1) * 1024] for n in range(6)], P)
                attend("dif", h)
            barrier(act, q, "sub")
            sqrt(64)
            barrier(act, q, "otr1")
            take_hi("otr1", ORDER, None, None)
            barrier(act, q, "out1")
            barrier(act, q, "norm3")
            norm("norm3", 3)
            barrier(act, q, "mlp1")
            mlp(1)
            barrier(act, q, "end")

        @block.vector
        def _(dve):
            q = nc.vector
            own = Count(dve, s_dve)
            std = [0]
            procs = [0]

            dve.wait_ge(s_const, 16 * NCONST)
            dve.wait_ge(s_made, 1)
            for n in range(16):
                own.mark(q.memset(invf[:, n:n + 1], float(np.float32(THETA ** (-n / 16)))))
            for n in range(8):
                own.mark(q.memset(invf[:, 16 + n:17 + n], float(np.float32(THETA ** (-n / 8)))))
            own.mark(q.tensor_copy(post[:, :], posi[:, :]))
            own.mark(q.tensor_scalar(gainq[:, 0, :], gainq[:, 0, :], MLA_DH ** -0.5, None, ALU.mult))
            own.mark(q.tensor_scalar(gainh[:, 0, :], gainh[:, 0, :], DH ** -0.5, None, ALU.mult))
            own.mark(q.tensor_scalar(gainh[:, 4, :], gainh[:, 4, :], DH ** -0.5, None, ALU.mult))
            own.mark(q.tensor_scalar(gsub[:, :], gsub[:, :], 1.0 - LAM_INIT, None, ALU.mult))
            own.mark(q.tensor_tensor(lamt[:, 0, :], lamt[:, 0, :], lamt[:, 1, :], ALU.mult))
            own.mark(q.tensor_tensor(lamt[:, 2, :], lamt[:, 2, :], lamt[:, 3, :], ALU.mult))
            dve.wait_ge(s_cond, 1)
            own.mark(q.tensor_scalar(cond[:, 1, :], cond[:, 1, :], 1.0, None, ALU.add))
            own.sync()
            own.mark(q.reciprocal(cond[:, 1, :], cond[:, 1, :]))
            own.mark(q.tensor_reduce(lams[:, 0:1], lamt[:, 0, :], AX.X, ALU.add))
            own.mark(q.tensor_reduce(lams[:, 1:2], lamt[:, 2, :], AX.X, ALU.add))
            own.link(q.tensor_tensor(ang, post[:, :].unsqueeze(2).broadcast_to([P, T + 1, 24]),
                                     invf[:, :].unsqueeze(1).broadcast_to([P, T + 1, 24]), ALU.mult))
            q.tensor_copy(lams[:, 4:5], lams[:, 0:1]).then_inc(s_lam, 1)
            own.mark(q.tensor_tensor(cond[:, 0, :], cond[:, 0, :], cond[:, 1, :], ALU.mult))
            own.link(q.tensor_scalar(turns, ang, 1.0 / (2 * math.pi), 12582912.0, ALU.mult, ALU.add))
            own.link(q.tensor_scalar(turns, turns, -12582912.0, None, ALU.add))
            C1 = 6.28125
            C2 = float(np.float32(np.round((2 * math.pi - C1) * 2 ** 21) / 2 ** 21))
            C3 = 2 * math.pi - C1 - C2
            for cc in (C1, C2, C3):
                own.link(q.scalar_tensor_tensor(ang, turns, -cc, ang, ALU.mult, ALU.add))
            q.tensor_scalar(ang, ang, 3.1415925, -3.1415925, ALU.min, ALU.max).then_inc(s_ang, 1)
            dve.wait_ge(s_sin, 2)
            own.link(q.scalar_tensor_tensor(rope[:, 0, :, :], half_ang, -2.0, half_ang, ALU.mult, ALU.mult))
            own.mark(q.tensor_scalar(rope[:, 0, :, :], rope[:, 0, :, :], 1.0, None, ALU.add))
            dve.wait_ge(s_cond, 2)
            own.link(q.tensor_tensor(lams[:, 5:6], lams[:, 3:4], lams[:, 2:3], ALU.subtract))
            own.link(q.tensor_scalar(lams[:, 6:7], lams[:, 5:6], -LAM_INIT, None, ALU.add))

            def ada(layer):
                acc = arena[:, 8192:9216]
                landed = [layer * 6 * 16, layer * 6 * 16]
                landed[0] += layer * 6 * 16
                for g in range(6):
                    n = layer * 6 + g
                    if n >= 1:
                        dve.wait_ge(s_adamm, n)
                    for half in range(2):
                        landed[half] += 32 if half == 0 else 16
                        dve.wait_ge(s_adal[half], landed[half])
                        piece = arena[:, half * 4096:half * 4096 + 4096].rearrange("p (k n) -> p k n", k=4)
                        for k in range(4):
                            s = cond[:, 0, 4 * half + k:4 * half + k + 1]
                            last = half == 1 and k == 3
                            if half == 0 and k == 0:
                                ins = q.tensor_scalar(acc, piece[:, k, :], s, None, ALU.mult)
                            else:
                                ins = q.scalar_tensor_tensor(acc, piece[:, k, :], s, acc, ALU.mult, ALU.add)
                            if last:
                                ins.then_inc(s_adaacc, 1)
                            elif k == 3:
                                ins.then_inc(s_adau, 1)
                                dve.wait_ge(s_adau, n + 1)
                            else:
                                own.link(ins)
                    dve.wait_ge(s_adamm, n + 1)
                    if g in (2, 5):
                        q.tensor_copy(gates[:, g // 3, :], psf[:, 0:1024]).then_inc(s_adaev, 1)
                    elif g in (1, 4):
                        w = g // 3
                        q.scalar_tensor_tensor(modv[:, 2 * w, :], ps[:, 0, 0:KD], 1.0, normv[:, 2 * layer + w, :],
                                               ALU.add, ALU.mult).then_inc(s_adaev, 1)
                    else:
                        q.tensor_copy(modv[:, 2 * (g // 3) + 1, :], ps[:, 0, 0:KD]).then_inc(s_adaev, 1)

            def rstd(n, width, src):
                q.tensor_scalar(small[:, 1, 0:n], src, 1.0 / width, EPS, ALU.mult, ALU.add).then_inc(s_var, 1)
                std[0] += 1
                dve.wait_ge(s_std, std[0])
                own.link(q.reciprocal(small[:, 0, 0:n], small[:, 2, 0:n]))

            def norm(name, n):
                dve.wait_ge(s_ss, 8 * n + 8)
                rstd(T, D, small[:, 0, 0:T])
                for t in range(T):
                    q.tensor_scalar(arena[:, t * D:(t + 1) * D], xr[:, t, :], small[:, 0, t:t + 1], None,
                                    ALU.mult).then_inc(s_xn, 1)
                for idx, (k, half) in enumerate(ORDER):
                    take_lo(name, idx, k, half, arena[:, 8192 + (idx % 2) * 512:8704 + (idx % 2) * 512])

            def take_lo(name, idx, k, half, src):
                dve.wait_ge(s_trh, TR[name] + idx + 1)
                cols = slice(half * 512, (half + 1) * 512)
                q.tensor_tensor(aT[:, 1, k, cols], src, aT[:, 0, k, cols].bitcast(F32),
                                ALU.subtract).then_inc(s_trl, 1)

            def norm_rope(v, heads, width, gain, half, cols, tiles, scratch, done):
                pn, tn = v.shape[0], v.shape[1]
                n = tn * heads
                sqs = scratch[0:pn, 0:n * width].rearrange("p (t h n) -> p t h n", t=tn, h=heads)
                if procs[0]:
                    dve.wait_ge(done, procs[0])
                procs[0] += 1
                own.link(q.tensor_tensor(sqs, v, v, ALU.mult))
                own.link(q.tensor_reduce(small[0:pn, 0, 0:n], sqs, AX.X, ALU.add))
                q.tensor_scalar(small[0:pn, 1, 0:n], small[0:pn, 0, 0:n], 1.0 / width, EPS, ALU.mult,
                                ALU.add).then_inc(s_var, 1)
                std[0] += 1
                dve.wait_ge(s_std, std[0])
                own.link(q.reciprocal(small[0:pn, 0, 0:n], small[0:pn, 2, 0:n]))
                r = small[0:pn, 0, 0:n].rearrange("p (t h) -> p t h", t=tn)
                ins = q.tensor_tensor(v, v, r.unsqueeze(3).broadcast_to([pn, tn, heads, width]), ALU.mult)
                if gain is None:
                    ins.then_inc(done, 1)
                    return
                own.link(ins)
                own_gain = gain[0:pn].unsqueeze(1).unsqueeze(1).broadcast_to([pn, tn, heads, width])
                ins = q.tensor_tensor(v, v, own_gain, ALU.mult)
                if not half:
                    ins.then_inc(done, 1)
                    return
                own.link(ins)
                cos, sin = [rope[0:pn, m, tiles, cols].unsqueeze(2).broadcast_to([pn, tn, heads, half])
                            for m in range(2)]
                x1, x2 = v[:, :, :, 0:half], v[:, :, :, half:2 * half]
                tmp = [scratch[0:pn, m * n * half:(m + 1) * n * half].rearrange("p (t h n) -> p t h n", t=tn, h=heads)
                       for m in range(4)]
                for m, (a, b) in enumerate(((x1, cos), (x2, sin), (x1, sin), (x2, cos))):
                    own.mark(q.tensor_tensor(tmp[m], a, b, ALU.mult))
                own.sync()
                own.link(q.tensor_tensor(x1, tmp[0], tmp[1], ALU.subtract))
                q.tensor_tensor(x2, tmp[2], tmp[3], ALU.add).then_inc(done, 1)

            ada(0)
            barrier(dve, q, "norm0")
            dve.wait_ge(s_x, 16)
            norm("norm0", 0)
            barrier(dve, q, "proj0")
            alltiles = slice(0, T)
            dve.wait_ge(s_raw, 8)
            norm_rope(raw[:, 0, :, :].rearrange("p t (h n) -> p t h n", h=HEADS), HEADS, DH, gainh[:, 0, :], 8,
                      slice(16, 24), alltiles, arena, s_proc)
            dve.wait_ge(s_raw, 16)
            norm_rope(raw[:, 1, :, 256:384].rearrange("p t (h n) -> p t h n", h=2), 2, DH, gainh[:, 2, :], 8,
                      slice(16, 24), alltiles, arena, s_proc)
            dve.wait_ge(s_raw, 24)
            norm_rope(raw[:, 0, :, 0:128].rearrange("p t (h n) -> p t h n", h=2), 2, DH, gainh[:, 3, :], 8,
                      slice(16, 24), alltiles, arena, s_proc)
            dve.wait_ge(s_cond, 3)
            own.link(q.tensor_scalar(gate3[:, :, :], gate3[:, :, :], 1.0, None, ALU.add))
            own.mark(q.reciprocal(gate3[:, :, :], gate3[:, :, :]))
            dve.wait_ge(s_raw, 32)
            norm_rope(raw[:, 1, :, :].rearrange("p t (h n) -> p t h n", h=2), 2, RANK, None, 0,
                      None, alltiles, arena, s_proc)
            barrier(dve, q, "latent")
            for idx, (k, half) in enumerate([(k, h) for h in range(2) for k in range(4)]):
                take_lo("latent", idx, k, half, arena[:, 8192 + (idx % 2) * 512:8704 + (idx % 2) * 512])
            barrier(dve, q, "up")
            for hf in range(2):
                dve.wait_ge(s_raw, RAW["up"] + 4 * hf + 4)
                norm_rope(upq[hf].rearrange("p t (h n) -> p t h n", h=HEADS), HEADS, MLA_DH, gainq[:, 0, :], 16,
                          slice(0, 16), slice(4 * hf, 4 * hf + 4), arena[:, 8192:11264], s_proc)
            for hf in range(2):
                own.link(q.tensor_copy(upk[hf][:, :, :, 0:32],
                                       kpe[:, 4 * hf:4 * hf + 4, :].unsqueeze(2).broadcast_to([P, 4, HEADS, 32])))
                dve.wait_ge(s_raw, RAW["up"] + 8 + 4 * hf + 4)
                norm_rope(upk[hf][:, :, :, 0:96], HEADS, MLA_DH, gainq[:, 1, :], 16,
                          slice(0, 16), slice(4 * hf, 4 * hf + 4), arena[:, 8192:11264], s_proc)
            barrier(dve, q, "cmp")
            tt = xres[:, 4096:6144].rearrange("p (a i m) -> p a i m", a=4, i=8)
            blk = arena[:, 4096:8192].rearrange("p (i a m) -> p i a m", i=16, a=4)
            own.mark(q.memset(arena[:, 4096:8192], 0.0))
            for a in range(4):
                dve.wait_ge(s_cpe, a + 1)
                own.mark(q.tensor_copy(tt[:, a, :, :], ps[:, a, :].rearrange("p (i m) -> p i m", i=8)))
            own.sync()
            dve.wait_ge(s_cmp, 16 * 12)
            for j in range(2):
                for i in range(16):
                    o = i // 8
                    ins = q.tensor_scalar(blk[:, i, 2 * j:2 * j + 2, 0:CMP - 1], tt[:, 2 * j:2 * j + 2, i % 8, o:o + CMP - 1],
                                          arena[:, 10368 + j * 16 + i:10369 + j * 16 + i], None, ALU.add)
                    if i == 15:
                        ins.then_inc(s_cdve, 1)
            dve.wait_ge(s_cpe, 7)
            own.link(q.tensor_copy(kcv[0:CMP, :, :], ps[0:CMP, 6, 0:256].rearrange("p (a n) -> p a n", a=4)))
            norm_rope(kcv[0:CMP, 0:2, :].unsqueeze(1), 2, DH, gainh[:, 1, :], 8, slice(16, 24), slice(T, T + 1),
                      arena[:, 8448:10240], s_proc)
            own.mark(q.memset(arena[:, 7680:7936], 0.0))
            own.mark(q.memset(actT[:, 7424:7552].bitcast(F32), 0.0))
            barrier(dve, q, "mla")

            def minus_hi(dst, src, hi, done):
                q.tensor_tensor(dst, src, hi.bitcast(F32), ALU.subtract).then_inc(done, 1)

            def attend(name, head, turn, cols, dv, factor):
                S, units, U, H = ATT[name], UNITS[name], ATT[name]["U"], ATT[name]["H"]
                before = [sum(u["halves"] for u in units[:n]) for n in range(U + 1)]

                def maxima(n):
                    u = units[n]
                    dve.wait_ge(S["s_qk"], head * U + (n + 1))
                    base = (n % 2) * 1024
                    q.tensor_reduce(rows[:, 0, n:n + 1], psf[:, base:base + u["n"] * P], AX.X, ALU.max,
                                    negate=True).then_inc(S["s_mx"], 1)

                def take_p(n):
                    u = units[n]
                    for half in range(u["halves"]):
                        k = before[n] + half
                        w = min(4, u["n"] - 4 * half) * P
                        dve.wait_ge(S["s_ph"], head * H + (k + 1))
                        cols2 = slice(512 * half, 512 * half + w)
                        minus_hi(pT[:, n % 2, 1, cols2], ps[:, 4 + k % 2, 0:w], pT[:, n % 2, 0, cols2], S["s_pl"])

                def take_o(n):
                    u = units[n]
                    turn.link(q.reciprocal(rows[:, 2, n:n + 1], rows[:, 1, n:n + 1]))
                    f = rows[:, 2, n:n + 1]
                    for by in factor(u):
                        turn.link(q.tensor_tensor(f, f, by, ALU.mult))
                    dve.wait_ge(S["s_pv"], head * U + (n + 1))
                    dst = xr[:, u["t"], cols]
                    src = ps[:, 6 + n % 2, 0:dv]
                    if u["add"]:
                        dve.wait_ge(S["s_o"], head * U + n)
                        ins = q.scalar_tensor_tensor(dst, src, f, dst, ALU.mult, ALU.add)
                    else:
                        ins = q.tensor_scalar(dst, src, f, None, ALU.mult)
                    ins.then_inc(S["s_o"], 1)

                maxima(0)
                maxima(1)
                for n in range(U):
                    take_p(n)
                    if n >= 1:
                        take_o(n - 1)
                    if n + 2 < U:
                        maxima(n + 2)
                take_o(U - 1)

            def take_stacks(head, ftr, per, fevd, stack_list, width):
                for n, dst in enumerate(stack_list):
                    dve.wait_ge(ftr, head * per + (2 * n + 2))
                    q.tensor_copy(dst[:, 512:1024], ps[0:width, (2 * n + 1) % 8, :]).then_inc(fevd, 1)

            S = ATT["mla"]
            turn = Count(dve, S["s_own"])
            with dve.Fori(0, HEADS) as h:
                turn.enter(h, 8)
                fm = arena[:, 2048:6144].rearrange("p (a t n) -> p a t n", a=4, t=T)
                hb = arena[:, 0:2048].rearrange("p (t n) -> p t n", t=T)
                v = actT[:, 4096:5120].rearrange("p (t s n) -> p t s n", t=T, s=2)
                dve.wait_ge(S["s_fhi"], h * 3 + 1)
                minus_hi(fm[:, 1, :, 0:96], hb[:, :, 0:96], fm[:, 0, :, 0:96], S["s_fmt"])
                dve.wait_ge(S["s_fhi"], h * 3 + 2)
                minus_hi(fm[:, 3, :, 0:96], hb[:, :, 96:192], fm[:, 2, :, 0:96], S["s_fmt"])
                dve.wait_ge(S["s_fhi"], h * 3 + 3)
                minus_hi(v[:, :, 1, :], hb[:, :, 192:256], v[:, :, 0, :], S["s_fmt"])
                take_stacks(h, S["s_ftr"], 8, S["s_fevd"],
                            [actT[0:MLA_DH, n * 1024:(n + 1) * 1024] for n in range(4)], MLA_DH)
                attend("mla", h, turn, bass.ds(h * DH, DH), MLA_V, lambda u: [])
            turn.leave(8, HEADS)
            barrier(dve, q, "nsa")
            S = ATT["nsa"]
            turn = Count(dve, S["s_own"])
            with dve.Fori(0, GROUPS) as g:
                kb = arena[:, 0:2048].rearrange("p (t b n) -> p t b n", t=T, b=4)
                fm = arena[:, 2560:6656].rearrange("p (a t r n) -> p a t r n", a=4, t=T, r=2)
                fc = arena[:, 7680:7936].rearrange("p (s r n) -> p s r n", s=2, r=2)
                for b in range(2):
                    dve.wait_ge(nsag["s_fhi"], g * 9 + (3 * b + 3))
                    src = kb[:, :, 2 * b:2 * b + 1, :].broadcast_to([P, T, 2, DH])
                    minus_hi(fm[:, 2 * b + 1, :, :, :], src, fm[:, 2 * b, :, :, :], nsag["s_fmt"])
                    v = actT[:, 5120 + b * 1024:6144 + b * 1024].rearrange("p (t s n) -> p t s n", t=T, s=2)
                    minus_hi(v[:, :, 1, :], kb[:, :, 2 * b + 1, :], v[:, :, 0, :], nsag["s_fmt"])
                dve.wait_ge(nsag["s_fhi"], g * 9 + 9)
                minus_hi(fc[0:CMP, 1, :, :], kcv[0:CMP, bass.ds(g, 1), :].broadcast_to([CMP, 2, DH]),
                         fc[0:CMP, 0, :, :], nsag["s_fmt"])
                minus_hi(actT[0:CMP, 7488:7552], kcv[0:CMP, bass.ds(g + 2, 1), :].rearrange("p a n -> p (a n)"),
                         actT[0:CMP, 7424:7488], nsag["s_fmt"])
                take_stacks(g, nsag["s_ftr"], 9, nsag["s_fevd"], [actT[:, n * 1024:(n + 1) * 1024] for n in range(4)], P)
                with dve.Fori(0, PER_GROUP) as hh:
                    h = g * PER_GROUP + hh
                    turn.enter(h, 49)
                    hb = arena[:, 2048:2560].rearrange("p (t n) -> p t n", t=T)
                    fq = arena[:, 6656:7680].rearrange("p (t r n) -> p t r n", t=T, r=2)
                    dve.wait_ge(S["s_fhi"], h + 1)
                    minus_hi(fq[:, :, 1, :], hb, fq[:, :, 0, :], S["s_fmt"])
                    take_stacks(h, S["s_ftr"], 2, S["s_fevd"], [actT[:, 4096:5120]], P)

                    def factor(u):
                        by = [gate3[:, u["t"], bass.ds(g * PER_GROUP + hh + 8 * u["factor"], 1)]]
                        return by + ([valid[:, :]] if u["kind"] == "cmp" and u["t"] == 0 else [])

                    attend("nsa", h, turn, bass.ds(h * DH + 512, DH), DH, factor)
                    assert turn.k == 49, turn.k
            turn.leave(49, HEADS)
            barrier(dve, q, "otr0")

            def otr(name):
                for idx, (k, half) in enumerate(ORDER):
                    take_lo(name, idx, k, half, ps[:, idx % 8, :])

            def residual(name, loads):
                dve.wait_ge(s_x, loads)
                for j in range(2):
                    for t in range(T):
                        if t == T - 1:
                            dve.wait_ge(s_wused, FIRST[name] + 2 * j + 2)
                        else:
                            dve.wait_ge(s_mm, MM[name] + 7 * j + t + 1)
                        dst = xr[:, t, j * 512:(j + 1) * 512]
                        q.tensor_tensor(dst, dst, ps[:, t, :], ALU.add).then_inc(s_raw, 1)

            def mlp(layer):
                first = FIRST[f"mlp{layer}"]
                with dve.Fori(0, FF_GROUPS) as g:
                    for idx, (half, f) in enumerate(((0, 0), (0, 1), (1, 0), (1, 1))):
                        dve.wait_ge(s_gr, g * 4 + (layer * 64 + idx + 1))
                        dve.wait_ge(s_gh, g * 4 + (layer * 64 + max(idx - 1, 0)))
                        dve.wait_ge(s_gl, g * 4 + (layer * 64 + max(idx - 1, 0)))
                        q.scalar_tensor_tensor(sq[:, idx % 2, :], ps[:, idx, :], 0.0, relu[:, idx % 2, :],
                                               ALU.max, ALU.mult).then_inc(s_gt, 1)
                        dve.wait_ge(s_gh, g * 4 + (layer * 64 + idx + 1))
                        cols = slice(half * 512, (half + 1) * 512)
                        q.tensor_tensor(gT[:, 1, f, cols], sq[:, idx % 2, :], gT[:, 0, f, cols].bitcast(F32),
                                        ALU.subtract).then_inc(s_gl, 1)
                    for idx in range(16):
                        if idx == 15:
                            dve.wait_ge(s_wused, g * 2 + (first + 2))
                        else:
                            dve.wait_ge(s_y, g * 15 + (layer * 240 + idx + 1))
                        t, n = idx // 2, idx % 2
                        dve.wait_ge(s_ya, g * 16 + layer * 256)
                        dst = xr[:, t, n * 512:(n + 1) * 512]
                        q.tensor_tensor(dst, dst, ps[:, 4 + idx % 4, :], ALU.add).then_inc(s_ya, 1)

            otr("otr0")
            barrier(dve, q, "out0")
            residual("out0", 32)
            barrier(dve, q, "norm1")
            norm("norm1", 1)
            barrier(dve, q, "mlp0")
            mlp(0)
            barrier(dve, q, "ada1")
            ada(1)
            barrier(dve, q, "norm2")
            dve.wait_ge(s_xs, 16)
            norm("norm2", 2)
            barrier(dve, q, "proj1")
            for j in range(4):
                dve.wait_ge(s_raw, RAW["proj1"] + 8 * (j + 1))
                norm_rope(raw[:, j % 2, :, :].rearrange("p t (h n) -> p t h n", h=HEADS), HEADS, DH,
                          gainh[:, 4 + j // 2, :], 8, slice(16, 24), alltiles, arena, s_proc)
            barrier(dve, q, "dif")
            S = ATT["dif"]
            turn = Count(dve, S["s_own"])
            with dve.Fori(0, HEADS) as h:
                turn.enter(h, 24)
                hb = arena[:, 0:3072].rearrange("p (t w m n) -> p t w m n", t=T, w=3, m=2)
                fm = arena[:, 3072:9216].rearrange("p (m a t r n) -> p m a t r n", m=2, a=3, t=T, r=2)
                v = actT[:, 6144:8192].rearrange("p (t s n) -> p t s n", t=T, s=2)
                for m in range(2):
                    dve.wait_ge(S["s_fhi"], h * 7 + (3 * m + 3))
                    minus_hi(fm[:, m, 0, :, 1, :], hb[:, :, 0, m, :], fm[:, m, 0, :, 0, :], S["s_fmt"])
                    src = hb[:, :, 1, m, :].unsqueeze(2).broadcast_to([P, T, 2, DH])
                    minus_hi(fm[:, m, 2, :, :, :], src, fm[:, m, 1, :, :, :], S["s_fmt"])
                dve.wait_ge(S["s_fhi"], h * 7 + 7)
                minus_hi(v[:, :, 1, :], arena[:, 0:3072].rearrange("p (t n) -> p t n", t=T)[:, :, 256:384],
                         v[:, :, 0, :], S["s_fmt"])
                take_stacks(h, S["s_ftr"], 12, S["s_fevd"], [actT[:, n * 1024:(n + 1) * 1024] for n in range(6)], P)
                attend("dif", h, turn, bass.ds(h * 2 * DH, 2 * DH), 2 * DH,
                       lambda u: [lams[:, 6:7]] if u["factor"] else [])
            turn.leave(24, HEADS)
            barrier(dve, q, "sub")
            norm_rope(xr[:, :, :].rearrange("p t (h n) -> p t h n", h=HEADS), HEADS, 2 * DH, gsub[:, :], 0,
                      None, alltiles, arena, s_proc)
            barrier(dve, q, "otr1")
            otr("otr1")
            barrier(dve, q, "out1")
            residual("out1", 48)
            barrier(dve, q, "norm3")
            norm("norm3", 3)
            barrier(dve, q, "mlp1")
            mlp(1)
            barrier(dve, q, "end")


_INS = ['x', 'c', 'positions', 'ada_w', 'ada_b', 'norm_mix', 'norm_mlp', 'mlp_w1', 'mlp_w2', 'hy_w_in', 'hy_w_out',
        'mla_q_norm', 'mla_w_uq', 'mla_kv_norm', 'mla_w_ukv', 'mla_q_gain', 'mla_k_gain', 'nsa_q_gain',
        'nsa_k_gain', 'nsa_cmp_pos', 'nsa_cmp_w1', 'nsa_cmp_w2', 'diff_w_qkv', 'diff_w_out', 'diff_q_gain',
        'diff_k_gain', 'diff_lambda', 'diff_sub_gain']


def kernel(**inputs):
    import numpy as _np
    import concourse.bacc as _bacc
    from concourse import mybir as _mybir
    from concourse.bass_utils import run_bass_kernel_spmd as _run

    nc = _bacc.Bacc("TRN2", target_bir_lowering=False, num_devices=1, dynamic_dma_scratch_size=512)
    arrays, args = {}, []
    for name in _INS:
        a = _np.ascontiguousarray(inputs[name])
        arrays[f"in_{name}"] = a
        args.append(nc.dram_tensor(f"in_{name}", a.shape, _mybir.dt.from_np(a.dtype), kind="ExternalInput").ap())
    o = nc.dram_tensor("out_0", inputs["x"].shape, _mybir.dt.float32, kind="ExternalOutput").ap()
    trunk(nc, *args, o)
    r = _run(nc, [arrays], core_ids=[0])
    return r.results[0]["out_0"]
```

```python
import math
from contextlib import ExitStack

import numpy as np

import concourse.bass as bass
from concourse import mybir

F32 = mybir.dt.float32
F32R = mybir.dt.float32r
I32 = mybir.dt.int32
ACT = mybir.ActivationFunctionType
ALU = mybir.AluOpType
AX = mybir.AxisListType

P = 128
SEQ = 1024
T = SEQ // P
D = 1024
KD = D // P
DFF = 4096
NEG = -1e30
EPS = 1e-6
THETA = 500000.0

HEADS = 8
DH = 64
MLA_DH, MLA_ROPE, MLA_NOPE, MLA_V, RANK = 96, 32, 64, 64, 256
GROUPS, PER_GROUP = 2, 4
WINDOW_TILES = 512 // P
CMP = 64
LATENT_W = 2 * RANK
NQ0 = LATENT_W + MLA_ROPE
NKV0 = NQ0 + HEADS * DH
GATE0 = NKV0 + 768
HY_IN = GATE0 + 24

WCH = 2048
FFG = 256
FF_GROUPS = DFF // FFG
TURN = 4
TURNS = HEADS // TURN
LAM_INIT = 0.8 - 0.6 * math.exp(-0.3)


class Count:

    def __init__(self, eng, sem):
        self.eng, self.sem, self.base, self.k, self.off = eng, sem, 0, 0, 0

    def enter(self, turn, per):
        self.base, self.k, self.off = self.base + self.k, 0, turn * per

    def leave(self, per, times):
        assert self.k == per, (self.k, per)
        self.base, self.k, self.off = self.base + per * times, 0, 0

    def mark(self, ins):
        self.k += 1
        ins.then_inc(self.sem, 1)

    def sync(self):
        self.eng.wait_ge(self.sem, self.off + (self.base + self.k))

    def link(self, ins):
        self.mark(ins)
        self.sync()


def trunk(nc, x, c, positions, ada_w, ada_b, norm_mix, norm_mlp, mlp_w1, mlp_w2, hy_w_in, hy_w_out,
          mla_q_norm, mla_w_uq, mla_kv_norm, mla_w_ukv, mla_q_gain, mla_k_gain, nsa_q_gain,
          nsa_k_gain, nsa_cmp_pos, nsa_cmp_w1, nsa_cmp_w2, diff_w_qkv, diff_w_out, diff_q_gain,
          diff_k_gain, diff_lambda, diff_sub_gain, out):
    ctx = ExitStack()
    with ctx:
        ctx.enter_context(nc.allow_non_contiguous_dma(reason="small vectors are loaded transposed"))

        def sb(name, shape, dt=F32):
            return ctx.enter_context(nc.sbuf_tensor(name, shape, dt))

        def sem(name):
            return ctx.enter_context(nc.semaphore(name))

        actT = sb("actT", [P, 2 * KD * SEQ], F32R)
        wts = sb("wts", [P, 2, 2, WCH], F32R)
        gT = sb("gT", [P, 2, FFG // P, SEQ], F32R)
        xres = sb("xres", [P, T * D])
        stage = sb("stage", [P, 2, WCH])
        arena = sb("arena", [P, 11264])
        gates = sb("gates", [P, 2, D])
        ident = sb("ident", [P, P])
        identr = sb("identr", [P, P], F32R)
        masks = sb("masks", [P, 3 * P], F32R)
        cmask = sb("cmask", [P, 184], F32R)
        ones = sb("ones", [P, P])
        rope = sb("rope", [P, 2, T + 1, 24])
        post = sb("post", [P, T + 1])
        posi = sb("posi", [P, T + 1], I32)
        cond = sb("cond", [P, 2, KD])
        normv = sb("normv", [P, 4, KD])
        latv = sb("latv", [P, 4])
        modv = sb("modv", [P, 4, KD])
        gainq = sb("gainq", [P, 2, 96])
        gainh = sb("gainh", [P, 6, DH])
        gsub = sb("gsub", [P, 2 * DH])
        lams = sb("lams", [P, 8])
        small = sb("small", [P, 3, T * 8])
        rows = sb("rows", [P, 3, 8])
        gate3 = sb("gate3", [P, T, 24])
        kpe = sb("kpe", [P, T, MLA_ROPE])
        lamt = kpe[:, :, :].rearrange("p t n -> p (t n)").rearrange("p (a n) -> p a n", a=4)
        kcv = arena[:, 7936:8192].rearrange("p (a n) -> p a n", a=4)
        xtra = gates[:, 1, :]
        valid = sb("valid", [P, 1])
        ps = ctx.enter_context(nc.psum_tensor("ps", [P, 8, 512], F32))
        psf = ps[:, :, :].rearrange("p b n -> p (b n)")

        xsave = nc.dram_tensor("xsave", (SEQ, D), F32).ap()
        nsad = nc.dram_tensor("nsad", (SEQ, 1280), F32).ap()
        mlad = nc.dram_tensor("mlad", (SEQ, 2048), F32).ap()
        difd = nc.dram_tensor("difd", (SEQ, 3072), F32).ap()

        aT = actT[:, :].rearrange("p (s k t) -> p s k t", s=2, k=KD)
        xr = xres[:, :].rearrange("p (t d) -> p t d", t=T)
        raw = xres[:, :].rearrange("p (s t n) -> p s t n", s=2, t=T)
        x_in = x.rearrange("b (t p) d -> p (b t) d", p=P)
        x_sv = xsave.rearrange("(t p) d -> p t d", p=P)
        x_out = out.rearrange("b (t p) d -> p (b t) d", p=P)
        nsav = nsad.rearrange("(t p) n -> p t n", p=P)
        mlav = mlad.rearrange("(t p) n -> p t n", p=P)
        difv = difd.rearrange("(t p) n -> p t n", p=P)

        s_const = sem("s_const")
        s_posz = sem("s_posz")
        s_made = sem("s_made")
        s_stage = [sem("s_stage0"), sem("s_stage1")]
        s_wready = sem("s_wready")
        s_wused = sem("s_wused")
        s_tick = sem("s_tick")
        s_pool = sem("s_pool")
        s_dve = sem("s_dve")
        s_act = sem("s_act")
        s_bar = sem("s_bar")
        s_adal = [sem("s_adal0"), sem("s_adal1")]
        s_adau = sem("s_adau")
        s_adaacc = sem("s_adaacc")
        s_adamm = sem("s_adamm")
        s_adaev = sem("s_adaev")
        s_x = sem("s_x")
        s_ss = sem("s_ss")
        s_var = sem("s_var")
        s_std = sem("s_std")
        s_xn = sem("s_xn")
        s_tr = sem("s_tr")
        s_trh = sem("s_trh")
        s_trl = sem("s_trl")
        s_mm = sem("s_mm")
        s_raw = sem("s_raw")
        s_proc = sem("s_proc")
        s_spill = [sem("s_spill0"), sem("s_spill1")]
        s_cmp = sem("s_cmp")
        s_cpe = sem("s_cpe")
        s_cact = sem("s_cact")
        s_cdve = sem("s_cdve")
        s_out = sem("s_out")
        s_xs = sem("s_xs")
        s_ones = sem("s_ones")

        s_cond = sem("s_cond")
        s_lam = sem("s_lam")
        s_ang = sem("s_ang")
        s_sin = sem("s_sin")
        s_g1 = sem("s_g1")
        s_gr = sem("s_gr")
        s_gt = sem("s_gt")
        s_gh = sem("s_gh")
        s_gl = sem("s_gl")
        s_y = sem("s_y")
        s_ya = sem("s_ya")

        pexp = arena[:, 9216:11264].rearrange("p (s n) -> p s n", s=2)
        pT = gT
        relu = arena[:, 0:1024].rearrange("p (s n) -> p s n", s=2)
        sq = arena[:, 1024:2048].rearrange("p (s n) -> p s n", s=2)
        upq = [xres[:, 0:3072].rearrange("p (t n) -> p t n", t=4),
               arena[:, 0:3072].rearrange("p (t n) -> p t n", t=4)]
        upk = [xres[:, 3072:8192].rearrange("p (t h n) -> p t h n", t=4, h=HEADS),
               arena[:, 3072:8192].rearrange("p (t h n) -> p t h n", t=4, h=HEADS)]
        ang = xtra[:, 0:216].rearrange("p (t n) -> p t n", t=T + 1)
        turns = xtra[:, 216:432].rearrange("p (t n) -> p t n", t=T + 1)
        half_ang = xtra[:, 432:648].rearrange("p (t n) -> p t n", t=T + 1)
        invf = xtra[:, 648:672]
        NCONST = 22
        ORDER = [(k, half) for half in range(2) for k in range(KD)]

        block = ctx.enter_context(nc.Block())

        STAGES = ["norm0", "proj0", "latent", "up", "cmp", "mla", "nsa", "otr0", "out0", "norm1", "mlp0",
                  "ada1", "norm2", "proj1", "dif", "sub", "otr1", "out1", "norm3", "mlp1", "end"]
        BAR = {name: n + 1 for n, name in enumerate(STAGES)}

        def barrier(eng, q, stage):
            q.drain().then_inc(s_bar, 1)
            eng.wait_ge(s_bar, 3 * BAR[stage])

        TR = {"norm0": 0, "latent": 16, "otr0": 24, "norm1": 40, "norm2": 56, "otr1": 72, "norm3": 88}
        MM = {"proj0": 0, "up": 28, "out0": 42, "proj1": 56, "out1": 98}
        RAW = {"proj0": 0, "up": 32, "out0": 48, "proj1": 64, "out1": 112}

        def unit(t, kind, k0, nblk, add, factor):
            return dict(t=t, kind=kind, k0=k0, n=nblk, add=add, factor=factor, halves=(nblk + 3) // 4)

        UNITS = {"mla": [unit(t, "full", 0, t + 1, False, None) for t in range(T)],
                 "nsa": [u for t in range(T) for u in (
                     unit(t, "slc", 0, t + 1, False, 1),
                     unit(t, "win", max(0, t - WINDOW_TILES), min(t, WINDOW_TILES) + 1, True, 2),
                     unit(t, "cmp", 0, 1, True, 0))],
                 "dif": [unit(t, f"map{m}", 0, t + 1, m == 1, m) for t in range(T) for m in range(2)]}
        ATT = {}
        for name, prep, steps in (("mla", 8, [2, 2, 3, 3, 4, 4, 5, 5]), ("nsa", 2, [12, 13]),
                                  ("dif", 12, list(range(2, 14)))):
            S = {k: sem(f"{name}_{k}") for k in (
                "s_load",
                "s_fhi",
                "s_fmt",
                "s_ftr",
                "s_feva",
                "s_fevd",
                "s_qk",
                "s_mx",
                "s_ex",
                "s_t",
                "s_ph",
                "s_pl",
                "s_pv",
                "s_o",
                "s_own",
                )}
            U = len(UNITS[name])
            S["U"], S["UT"], S["prep"] = U, U * TURN, prep
            S["units"] = [dict(u, head=i) for i in range(TURN) for u in UNITS[name]]
            S["before"] = [sum(u["halves"] for u in S["units"][:n]) for n in range(S["UT"] + 1)]
            S["HT"] = S["before"][-1]
            S["at"] = [[] for _ in S["units"]]
            for i in range(1, TURN):
                for b, step in enumerate(steps):
                    S["at"][(i - 1) * U + step].append((i, b))
            S["uses"] = [("stack", 0, b) for b in range(prep)]
            for n, u in enumerate(S["units"]):
                S["uses"] += [("half", n, half) for half in range(u["halves"])]
                S["uses"] += [("stack", i, b) for i, b in S["at"][n]]
            ATT[name] = S
        VW = {"mla": 2 * MLA_V + 2, "nsa": 2 * DH + 2, "dif": 4 * DH}
        NSA_V = [5120, 5120 + T * VW["nsa"]]
        NSA_CK = NSA_V[1] + T * VW["nsa"]
        NSA_CV = NSA_CK + 2 * P
        nsag = {k: sem(f"nsag_{k}") for k in ("s_load", "s_fhi", "s_fmt", "s_ftr", "s_feva", "s_fevd")}
        for name in ATT:
            ATT[name]["pv0"] = ATT[name]["U"] + 1

        def dve_takes(i, b):
            return i == 0 and b % 2 == 1

        def stacks_taken(S, i, b, eng):
            order = [(0, c) for c in range(S["prep"])] + [x for step in S["at"] for x in step]
            upto = order[:order.index((i, b)) + 1]
            return sum(dve_takes(*x) == bool(eng) for x in upto)

        def stacks_done(S, i, b):
            return ([(0, c) for c in range(S["prep"])] + [x for step in S["at"] for x in step]).index((i, b)) + 1

        stack_slots = {
            "mla": lambda i, b: actT[0:MLA_DH, (i % 2) * 8192 + b * 512:(i % 2) * 8192 + (b + 1) * 512],
            "nsa": lambda i, b: actT[:, 8192 + (i % 2) * 1024 + b * 512:8192 + (i % 2) * 1024 + (b + 1) * 512],
            "dif": lambda i, b: actT[:, (i % 2) * 8192 + b * 512:(i % 2) * 8192 + (b + 1) * 512]}
        ATT["mla"]["nfmt"], ATT["nsa"]["nfmt"], ATT["dif"]["nfmt"] = 3, 1, 5

        def wview(a, row0, nk, c0, n):
            return a[row0:row0 + nk * P, c0:c0 + n].rearrange("(k p) n -> p k n", p=P)

        HYC = [[(NQ0, 512)], [(NKV0, 512)], [(NKV0 + 512, 280), (LATENT_W, 32)], [(0, 512)]]
        PROJ0 = []
        for cols in HYC:
            for kh in range(2):
                PROJ0.append(("cols", hy_w_in[0], kh * 512, 4, cols, None))
        PROJ0.append(("cols", mla_w_uq[0], 0, 2, [(0, 768)], None))
        PROJ0.append(("cols", mla_w_ukv[0], 0, 2, [(0, 1024)], None))
        OUT0 = [("cols", hy_w_out[0], kh * 512, 4, [(n * 512, 512)], (0, n * 512, 512))
                for n in range(2) for kh in range(2)]
        PROJ1 = [("cols", diff_w_qkv[0], kh * 512, 4, [(n * 512, 512)], None)
                 for n in range(6) for kh in range(2)]
        OUT1 = [("cols", diff_w_out[0], kh * 512, 4, [(n * 512, 512)], (0, n * 512, 512))
                for n in range(2) for kh in range(2)]
        FIRST = {"proj0": 0}
        FIRST["out0"] = len(PROJ0)
        FIRST["mlp0"] = FIRST["out0"] + len(OUT0)
        FIRST["proj1"] = FIRST["mlp0"] + 2 * FF_GROUPS
        FIRST["out1"] = FIRST["proj1"] + len(PROJ1)
        FIRST["mlp1"] = FIRST["out1"] + len(OUT1)
        assert all(v % 2 == 0 for v in FIRST.values())

        def mlp_views(layer, g):
            w1 = mlp_w1[layer].rearrange("(k p) n -> p k n", p=P)[:, :, bass.ds(g * FFG, FFG)]
            w2 = mlp_w2[layer].rearrange("(q p) n -> p q n", p=P)[:, bass.ds(g * 2, 2), :]
            return w1, w2

        @block.sync
        def _(sp):
            def load(dst, src, s):
                sp.dma_start(dst, src).then_inc(s, 16)

            sp.wait_ge(s_posz, 1)
            load(posi[:, 0:T], positions.rearrange("b (t p) -> p (b t)", p=P), s_const)
            load(posi[0:CMP - 1, T:T + 1], positions[0:1, 31:SEQ:16].rearrange("b c -> c b"), s_const)
            load(cond[:, 0, :], c.rearrange("b (p k) -> p (b k)", p=P), s_const)
            for i in range(2):
                load(normv[:, 2 * i, :], norm_mix[i:i + 1, :].rearrange("b (k p) -> p (b k)", p=P), s_const)
                load(normv[:, 2 * i + 1, :], norm_mlp[i:i + 1, :].rearrange("b (k p) -> p (b k)", p=P), s_const)
            load(latv[:, 0:2], mla_q_norm.rearrange("b (k p) -> p (b k)", p=P), s_const)
            load(latv[:, 2:4], mla_kv_norm.rearrange("b (k p) -> p (b k)", p=P), s_const)
            load(gainq[:, 0, :], mla_q_gain.broadcast_to([P, 96]), s_const)
            load(gainq[:, 1, :], mla_k_gain.broadcast_to([P, 96]), s_const)
            load(gainh[:, 0, :], nsa_q_gain.broadcast_to([P, DH]), s_const)
            for b in range(3):
                load(gainh[:, 1 + b, :], nsa_k_gain[0, b:b + 1, :].broadcast_to([P, DH]), s_const)
            load(gainh[:, 4, :], diff_q_gain.broadcast_to([P, DH]), s_const)
            load(gainh[:, 5, :], diff_k_gain.broadcast_to([P, DH]), s_const)
            load(gsub[:, :], diff_sub_gain.broadcast_to([P, 2 * DH]), s_const)
            for b in range(4):
                load(lamt[:, b, :], diff_lambda[0, b:b + 1, :].broadcast_to([P, DH]), s_const)

            def chunk(n, kind):
                _, w, row0, nk, cols, _ = kind
                if n >= 2:
                    sp.wait_ge(s_wready, n - 1)
                width = sum(m for _, m in cols)
                dst = stage[:, n % 2, 0:nk * width].rearrange("p (k n) -> p k n", k=nk)
                at = 0
                for c0, m in cols:
                    load(dst[:, :, at:at + m], wview(w, row0, nk, c0, m), s_stage[n % 2])
                    at += m

            def ada(layer):
                w = ada_w[layer].rearrange("(p k) n -> p k n", k=KD)
                for g in range(6):
                    for half in range(2):
                        n = layer * 12 + g * 2 + half
                        if n >= 2:
                            sp.wait_ge(s_adaacc if half else s_adau, n // 2)
                        dst = arena[:, (n % 2) * 4096:(n % 2) * 4096 + 4096].rearrange("p (k n) -> p k n", k=4)
                        load(dst, w[:, 4 * half:4 * half + 4, g * 1024:(g + 1) * 1024], s_adal[n % 2])
                        if half == 0:
                            load(arena[0:1, 9216 + (g % 2) * 1024:10240 + (g % 2) * 1024],
                                 ada_b[layer:layer + 1, g * 1024:(g + 1) * 1024], s_adal[n % 2])

            def mlp(layer):
                with sp.Fori(0, FF_GROUPS) as g:
                    w1, w2 = mlp_views(layer, g)
                    first = FIRST[f"mlp{layer}"]
                    sp.wait_ge(s_wready, g * 2 + first - 1)
                    load(stage[:, 0, :].rearrange("p (k n) -> p k n", k=KD), w1, s_stage[0])
                    sp.wait_ge(s_wready, g * 2 + first)
                    load(stage[:, 1, :].rearrange("p (k n) -> p k n", k=2), w2, s_stage[1])

            load(xr, x_in, s_x)
            chunk(0, PROJ0[0])
            chunk(1, PROJ0[1])
            ada(0)
            for n in range(2, len(PROJ0)):
                chunk(n, PROJ0[n])
            for n, kind in enumerate(OUT0):
                chunk(FIRST["out0"] + n, kind)
            sp.wait_ge(s_bar, 3 * BAR["cmp"])
            for a in range(4):
                load(xres[0:CMP, a * 1024:(a + 1) * 1024].rearrange("p (l n) -> p l n", l=16),
                     nsad[:, 512 + a * DH:512 + (a + 1) * DH].rearrange("(m l) n -> m l n", l=16), s_cmp)
            for j in range(2):
                load(arena[:, j * 2048:(j + 1) * 2048].rearrange("p (i n) -> p i n", i=16),
                     nsa_cmp_w1[0, j].rearrange("(i q) n -> q i n", q=P), s_cmp)
                load(arena[:, 10240 + j * 64:10304 + j * 64], nsa_cmp_w2[0, j], s_cmp)
                for par in range(2):
                    load(arena[64 * par:64 * par + 64, 10368 + j * 16:10384 + j * 16],
                         nsa_cmp_pos[0, j].rearrange("(i r) d -> r d i", r=2)[par], s_cmp)
            sp.wait_ge(s_bar, 3 * BAR["mla"])
            mla = ATT["mla"]
            with sp.Fori(0, HEADS) as h:
                sp.wait_ge(mla["s_fmt"], h * 3 + 1)
                src = [mlav[:, :, bass.ds(h * 96, 96)], mlav[:, :, bass.ds(h * 96 + 768, 96)],
                       mlav[:, :, bass.ds(h * 64 + 1536, 64)]]
                hb = arena[:, 0:T * 256].rearrange("p (t n) -> p t n", t=T)
                load(hb[:, :, 0:96], src[0], mla["s_load"])
                load(hb[:, :, 96:192], src[1], mla["s_load"])
                load(hb[:, :, 192:256], src[2], mla["s_load"])
            sp.wait_ge(s_bar, 3 * BAR["nsa"])
            nsa = ATT["nsa"]
            with sp.Fori(0, GROUPS) as g:
                sp.wait_ge(nsag["s_fmt"], g * 6 + 1)
                kb = arena[:, 0:T * 256].rearrange("p (t n) -> p t n", t=T)
                for m, col in enumerate([768, 768 + 128, 1024, 1024 + 128]):
                    load(kb[:, :, m * 64:(m + 1) * 64], nsav[:, :, bass.ds(g * 64 + col, 64)], nsag["s_load"])
                with sp.Fori(0, PER_GROUP) as hh:
                    sp.wait_ge(nsa["s_fmt"], g * PER_GROUP + hh + 1)
                    sp.sem_inc(s_tick, 1)
                    load(arena[:, 2048:2560].rearrange("p (t n) -> p t n", t=T),
                         nsav[:, :, bass.ds((g * PER_GROUP + hh) * 64, 64)], nsa["s_load"])
            sp.wait_ge(s_bar, 3 * BAR["out0"])
            load(xr, x_in, s_x)
            mlp(0)
            sp.wait_ge(s_bar, 3 * BAR["ada1"])
            load(x_sv, xr, s_xs)
            n0 = FIRST["proj1"]
            chunk(n0, PROJ1[0])
            chunk(n0 + 1, PROJ1[1])
            ada(1)
            for n in range(2, len(PROJ1)):
                chunk(n0 + n, PROJ1[n])
            for n, kind in enumerate(OUT1):
                chunk(FIRST["out1"] + n, kind)
            sp.wait_ge(s_bar, 3 * BAR["dif"])
            dif = ATT["dif"]
            with sp.Fori(0, HEADS) as h:
                sp.wait_ge(dif["s_fmt"], h * 5 + 1)
                hb = arena[:, 0:T * 384].rearrange("p (t n) -> p t n", t=T)
                for m in range(3):
                    load(hb[:, :, m * 128:(m + 1) * 128], difv[:, :, bass.ds(h * 128 + m * 1024, 128)],
                         dif["s_load"])
            sp.wait_ge(s_bar, 3 * BAR["out1"])
            load(xr, x_sv, s_x)
            mlp(1)
            sp.wait_ge(s_bar, 3 * BAR["end"])
            load(x_out, xr, s_out)
            sp.wait_ge(s_out, 16)
            sp.wait_ge(s_xs, 16)

        @block.gpsimd
        def _(pool):
            own = Count(pool, s_pool)
            q = nc.gpsimd
            for name in ATT:
                pool.sem_inc(ATT[name]["s_fmt"], 1)
            pool.sem_inc(nsag["s_fmt"], 1)
            own.mark(q.memset(ones[:, :], 1.0))
            own.mark(q.memset(gates[:, 0, 0:184], 0.0))
            q.memset(posi[:, :], 0).then_inc(s_posz, 1)
            own.sync()
            own.link(q.affine_select(out=ident[:, :], in_=gates[:, 0, 0:P], compare_op=ALU.not_equal, fill=1.0,
                                     base=0, pattern=[[-1, P]], channel_multiplier=1))
            own.mark(q.affine_select(out=masks[:, 2 * P:3 * P], in_=gates[:, 0, 0:P], compare_op=ALU.is_ge, fill=NEG,
                                     base=0, pattern=[[-1, P]], channel_multiplier=1))
            own.mark(q.memset(masks[:, P:2 * P].bitcast(F32), 0.0))
            own.mark(q.affine_select(out=masks[:, 0:P], in_=gates[:, 0, 0:P], compare_op=ALU.is_gt, fill=NEG,
                                     base=0, pattern=[[1, P]], channel_multiplier=-1))
            own.mark(q.affine_select(out=cmask[:, :], in_=gates[:, 0, 0:184], compare_op=ALU.is_ge,
                                     fill=NEG, base=16 * 56 - 31, pattern=[[-16, 184]], channel_multiplier=1))
            own.mark(q.affine_select(out=valid[:, :], in_=ones[:, 0:1], compare_op=ALU.is_ge, fill=0.0,
                                     base=-31, pattern=[[0, 1]], channel_multiplier=1))
            own.mark(q.tensor_copy(identr[:, :], ident[:, :]))
            own.sync()
            q.drain().then_inc(s_made, 1)

            def split(n, slot, length, staged, gate):
                w = stage[:, slot, 0:length]
                pool.wait_ge(s_stage[slot], staged)
                if gate is not None:
                    nk, g, c0, m = gate
                    v = w.rearrange("p (k n) -> p k n", k=nk)
                    own.link(q.tensor_tensor(v, v, gates[:, g:g + 1, c0:c0 + m].broadcast_to([P, nk, m]), ALU.mult))
                hi, lo = wts[:, slot, 0, 0:length], wts[:, slot, 1, 0:length]
                if not (isinstance(n, int) and n < 2):
                    pool.wait_ge(s_wused, n - 1)
                own.link(q.tensor_tensor(hi, w, ones[:, 0:1].broadcast_to([P, length]), ALU.mult))
                q.tensor_tensor(lo, w, hi.bitcast(F32), ALU.subtract).then_inc(s_wready, 1)

            def hi_of(dst, src, done):
                shape = list(dst.shape)
                one = ones[0:shape[0], 0:1]
                for _ in shape[2:]:
                    one = one.unsqueeze(1)
                q.tensor_tensor(dst, src, one.broadcast_to(shape), ALU.mult).then_inc(done, 1)

            def lo_of(dst, src, hi, done):
                q.tensor_tensor(dst, src, hi.bitcast(F32), ALU.subtract).then_inc(done, 1)

            def format_heads_mla():
                S = ATT["mla"]
                hb = arena[:, 0:2048].rearrange("p (t n) -> p t n", t=T)
                fm = arena[:, 2048:6144].rearrange("p (a t n) -> p a t n", a=4, t=T)
                with pool.Fori(0, HEADS // 2) as pair:
                    for par in range(2):
                        h = pair * 2 + par
                        v = actT[:, par * 8192 + 4096:par * 8192 + 4096 + T * VW["mla"]].rearrange("p (t n) -> p t n", t=T)
                        pool.wait_ge(S["s_load"], h * 48 + 48)
                        pool.wait_ge(S["s_ftr"], h * 8 + 1)
                        hi_of(fm[:, 0, :, 0:96].bitcast(F32R), hb[:, :, 0:96], S["s_fhi"])
                        hi_of(fm[:, 2, :, 0:96].bitcast(F32R), hb[:, :, 96:192], S["s_fhi"])
                        pool.wait_ge(S["s_pv"], h * S["U"] + 1)
                        hi_of(v[:, :, 0:64], hb[:, :, 192:256], S["s_fhi"])
                        pool.wait_ge(S["s_fhi"], h * 3 + 3)
                        lo_of(fm[:, 1, :, 0:96], hb[:, :, 0:96], fm[:, 0, :, 0:96], S["s_fmt"])
                        lo_of(fm[:, 3, :, 0:96], hb[:, :, 96:192], fm[:, 2, :, 0:96], S["s_fmt"])
                        lo_of(v[:, :, 64:128], hb[:, :, 192:256], v[:, :, 0:64], S["s_fmt"])

            def format_heads_nsa():
                S = ATT["nsa"]
                kb = arena[:, 0:2048].rearrange("p (t b n) -> p t b n", t=T, b=4)
                fm = arena[:, 2560:6656].rearrange("p (a t r n) -> p a t r n", a=4, t=T, r=2)
                fc = arena[:, 7680:7936].rearrange("p (s r n) -> p s r n", s=2, r=2)
                hb = arena[:, 2048:2560].rearrange("p (t n) -> p t n", t=T)
                fq = arena[:, 6656:7680].rearrange("p (t r n) -> p t r n", t=T, r=2)
                vs = [actT[:, NSA_V[b]:NSA_V[b] + T * VW["nsa"]].rearrange("p (t n) -> p t n", t=T) for b in range(2)]
                cv = actT[0:CMP, NSA_CV:NSA_CV + P].rearrange("p (s n) -> p s n", s=2)
                with pool.Fori(0, GROUPS) as g:
                    kc = kcv[0:CMP, bass.ds(g, 1), :]
                    vc = kcv[0:CMP, bass.ds(g + 2, 1), :]
                    pool.wait_ge(nsag["s_load"], g * 64 + 64)
                    pool.wait_ge(nsag["s_ftr"], g * 9 + 1)
                    srcs = [kb[:, :, 2 * b:2 * b + 1, :].broadcast_to([P, T, 2, DH]) for b in range(2)]
                    for b in range(2):
                        hi_of(fm[:, 2 * b, :, :, :].bitcast(F32R), srcs[b], nsag["s_fhi"])
                    hi_of(fc[0:CMP, 0, :, :].bitcast(F32R), kc.broadcast_to([CMP, 2, DH]), nsag["s_fhi"])
                    pool.wait_ge(nsag["s_fhi"], g * 6 + 3)
                    for b in range(2):
                        lo_of(fm[:, 2 * b + 1, :, :, :], srcs[b], fm[:, 2 * b, :, :, :], nsag["s_fmt"])
                    lo_of(fc[0:CMP, 1, :, :], kc.broadcast_to([CMP, 2, DH]), fc[0:CMP, 0, :, :], nsag["s_fmt"])
                    pool.wait_ge(S["s_pv"], g * S["UT"] + S["pv0"])
                    for b in range(2):
                        hi_of(vs[b][:, :, 0:64], kb[:, :, 2 * b + 1, :], nsag["s_fhi"])
                    hi_of(cv[:, 0:1, :], vc, nsag["s_fhi"])
                    pool.wait_ge(nsag["s_fhi"], g * 6 + 6)
                    for b in range(2):
                        lo_of(vs[b][:, :, 64:128], kb[:, :, 2 * b + 1, :], vs[b][:, :, 0:64], nsag["s_fmt"])
                    lo_of(cv[:, 1:2, :], vc, cv[:, 0:1, :], nsag["s_fmt"])
                    with pool.Fori(0, PER_GROUP) as hh:
                        h = g * PER_GROUP + hh
                        pool.wait_ge(S["s_load"], h * 16 + 16)
                        pool.wait_ge(S["s_ftr"], h * 2 + 1)
                        hi_of(fq[:, :, 0, :].bitcast(F32R), hb, S["s_fhi"])
                        pool.wait_ge(S["s_fhi"], h + 1)
                        lo_of(fq[:, :, 1, :], hb, fq[:, :, 0, :], S["s_fmt"])

            def format_heads_dif():
                S = ATT["dif"]
                hb = arena[:, 0:3072].rearrange("p (t w m n) -> p t w m n", t=T, w=3, m=2)
                hv = arena[:, 0:3072].rearrange("p (t n) -> p t n", t=T)[:, :, 256:384]
                fm = arena[:, 3072:9216].rearrange("p (m a t r n) -> p m a t r n", m=2, a=3, t=T, r=2)
                with pool.Fori(0, HEADS // 2) as pair:
                    for par in range(2):
                        h = pair * 2 + par
                        v = actT[:, par * 8192 + 6144:par * 8192 + 8192].rearrange("p (t s n) -> p t s n", t=T, s=2)
                        k_src = [hb[:, :, 1, m, :].unsqueeze(2).broadcast_to([P, T, 2, DH]) for m in range(2)]
                        pool.wait_ge(S["s_load"], h * 48 + 48)
                        pool.wait_ge(S["s_ftr"], h * 12 + 1)
                        for m in range(2):
                            hi_of(fm[:, m, 0, :, 0, :].bitcast(F32R), hb[:, :, 0, m, :], S["s_fhi"])
                            hi_of(fm[:, m, 1, :, :, :].bitcast(F32R), k_src[m], S["s_fhi"])
                        pool.wait_ge(S["s_pv"], h * S["U"] + 1)
                        hi_of(v[:, :, 0, :], hv, S["s_fhi"])
                        pool.wait_ge(S["s_fhi"], h * 5 + 5)
                        for m in range(2):
                            lo_of(fm[:, m, 0, :, 1, :], hb[:, :, 0, m, :], fm[:, m, 0, :, 0, :], S["s_fmt"])
                            lo_of(fm[:, m, 2, :, :, :], k_src[m], fm[:, m, 1, :, :, :], S["s_fmt"])
                        lo_of(v[:, :, 1, :], hv, v[:, :, 0, :], S["s_fmt"])

            staged = [0, 0]

            def straight(first, kinds):
                for m, (_, _, _, nk, cols, gate) in enumerate(kinds):
                    n = first + m
                    staged[n % 2] += 16 * len(cols)
                    width = sum(w for _, w in cols)
                    split(n, n % 2, nk * width, staged[n % 2], None if gate is None else (nk, *gate))

            def mlp(layer):
                first = FIRST[f"mlp{layer}"]
                with pool.Fori(0, FF_GROUPS) as g:
                    own.enter(g, 3)
                    split(g * 2 + first, 0, WCH, g * 16 + (staged[0] + 16), None)
                    split(g * 2 + (first + 1), 1, WCH, g * 16 + (staged[1] + 16), (2, 1, 0, D))
                own.leave(3, FF_GROUPS)
                staged[0] += 16 * FF_GROUPS
                staged[1] += 16 * FF_GROUPS

            straight(FIRST["proj0"], PROJ0)
            pool.wait_ge(s_adaev, 6)
            straight(FIRST["out0"], OUT0[:2])
            pool.wait_ge(s_bar, 3 * BAR["mla"])
            format_heads_mla()
            pool.wait_ge(s_bar, 3 * BAR["nsa"])
            format_heads_nsa()
            straight(FIRST["out0"] + 2, OUT0[2:])
            mlp(0)
            straight(FIRST["proj1"], PROJ1)
            pool.wait_ge(s_adaev, 12)
            straight(FIRST["out1"], OUT1[:2])
            pool.wait_ge(s_bar, 3 * BAR["dif"])
            format_heads_dif()
            straight(FIRST["out1"] + 2, OUT1[2:])
            mlp(1)


        @block.tensor
        def _(pe):
            q = nc.tensor

            def product(dst, passes, last):
                ins = None
                for n, (a, b) in enumerate(passes):
                    ins = q.matmul(dst, a, b, start=(n == 0), stop=(n == len(passes) - 1 and last))
                return ins

            def ada(layer):
                for g in range(6):
                    n = layer * 6 + g
                    pe.wait_ge(s_adaacc, n + 1)
                    if n >= 1:
                        pe.wait_ge(s_adaev, n)
                    acc = arena[:, 8192:9216]
                    bias = arena[0:1, 9216 + (g % 2) * 1024:10240 + (g % 2) * 1024]
                    if g in (2, 5):
                        for h in range(2):
                            q.matmul(ps[:, h, :], ones[:, :], acc[:, h * 512:(h + 1) * 512], start=True, stop=False)
                            ins = q.matmul(ps[:, h, :], ones[0:1, :], bias[:, h * 512:(h + 1) * 512],
                                           start=False, stop=True)
                    else:
                        for k in range(KD):
                            q.matmul(ps[:, 0, k:k + 1], acc[:, k * P:(k + 1) * P], ones[:, 0:1], start=True, stop=False)
                            ins = q.matmul(ps[:, 0, k:k + 1], bias[:, k * P:(k + 1) * P], ones[0:1, 0:1],
                                           start=False, stop=True)
                    ins.then_inc(s_adamm, 1)

            def transposes(name, src, order):
                for idx, (k, half) in enumerate(order):
                    if idx >= 8:
                        pe.wait_ge(s_trl, TR[name] + idx - 7)
                    for m in range(4):
                        ins = q.transpose(ps[:, idx % 8, m * P:(m + 1) * P], src(4 * half + m, k), ident[:, :])
                    ins.then_inc(s_tr, 1)

            def norm_banks(name, n):
                for idx, (k, half) in enumerate(ORDER):
                    pe.wait_ge(s_xn, 8 * n + 4 * half + 4)
                    if idx >= 8:
                        pe.wait_ge(s_trl, TR[name] + idx - 7)
                    for m in range(4):
                        t = 4 * half + m
                        ins = q.transpose(ps[:, idx % 8, m * P:(m + 1) * P],
                                          arena[:, t * D + k * P:t * D + (k + 1) * P], ident[:, :])
                    ins.then_inc(s_tr, 1)

            def splits(a, b, n):
                return [(a[0], b[0]), (a[0], b[1]), (a[1], b[0])]

            def project(chunk, width, raw_free):
                for kh in range(2):
                    pe.wait_ge(s_wready, chunk + (kh + 1))
                    w = [wts[:, kh, s, 0:4 * width].rearrange("p (k n) -> p k n", k=4) for s in range(2)]
                    for t in range(T):
                        if kh == 0 and raw_free is not None:
                            pe.wait_ge(s_raw, raw_free + (t + 1))
                        passes = []
                        for k in range(4):
                            a = [aT[:, s, kh * 4 + k, t * P:(t + 1) * P] for s in range(2)]
                            passes += splits(a, [w[s][:, k, :] for s in range(2)], t)
                        for n, (a, b) in enumerate(passes):
                            ins = q.matmul(ps[:, t, 0:width], a, b, start=(kh == 0 and n == 0),
                                           stop=(kh == 1 and n == len(passes) - 1))
                        if t == T - 1:
                            ins.then_inc(s_wused, 1)
                        elif kh == 1:
                            ins.then_inc(s_mm, 1)

            def up():
                for which, (k0, halfw) in enumerate(((0, 384), (2, 512))):
                    n = FIRST["proj0"] + 8 + which
                    pe.wait_ge(s_wready, n + 1)
                    w = [wts[:, which, s, 0:4 * halfw].rearrange("p (k n) -> p k n", k=2) for s in range(2)]
                    for t in range(T):
                        u = which * T + t
                        if u >= 4:
                            pe.wait_ge(s_raw, RAW["up"] + u - 3)
                        for h in range(2):
                            passes = []
                            for k in range(2):
                                a = [aT[:, s, k0 + k, t * P:(t + 1) * P] for s in range(2)]
                                passes += splits(a, [w[s][:, k, h * halfw:(h + 1) * halfw] for s in range(2)], t)
                            ins = product(ps[:, (u % 4) * 2 + h, 0:halfw], passes, True)
                        ins.then_inc(s_wused if t == T - 1 else s_mm, 1)

            def compress():
                pe.wait_ge(s_cmp, 16 * 12)
                cb = xres[0:CMP, 0:4096].rearrange("p (a n) -> p a n", a=4)
                for a in range(4):
                    for i in range(8):
                        ins = q.transpose(ps[:, a, i * CMP:(i + 1) * CMP],
                                          cb[:, a, i * P:(i + 1) * P], ident[0:CMP, 0:CMP])
                    ins.then_inc(s_cpe, 1)
                w1 = arena[:, 0:4096].rearrange("p (j i n) -> p j i n", j=2, i=16)
                blk = arena[:, 4096:8192].rearrange("p (i a m) -> p i a m", i=16, a=4)
                pe.wait_ge(s_cdve, 2)
                for j in range(2):
                    ins = product(ps[:, 4 + j, 0:P], [(w1[:, j, i, :], blk[:, i, 2 * j:2 * j + 2, :])
                                                      for i in range(16)], True)
                    ins.then_inc(s_cpe, 1)
                hid = arena[:, 8192:8448].rearrange("p (j g m) -> p j g m", j=2, g=2)
                w2 = arena[:, 10240:10368].rearrange("p (j n) -> p j n", j=2)
                pe.wait_ge(s_cact, 2)
                for j in range(2):
                    for g in range(2):
                        ins = q.matmul(ps[0:CMP, 6, (2 * j + g) * DH:(2 * j + g + 1) * DH], hid[:, j, g, :],
                                       w2[:, j, :], start=True, stop=True)
                ins.then_inc(s_cpe, 1)

            def attend(name, turn, stack_src, width, scores, values, more_scores):
                S = ATT[name]
                U, UT, HT, units, before = S["U"], S["UT"], S["HT"], S["units"], S["before"]
                NA = stacks_taken(S, TURN - 1, S["prep"] - 1, 0)
                ND = stacks_taken(S, TURN - 1, S["prep"] - 1, 1)
                NF = S["prep"] * TURN

                def bank(use):
                    k = S["uses"].index(use)
                    if k >= 2:
                        kind, a, b = S["uses"][k - 2]
                        if kind == "half":
                            pe.wait_ge(S["s_pl"], turn * HT + (before[a] + b + 2))
                        elif dve_takes(a, b):
                            pe.wait_ge(S["s_fevd"], turn * ND + (stacks_taken(S, a, b, 1) + 1))
                        else:
                            pe.wait_ge(S["s_feva"], turn * NA + (stacks_taken(S, a, b, 0) + 1))
                    return 4 + k % 2

                def stack(i, b):
                    at = bank(("stack", i, b))
                    if b == 0:
                        pe.wait_ge(S["s_fmt"], turn * (TURN * S["nfmt"]) + ((i + 1) * S["nfmt"] + 1))
                    for m in range(4):
                        ins = q.transpose(ps[0:width, at, m * P:(m + 1) * P],
                                          stack_src[b // 2][:, 4 * (b % 2) + m, 0:width], ident[:, :])
                    ins.then_inc(S["s_ftr"], 1)

                def qk(n):
                    u = units[n]
                    if n % U == 0:
                        i = u["head"]
                        pe.wait_ge(S["s_feva"], turn * NA + (stacks_taken(S, i, S["prep"] - 1, 0) + 1))
                        if i == 0:
                            pe.wait_ge(S["s_fevd"], turn * ND + (stacks_taken(S, i, S["prep"] - 1, 1) + 1))
                            more_scores()
                    pe.wait_ge(S["s_ex"], turn * UT + (max(n - 1, 0) + 1))
                    base = (n % 2) * 1024
                    for b in range(0, u["n"], 4):
                        w = min(4, u["n"] - b) * P
                        dst = psf[:, base + b * P:base + b * P + w]
                        for m, (a, c2) in enumerate(scores(u, (u["k0"] + b) * P, w)):
                            ins = q.matmul(dst, a, c2, start=(m == 0), stop=False, skip_group_check=True)
                        if u["kind"] == "cmp":
                            wanted = [(0, 0, 1, cmask[:, 56 - 8 * u["t"]:184 - 8 * u["t"]])]
                        else:
                            at = u["t"] - u["k0"]
                            two = 1 if at > b else 0
                            wanted = [(at, at - two, 1 + two, masks[:, (2 - two) * P:3 * P])]
                            if u["kind"] == "win" and u["t"] >= WINDOW_TILES:
                                wanted.append((0, 0, 2, masks[:, 0:2 * P]))
                        for at, first, tiles, mask in wanted:
                            if b <= at < b + 4:
                                ins = q.matmul(psf[:, base + first * P:base + (first + tiles) * P], identr[:, :],
                                               mask, start=False, stop=False, skip_group_check=True)
                    ins.then_inc(S["s_qk"], 1)

                def tr(n):
                    u = units[n]
                    pe.wait_ge(S["s_ex"], turn * UT + (n + 2))
                    for half in range(u["halves"]):
                        at = bank(("half", n, half))
                        for m in range(4 * half, min(4 * half + 4, u["n"])):
                            ins = q.transpose(ps[:, at, (m % 4) * P:(m % 4 + 1) * P],
                                              pexp[:, n % 2, m * P:(m + 1) * P], ident[:, :])
                        ins.then_inc(S["s_t"], 1)

                def pv(n):
                    u = units[n]
                    pe.wait_ge(S["s_pl"], turn * HT + (before[n + 1] + 1))
                    pe.wait_ge(S["s_o"], turn * UT + (max(n - 1, 0) + 1))
                    passes = []
                    for m in range(u["n"]):
                        passes += [(pT[:, n % 2, s, m * P:(m + 1) * P], values(u, u["k0"] + m)) for s in range(2)]
                    product(ps[:, 6 + n % 2, 0:VW[name]], passes, True).then_inc(S["s_pv"], 1)

                pe.wait_ge(S["s_o"], turn * UT + 1)
                pe.wait_ge(S["s_pl"], turn * HT + 1)
                pe.wait_ge(S["s_ex"], turn * UT + 1)
                for b in range(S["prep"]):
                    stack(0, b)
                qk(0)
                qk(1)
                for n in range(UT):
                    if n + 2 < UT:
                        qk(n + 2)
                    tr(n)
                    for i, b in S["at"][n]:
                        stack(i, b)
                    if n >= 1:
                        pv(n - 1)
                pv(UT - 1)

            def mla():
                pe.wait_ge(s_ones, 2)
                fm = arena[:, 2048:6144].rearrange("p (a t n) -> p a t n", a=4, t=T)
                with pe.Fori(0, TURNS) as turn:
                    def scores(u, c0, w):
                        o = (u["head"] % 2) * 8192
                        st = [actT[0:MLA_DH, o + n * 1024:o + (n + 1) * 1024] for n in range(4)]
                        qt = [st[s][:, u["t"] * P:(u["t"] + 1) * P] for s in range(2)]
                        return splits(qt, [st[2 + s][:, c0:c0 + w] for s in range(2)], 0)

                    def values(u, kb):
                        o = (u["head"] % 2) * 8192 + 4096 + kb * VW["mla"]
                        return actT[:, o:o + VW["mla"]]

                    attend("mla", turn, [fm[:, n, :, :] for n in range(4)], MLA_DH, scores, values, lambda: None)

            def nsa():
                st = {"slc": [actT[:, 0:1024], actT[:, 1024:2048]], "win": [actT[:, 2048:3072], actT[:, 3072:4096]],
                      "cmp": [actT[:, NSA_CK + s * P:NSA_CK + (s + 1) * P] for s in range(2)]}
                v = {"slc": NSA_V[0], "win": NSA_V[1], "cmp": NSA_CV}
                fm = arena[:, 2560:6656].rearrange("p (a t n) -> p a t n", a=4, t=T)
                fq = arena[:, 6656:7680].rearrange("p (t n) -> p t n", t=T)
                fc = arena[:, 7680:7936].rearrange("p (s n) -> p s n", s=2)
                S = ATT["nsa"]
                pe.wait_ge(s_ones, 4)
                with pe.Fori(0, GROUPS) as g:
                    pe.wait_ge(S["s_o"], g * S["UT"] + 1)
                    pe.wait_ge(S["s_pl"], g * S["HT"] + 1)
                    pe.wait_ge(S["s_ex"], g * S["UT"] + 1)
                    pe.wait_ge(nsag["s_fmt"], g * 6 + 4)
                    for n in range(4):
                        for half in range(2):
                            for m in range(4):
                                ins = q.transpose(ps[:, 2 * n + half, m * P:(m + 1) * P],
                                                  fm[:, n, 4 * half + m, :], ident[:, :])
                            ins.then_inc(nsag["s_ftr"], 1)
                    pe.wait_ge(nsag["s_feva"], g * 5 + 1)
                    for s in range(2):
                        ins = q.transpose(ps[:, 0, s * P:(s + 1) * P], fc[:, s, :], ident[:, :])
                    ins.then_inc(nsag["s_ftr"], 1)
                    pe.wait_ge(nsag["s_feva"], g * 5 + 5)
                    pe.wait_ge(nsag["s_fevd"], g * 4 + 4)

                    def values_ready():
                        pe.wait_ge(nsag["s_fmt"], g * 6 + 7)

                    def scores(u, c0, w):
                        o = 8192 + (u["head"] % 2) * 1024 + u["t"] * P
                        return [(actT[:, o:o + P], st[u["kind"]][s][:, c0:c0 + w]) for s in range(2)]

                    def values(u, kb):
                        o = v[u["kind"]] + kb * VW["nsa"]
                        return actT[:, o:o + VW["nsa"]]

                    attend("nsa", g, [fq], P, scores, values, values_ready)

            def dif():
                fm = arena[:, 3072:9216].rearrange("p (a t n) -> p a t n", a=6, t=T)
                with pe.Fori(0, TURNS) as turn:
                    def scores(u, c0, w):
                        o = (u["head"] % 2) * 8192 + 3072 * u["factor"]
                        qt = actT[:, o + u["t"] * P:o + (u["t"] + 1) * P]
                        return [(qt, actT[:, o + (1 + s) * 1024 + c0:o + (1 + s) * 1024 + c0 + w]) for s in range(2)]

                    def values(u, kb):
                        o = (u["head"] % 2) * 8192 + 6144 + kb * VW["dif"]
                        return actT[:, o:o + VW["dif"]]

                    attend("dif", turn, [fm[:, n, :, :] for n in range(6)], P, scores, values, lambda: None)

            def mlp(layer):
                first = FIRST[f"mlp{layer}"]
                w1 = [wts[:, 0, s, :].rearrange("p (k n) -> p k n", k=KD) for s in range(2)]
                w2 = [wts[:, 1, s, :].rearrange("p (k n) -> p k n", k=2) for s in range(2)]
                with pe.Fori(0, FF_GROUPS) as g:
                    pe.wait_ge(s_wready, g * 2 + (first + 1))
                    for idx, (half, f) in enumerate(((0, 0), (0, 1), (1, 0), (1, 1))):
                        pe.wait_ge(s_gl, g * 4 + (layer * 64 + max(idx - 3, 0) + 1))
                        passes = []
                        for k in range(KD):
                            passes += splits([w1[s][:, k, f * P:(f + 1) * P] for s in range(2)],
                                             [aT[:, s, k, half * 512:(half + 1) * 512] for s in range(2)], 0)
                        product(ps[:, idx, :], passes, True).then_inc(s_wused if idx == 3 else s_g1, 1)
                    pe.wait_ge(s_wready, g * 2 + (first + 2))
                    for idx in range(16):
                        t, n = idx // 2, idx % 2
                        if idx == 0:
                            pe.wait_ge(s_gl, g * 4 + (layer * 64 + 3))
                        if idx == 8:
                            pe.wait_ge(s_gl, g * 4 + (layer * 64 + 5))
                        pe.wait_ge(s_ya, g * 16 + (layer * 256 + max(idx - 3, 0) + 1))
                        passes = []
                        for f in range(2):
                            passes += splits([gT[:, s, f, t * P:(t + 1) * P] for s in range(2)],
                                             [w2[s][:, f, n * 512:(n + 1) * 512] for s in range(2)], 0)
                        product(ps[:, 4 + idx % 4, :], passes, True).then_inc(s_wused if idx == 15 else s_y, 1)

            for name in ATT:
                for key in ("s_t", "s_ftr"):
                    pe.sem_inc(ATT[name][key], 1)
                pe.sem_inc(ATT[name]["s_pv"], ATT[name]["pv0"])
            pe.sem_inc(nsag["s_ftr"], 1)
            pe.sem_inc(s_y, 1)
            pe.wait_ge(s_made, 1)
            ada(0)
            barrier(pe, q, "norm0")
            norm_banks("norm0", 0)
            barrier(pe, q, "proj0")
            for j, cols in enumerate(HYC):
                project(2 * j, sum(w for _, w in cols), None if j == 0 else 8 * (j - 1))
            barrier(pe, q, "latent")
            latents = xres[:, 4096:8192].rearrange("p (t n) -> p t n", t=T)
            pe.wait_ge(s_proc, 3)
            transposes("latent", lambda t, k: latents[:, t, k * P:(k + 1) * P],
                       [(k, h) for h in range(2) for k in range(4)])
            barrier(pe, q, "up")
            up()
            barrier(pe, q, "cmp")
            compress()
            barrier(pe, q, "mla")
            mla()
            barrier(pe, q, "nsa")
            nsa()
            barrier(pe, q, "otr0")
            transposes("otr0", lambda t, k: xr[:, t, k * P:(k + 1) * P], ORDER)
            barrier(pe, q, "out0")
            for j in range(2):
                project(FIRST["out0"] + 2 * j, 512, None if j == 0 else RAW["out0"])
            barrier(pe, q, "norm1")
            norm_banks("norm1", 1)
            barrier(pe, q, "mlp0")
            mlp(0)
            barrier(pe, q, "ada1")
            ada(1)
            barrier(pe, q, "norm2")
            norm_banks("norm2", 2)
            barrier(pe, q, "proj1")
            project(FIRST["proj1"], 512, None)
            with pe.Fori(0, 5) as j:
                project(j * 2 + (FIRST["proj1"] + 2), 512, j * 8 + RAW["proj1"])
            barrier(pe, q, "dif")
            dif()
            barrier(pe, q, "sub")
            barrier(pe, q, "otr1")
            transposes("otr1", lambda t, k: xr[:, t, k * P:(k + 1) * P], ORDER)
            barrier(pe, q, "out1")
            for j in range(2):
                project(FIRST["out1"] + 2 * j, 512, None if j == 0 else RAW["out1"])
            barrier(pe, q, "norm3")
            norm_banks("norm3", 3)
            barrier(pe, q, "mlp1")
            mlp(1)
            barrier(pe, q, "end")

        @block.scalar
        def _(act):
            q = nc.scalar
            own = Count(act, s_act)
            std = [0]
            spills = [0, 0]

            def sqrt(n):
                std[0] += 1
                act.wait_ge(s_var, std[0])
                q.activation(small[:, 2, 0:n], small[:, 1, 0:n], ACT.Sqrt).then_inc(s_std, 1)

            def sumsq(n):
                for t in range(T):
                    if t >= 1:
                        act.wait_ge(s_ss, 8 * n + t)
                    q.activation(arena[:, 8192:9216], xr[:, t, :], ACT.Square,
                                 accum_out=small[:, 0, t:t + 1]).then_inc(s_ss, 1)

            def take_hi(name, order, scale, shift):
                for idx, (k, half) in enumerate(order):
                    act.wait_ge(s_tr, TR[name] + idx + 1)
                    dst = aT[:, 0, k, half * 512:(half + 1) * 512]
                    src = ps[:, idx % 8, :]
                    if scale is not None:
                        act.wait_ge(s_trl, TR[name] + max(idx - 1, 0))
                        tmp = arena[:, 8192 + (idx % 2) * 512:8704 + (idx % 2) * 512]
                        if shift is not None:
                            own.link(q.activation(tmp, src, ACT.Identity, bias=shift(k), scale=scale(k)))
                        else:
                            own.link(q.activation(tmp, src, ACT.Copy, scale=scale(k)))
                        src = tmp
                    q.activation(dst, src, ACT.Copy).then_inc(s_trh, 1)

            def norm(name, n):
                sumsq(n)
                sqrt(T)
                w = n % 2
                take_hi(name, ORDER, lambda k: modv[:, 2 * w, k:k + 1], lambda k: modv[:, 2 * w + 1, k:k + 1])

            def spill(slot, ready, pairs):
                if ready is not None:
                    act.wait_ge(s_proc, ready)
                for dst, src in pairs:
                    act.dma_start(dst, src).then_inc(s_spill[slot], 16)
                    spills[slot] += 16

            def stored(*slots):
                for slot in slots:
                    act.wait_ge(s_spill[slot], spills[slot])

            def take(mm, wused, name, t, dst, src):
                if t == T - 1:
                    act.wait_ge(s_wused, wused)
                else:
                    act.wait_ge(s_mm, mm + t + 1)
                q.activation(dst, src, ACT.Copy).then_inc(s_raw, 1)

            for name in ATT:
                for key in ("s_ex", "s_feva"):
                    act.sem_inc(ATT[name][key], 1)
            act.sem_inc(s_gh, 1)
            act.wait_ge(s_const, 16 * NCONST)
            q.activation(cond[:, 1, :], cond[:, 0, :], ACT.Exp, scale=-1.0).then_inc(s_cond, 1)
            act.wait_ge(s_ang, 1)
            q.activation(rope[:, 1, :, :], ang, ACT.Sin).then_inc(s_sin, 1)
            q.activation(half_ang, ang, ACT.Sin, scale=0.5).then_inc(s_sin, 1)
            act.wait_ge(s_lam, 1)
            q.activation(lams[:, 2:4], lams[:, 0:2], ACT.Exp).then_inc(s_cond, 1)
            barrier(act, q, "norm0")
            act.wait_ge(s_x, 16)
            norm("norm0", 0)
            barrier(act, q, "proj0")
            for j in range(4):
                width = sum(w for _, w in HYC[j])
                stored(j % 2)
                for t in range(T):
                    take(7 * j, 2 * j + 2, "proj0", t, raw[:, j % 2, t, 0:width], ps[:, t, 0:width])
                if j != 2:
                    sqrt({0: 64, 1: 16, 3: 16}[j])
                else:
                    sqrt(16)
                    act.wait_ge(s_raw, 24)
                    q.activation(gate3[:, :, :], raw[:, 0, :, 256:280], ACT.Exp, scale=-1.0).then_inc(s_cond, 1)
                    q.activation(kpe[:, :, :], raw[:, 0, :, 280:312], ACT.Copy).then_inc(s_cond, 1)
                if j == 0:
                    spill(0, 1, [(nsav[:, :, 0:512], raw[:, 0, :, :])])
                if j == 1:
                    spill(1, 2, [(nsav[:, :, 512:1024], raw[:, 1, :, :])])
                if j == 2:
                    spill(0, 3, [(nsav[:, :, 1024:1280], raw[:, 0, :, 0:256])])
            stored(0, 1)
            barrier(act, q, "latent")
            take_hi("latent", [(k, h) for h in range(2) for k in range(4)], lambda k: latv[:, k:k + 1], None)
            barrier(act, q, "up")
            for t in range(T):
                take(MM["up"], 9, "up", t, upq[t // 4][:, t % 4, :].rearrange("p (h n) -> p h n", h=2),
                     ps[:, (t % 4) * 2:(t % 4) * 2 + 2, 0:384])
            for t in range(T):
                take(MM["up"] + 7, 10, "up", t, upk[t // 4][:, t % 4, :, 32:160],
                     psf[:, (t % 4) * 1024:(t % 4) * 1024 + 1024].rearrange("p (h n) -> p h n", h=HEADS))
            for n in range(4):
                sqrt(32)
            for hf in range(2):
                rowsd = mlav[:, 4 * hf:4 * hf + 4, :]
                spill(hf, 5 + hf, [(rowsd[:, :, 0:768], upq[hf])])
            for hf in range(2):
                rowsd = mlav[:, 4 * hf:4 * hf + 4, :]
                spill(hf, 7 + hf, [(rowsd[:, t, 768:1536].rearrange("p (h n) -> p h n", h=HEADS),
                                 upk[hf][:, t, :, 0:96]) for t in range(4)] +
                      [(rowsd[:, t, 1536:2048].rearrange("p (h n) -> p h n", h=HEADS),
                        upk[hf][:, t, :, 96:160]) for t in range(4)])
            stored(0, 1)
            barrier(act, q, "cmp")
            for j in range(2):
                act.wait_ge(s_cpe, 5 + j)
                q.activation(arena[:, 8192 + j * P:8320 + j * P], ps[:, 4 + j, 0:P],
                             ACT.Gelu_apprx_tanh).then_inc(s_cact, 1)
            sqrt(2)
            barrier(act, q, "mla")

            def attend(name, turn, stack_dst, width):
                S = ATT[name]
                U, UT, HT, units, before = S["U"], S["UT"], S["HT"], S["units"], S["before"]
                NF = S["prep"] * TURN

                def exps(n):
                    u = units[n]
                    act.wait_ge(S["s_mx"], turn * UT + (n + 1))
                    act.wait_ge(S["s_t"], turn * HT + (before[max(n - 1, 0)] + 1))
                    base = (n % 2) * 1024
                    sums = dict(accum_out=rows[:, 1, n % 8:n % 8 + 1]) if name == "dif" else {}
                    q.activation(pexp[:, n % 2, 0:u["n"] * P], psf[:, base:base + u["n"] * P], ACT.Exp,
                                 bias=rows[:, 0, n % 8:n % 8 + 1], **sums).then_inc(S["s_ex"], 1)

                def take_p(n):
                    u = units[n]
                    for half in range(u["halves"]):
                        at = 4 + S["uses"].index(("half", n, half)) % 2
                        w = min(4, u["n"] - 4 * half) * P
                        act.wait_ge(S["s_t"], turn * HT + (before[n] + half + 2))
                        act.wait_ge(S["s_pv"], turn * UT + (max(n - 1, 0) + S["pv0"]))
                        q.activation(pT[:, n % 2, 0, 512 * half:512 * half + w], ps[:, at, 0:w],
                                     ACT.Copy).then_inc(S["s_ph"], 1)

                def take_stack(i, b):
                    at = 4 + S["uses"].index(("stack", i, b)) % 2
                    act.wait_ge(S["s_ftr"], turn * NF + (stacks_done(S, i, b) + 1))
                    q.activation(stack_dst(i, b), ps[0:width, at, :], ACT.Copy).then_inc(S["s_feva"], 1)

                for b in range(0, S["prep"], 2):
                    take_stack(0, b)
                exps(0)
                exps(1)
                for n in range(UT):
                    take_p(n)
                    for i, b in S["at"][n]:
                        take_stack(i, b)
                    if n + 2 < UT:
                        exps(n + 2)

            with act.Fori(0, TURNS) as turn:
                attend("mla", turn, stack_slots["mla"], MLA_DH)
            barrier(act, q, "nsa")
            with act.Fori(0, GROUPS) as g:
                for n in range(4):
                    act.wait_ge(nsag["s_ftr"], g * 9 + (2 * n + 2))
                    q.activation(actT[:, n * 1024:n * 1024 + 512], ps[:, 2 * n, :], ACT.Copy).then_inc(nsag["s_feva"], 1)
                act.wait_ge(nsag["s_ftr"], g * 9 + 10)
                q.activation(actT[:, NSA_CK:NSA_CV], ps[:, 0, 0:256], ACT.Copy).then_inc(nsag["s_feva"], 1)
                attend("nsa", g, stack_slots["nsa"], P)
            barrier(act, q, "otr0")
            take_hi("otr0", ORDER, None, None)
            barrier(act, q, "out0")
            barrier(act, q, "norm1")
            norm("norm1", 1)

            def mlp(layer):
                first = FIRST[f"mlp{layer}"]
                with act.Fori(0, FF_GROUPS) as g:
                    for idx, (half, f) in enumerate(((0, 0), (0, 1), (1, 0), (1, 1))):
                        if idx == 3:
                            act.wait_ge(s_wused, g * 2 + (first + 1))
                        else:
                            act.wait_ge(s_g1, g * 3 + (layer * 48 + idx + 1))
                        act.wait_ge(s_gt, g * 4 + (layer * 64 + max(idx - 1, 0) + 1))
                        q.activation(relu[:, idx % 2, :], ps[:, idx, :], ACT.Relu).then_inc(s_gr, 1)
                        act.wait_ge(s_gt, g * 4 + (layer * 64 + idx + 2))
                        act.wait_ge(s_y, g * 15 + (layer * 240 + 1))
                        q.activation(gT[:, 0, f, half * 512:(half + 1) * 512], sq[:, idx % 2, :],
                                     ACT.Copy).then_inc(s_gh, 1)

            barrier(act, q, "mlp0")
            mlp(0)
            barrier(act, q, "ada1")
            barrier(act, q, "norm2")
            norm("norm2", 2)
            barrier(act, q, "proj1")
            for j in range(6):
                stored(j % 2)
                for t in range(T):
                    take(MM["proj1"] + 7 * j, FIRST["proj1"] + 2 * j + 2, "proj1", t, raw[:, j % 2, t, :], ps[:, t, :])
                if j < 4:
                    sqrt(64)
                    spill(j % 2, 10 + j, [(difv[:, :, j * 512:(j + 1) * 512], raw[:, j % 2, :, :])])
                else:
                    act.wait_ge(s_raw, RAW["proj1"] + 8 * (j + 1))
                    spill(j % 2, None, [(difv[:, :, j * 512:(j + 1) * 512], raw[:, j % 2, :, :])])
            stored(0, 1)
            barrier(act, q, "dif")
            with act.Fori(0, TURNS) as turn:
                attend("dif", turn, stack_slots["dif"], P)
            barrier(act, q, "sub")
            sqrt(64)
            barrier(act, q, "otr1")
            take_hi("otr1", ORDER, None, None)
            barrier(act, q, "out1")
            barrier(act, q, "norm3")
            norm("norm3", 3)
            barrier(act, q, "mlp1")
            mlp(1)
            barrier(act, q, "end")

        @block.vector
        def _(dve):
            q = nc.vector
            own = Count(dve, s_dve)
            std = [0]
            procs = [0]

            for name in ATT:
                for key in ("s_pl", "s_o", "s_fevd"):
                    dve.sem_inc(ATT[name][key], 1)
            for primed in (s_gt, s_gl, s_ya):
                dve.sem_inc(primed, 1)
            dve.wait_ge(s_const, 16 * NCONST)
            dve.wait_ge(s_made, 1)
            for n in range(16):
                own.mark(q.memset(invf[:, n:n + 1], float(np.float32(THETA ** (-n / 16)))))
            for n in range(8):
                own.mark(q.memset(invf[:, 16 + n:17 + n], float(np.float32(THETA ** (-n / 8)))))
            own.mark(q.tensor_copy(post[:, :], posi[:, :]))
            own.mark(q.tensor_scalar(gainq[:, 0, :], gainq[:, 0, :], MLA_DH ** -0.5, None, ALU.mult))
            own.mark(q.tensor_scalar(gainh[:, 0, :], gainh[:, 0, :], DH ** -0.5, None, ALU.mult))
            own.mark(q.tensor_scalar(gainh[:, 4, :], gainh[:, 4, :], DH ** -0.5, None, ALU.mult))
            own.mark(q.tensor_scalar(gsub[:, :], gsub[:, :], 1.0 - LAM_INIT, None, ALU.mult))
            own.mark(q.tensor_tensor(lamt[:, 0, :], lamt[:, 0, :], lamt[:, 1, :], ALU.mult))
            own.mark(q.tensor_tensor(lamt[:, 2, :], lamt[:, 2, :], lamt[:, 3, :], ALU.mult))
            dve.wait_ge(s_cond, 1)
            own.mark(q.tensor_scalar(cond[:, 1, :], cond[:, 1, :], 1.0, None, ALU.add))
            own.sync()
            own.mark(q.reciprocal(cond[:, 1, :], cond[:, 1, :]))
            own.mark(q.tensor_reduce(lams[:, 0:1], lamt[:, 0, :], AX.X, ALU.add))
            own.mark(q.tensor_reduce(lams[:, 1:2], lamt[:, 2, :], AX.X, ALU.add))
            own.link(q.tensor_tensor(ang, post[:, :].unsqueeze(2).broadcast_to([P, T + 1, 24]),
                                     invf[:, :].unsqueeze(1).broadcast_to([P, T + 1, 24]), ALU.mult))
            q.tensor_copy(lams[:, 4:5], lams[:, 0:1]).then_inc(s_lam, 1)
            own.mark(q.tensor_tensor(cond[:, 0, :], cond[:, 0, :], cond[:, 1, :], ALU.mult))
            own.link(q.tensor_scalar(turns, ang, 1.0 / (2 * math.pi), 12582912.0, ALU.mult, ALU.add))
            own.link(q.tensor_scalar(turns, turns, -12582912.0, None, ALU.add))
            C1 = 6.28125
            C2 = float(np.float32(np.round((2 * math.pi - C1) * 2 ** 21) / 2 ** 21))
            C3 = 2 * math.pi - C1 - C2
            for cc in (C1, C2, C3):
                own.link(q.scalar_tensor_tensor(ang, turns, -cc, ang, ALU.mult, ALU.add))
            q.tensor_scalar(ang, ang, 3.1415925, -3.1415925, ALU.min, ALU.max).then_inc(s_ang, 1)
            dve.wait_ge(s_sin, 2)
            own.link(q.scalar_tensor_tensor(rope[:, 0, :, :], half_ang, -2.0, half_ang, ALU.mult, ALU.mult))
            own.mark(q.tensor_scalar(rope[:, 0, :, :], rope[:, 0, :, :], 1.0, None, ALU.add))
            dve.wait_ge(s_cond, 2)
            own.link(q.tensor_tensor(lams[:, 5:6], lams[:, 3:4], lams[:, 2:3], ALU.subtract))
            own.link(q.tensor_scalar(lams[:, 6:7], lams[:, 5:6], -LAM_INIT, None, ALU.add))

            def ada(layer):
                acc = arena[:, 8192:9216]
                landed = [layer * 6 * 16, layer * 6 * 16]
                landed[0] += layer * 6 * 16
                for g in range(6):
                    n = layer * 6 + g
                    if n >= 1:
                        dve.wait_ge(s_adamm, n)
                    for half in range(2):
                        landed[half] += 32 if half == 0 else 16
                        dve.wait_ge(s_adal[half], landed[half])
                        piece = arena[:, half * 4096:half * 4096 + 4096].rearrange("p (k n) -> p k n", k=4)
                        for k in range(4):
                            s = cond[:, 0, 4 * half + k:4 * half + k + 1]
                            last = half == 1 and k == 3
                            if half == 0 and k == 0:
                                ins = q.tensor_scalar(acc, piece[:, k, :], s, None, ALU.mult)
                            else:
                                ins = q.scalar_tensor_tensor(acc, piece[:, k, :], s, acc, ALU.mult, ALU.add)
                            if last:
                                ins.then_inc(s_adaacc, 1)
                            elif k == 3:
                                ins.then_inc(s_adau, 1)
                                dve.wait_ge(s_adau, n + 1)
                            else:
                                own.link(ins)
                    dve.wait_ge(s_adamm, n + 1)
                    if g in (2, 5):
                        q.tensor_copy(gates[:, g // 3, :], psf[:, 0:1024]).then_inc(s_adaev, 1)
                    elif g in (1, 4):
                        w = g // 3
                        q.scalar_tensor_tensor(modv[:, 2 * w, :], ps[:, 0, 0:KD], 1.0, normv[:, 2 * layer + w, :],
                                               ALU.add, ALU.mult).then_inc(s_adaev, 1)
                    else:
                        q.tensor_copy(modv[:, 2 * (g // 3) + 1, :], ps[:, 0, 0:KD]).then_inc(s_adaev, 1)

            def rstd(n, width, src):
                q.tensor_scalar(small[:, 1, 0:n], src, 1.0 / width, EPS, ALU.mult, ALU.add).then_inc(s_var, 1)
                std[0] += 1
                dve.wait_ge(s_std, std[0])
                own.link(q.reciprocal(small[:, 0, 0:n], small[:, 2, 0:n]))

            def norm(name, n):
                dve.wait_ge(s_ss, 8 * n + 8)
                rstd(T, D, small[:, 0, 0:T])
                for t in range(T):
                    q.tensor_scalar(arena[:, t * D:(t + 1) * D], xr[:, t, :], small[:, 0, t:t + 1], None,
                                    ALU.mult).then_inc(s_xn, 1)
                for idx, (k, half) in enumerate(ORDER):
                    take_lo(name, idx, k, half, arena[:, 8192 + (idx % 2) * 512:8704 + (idx % 2) * 512])

            def take_lo(name, idx, k, half, src):
                dve.wait_ge(s_trh, TR[name] + idx + 1)
                cols = slice(half * 512, (half + 1) * 512)
                q.tensor_tensor(aT[:, 1, k, cols], src, aT[:, 0, k, cols].bitcast(F32),
                                ALU.subtract).then_inc(s_trl, 1)

            def norm_rope(v, heads, width, gain, half, cols, tiles, scratch, done):
                pn, tn = v.shape[0], v.shape[1]
                n = tn * heads
                sqs = scratch[0:pn, 0:n * width].rearrange("p (t h n) -> p t h n", t=tn, h=heads)
                if procs[0]:
                    dve.wait_ge(done, procs[0])
                procs[0] += 1
                own.link(q.tensor_tensor(sqs, v, v, ALU.mult))
                own.link(q.tensor_reduce(small[0:pn, 0, 0:n], sqs, AX.X, ALU.add))
                q.tensor_scalar(small[0:pn, 1, 0:n], small[0:pn, 0, 0:n], 1.0 / width, EPS, ALU.mult,
                                ALU.add).then_inc(s_var, 1)
                std[0] += 1
                dve.wait_ge(s_std, std[0])
                own.link(q.reciprocal(small[0:pn, 0, 0:n], small[0:pn, 2, 0:n]))
                r = small[0:pn, 0, 0:n].rearrange("p (t h) -> p t h", t=tn)
                ins = q.tensor_tensor(v, v, r.unsqueeze(3).broadcast_to([pn, tn, heads, width]), ALU.mult)
                if gain is None:
                    ins.then_inc(done, 1)
                    return
                own.link(ins)
                own_gain = gain[0:pn].unsqueeze(1).unsqueeze(1).broadcast_to([pn, tn, heads, width])
                ins = q.tensor_tensor(v, v, own_gain, ALU.mult)
                if not half:
                    ins.then_inc(done, 1)
                    return
                own.link(ins)
                cos, sin = [rope[0:pn, m, tiles, cols].unsqueeze(2).broadcast_to([pn, tn, heads, half])
                            for m in range(2)]
                x1, x2 = v[:, :, :, 0:half], v[:, :, :, half:2 * half]
                tmp = [scratch[0:pn, m * n * half:(m + 1) * n * half].rearrange("p (t h n) -> p t h n", t=tn, h=heads)
                       for m in range(4)]
                for m, (a, b) in enumerate(((x1, cos), (x2, sin), (x1, sin), (x2, cos))):
                    own.mark(q.tensor_tensor(tmp[m], a, b, ALU.mult))
                own.sync()
                own.link(q.tensor_tensor(x1, tmp[0], tmp[1], ALU.subtract))
                q.tensor_tensor(x2, tmp[2], tmp[3], ALU.add).then_inc(done, 1)

            ada(0)
            barrier(dve, q, "norm0")
            dve.wait_ge(s_x, 16)
            norm("norm0", 0)
            barrier(dve, q, "proj0")
            alltiles = slice(0, T)
            dve.wait_ge(s_raw, 8)
            norm_rope(raw[:, 0, :, :].rearrange("p t (h n) -> p t h n", h=HEADS), HEADS, DH, gainh[:, 0, :], 8,
                      slice(16, 24), alltiles, arena, s_proc)
            dve.wait_ge(s_raw, 16)
            norm_rope(raw[:, 1, :, 256:384].rearrange("p t (h n) -> p t h n", h=2), 2, DH, gainh[:, 2, :], 8,
                      slice(16, 24), alltiles, arena, s_proc)
            dve.wait_ge(s_raw, 24)
            norm_rope(raw[:, 0, :, 0:128].rearrange("p t (h n) -> p t h n", h=2), 2, DH, gainh[:, 3, :], 8,
                      slice(16, 24), alltiles, arena, s_proc)
            dve.wait_ge(s_cond, 3)
            own.link(q.tensor_scalar(gate3[:, :, :], gate3[:, :, :], 1.0, None, ALU.add))
            own.mark(q.reciprocal(gate3[:, :, :], gate3[:, :, :]))
            dve.wait_ge(s_raw, 32)
            norm_rope(raw[:, 1, :, :].rearrange("p t (h n) -> p t h n", h=2), 2, RANK, None, 0,
                      None, alltiles, arena, s_proc)
            barrier(dve, q, "latent")
            for idx, (k, half) in enumerate([(k, h) for h in range(2) for k in range(4)]):
                take_lo("latent", idx, k, half, arena[:, 8192 + (idx % 2) * 512:8704 + (idx % 2) * 512])
            barrier(dve, q, "up")
            for hf in range(2):
                dve.wait_ge(s_raw, RAW["up"] + 4 * hf + 4)
                norm_rope(upq[hf].rearrange("p t (h n) -> p t h n", h=HEADS), HEADS, MLA_DH, gainq[:, 0, :], 16,
                          slice(0, 16), slice(4 * hf, 4 * hf + 4), arena[:, 8192:11264], s_proc)
            for hf in range(2):
                own.link(q.tensor_copy(upk[hf][:, :, :, 0:32],
                                       kpe[:, 4 * hf:4 * hf + 4, :].unsqueeze(2).broadcast_to([P, 4, HEADS, 32])))
                dve.wait_ge(s_raw, RAW["up"] + 8 + 4 * hf + 4)
                norm_rope(upk[hf][:, :, :, 0:96], HEADS, MLA_DH, gainq[:, 1, :], 16,
                          slice(0, 16), slice(4 * hf, 4 * hf + 4), arena[:, 8192:11264], s_proc)
            barrier(dve, q, "cmp")
            tt = xres[:, 4096:6144].rearrange("p (a i m) -> p a i m", a=4, i=8)
            blk = arena[:, 4096:8192].rearrange("p (i a m) -> p i a m", i=16, a=4)
            own.mark(q.memset(arena[:, 4096:8192], 0.0))
            for a in range(4):
                dve.wait_ge(s_cpe, a + 1)
                own.mark(q.tensor_copy(tt[:, a, :, :], ps[:, a, :].rearrange("p (i m) -> p i m", i=8)))
            own.sync()
            dve.wait_ge(s_cmp, 16 * 12)
            for j in range(2):
                for i in range(16):
                    o = i // 8
                    ins = q.tensor_scalar(blk[:, i, 2 * j:2 * j + 2, 0:CMP - 1], tt[:, 2 * j:2 * j + 2, i % 8, o:o + CMP - 1],
                                          arena[:, 10368 + j * 16 + i:10369 + j * 16 + i], None, ALU.add)
                    if i == 15:
                        ins.then_inc(s_cdve, 1)
            dve.wait_ge(s_cpe, 7)
            own.link(q.tensor_copy(kcv[0:CMP, :, :], ps[0:CMP, 6, 0:256].rearrange("p (a n) -> p a n", a=4)))
            norm_rope(kcv[0:CMP, 0:2, :].unsqueeze(1), 2, DH, gainh[:, 1, :], 8, slice(16, 24), slice(T, T + 1),
                      arena[:, 8448:10240], s_proc)
            own.mark(q.memset(arena[:, 7680:7936], 0.0))
            own.mark(q.memset(actT[:, NSA_CV:NSA_CV + P].bitcast(F32), 0.0))
            own.mark(q.memset(actT[:, NSA_CV + P:NSA_CV + VW["nsa"]].bitcast(F32), 1.0))
            barrier(dve, q, "mla")

            def attend(name, turn, own_steps, cols, dv, factor, stack_dst, width):
                S = ATT[name]
                U, UT, HT, units, before = S["U"], S["UT"], S["HT"], S["units"], S["before"]
                NF = S["prep"] * TURN

                def maxima(n):
                    u = units[n]
                    dve.wait_ge(S["s_qk"], turn * UT + (n + 1))
                    base = (n % 2) * 1024
                    q.tensor_reduce(rows[:, 0, n % 8:n % 8 + 1], psf[:, base:base + u["n"] * P], AX.X, ALU.max,
                                    negate=True).then_inc(S["s_mx"], 1)

                def take_p(n):
                    u = units[n]
                    for half in range(u["halves"]):
                        at = 4 + S["uses"].index(("half", n, half)) % 2
                        w = min(4, u["n"] - 4 * half) * P
                        dve.wait_ge(S["s_ph"], turn * HT + (before[n] + half + 1))
                        at2 = slice(512 * half, 512 * half + w)
                        q.tensor_tensor(pT[:, n % 2, 1, at2], ps[:, at, 0:w], pT[:, n % 2, 0, at2].bitcast(F32),
                                        ALU.subtract).then_inc(S["s_pl"], 1)

                def take_o(n):
                    u = units[n]
                    f = rows[:, 2, n % 8:n % 8 + 1]
                    o = ps[:, 6 + n % 2, :]
                    dve.wait_ge(S["s_pv"], turn * UT + (n + 1 + S["pv0"]))
                    own_steps.link(q.reciprocal(f, rows[:, 1, n % 8:n % 8 + 1] if name == "dif" else o[:, 2 * dv:2 * dv + 1]))
                    for by in factor(u):
                        own_steps.link(q.tensor_tensor(f, f, by, ALU.mult))
                    dst = xr[:, u["t"], cols(u["head"])]
                    if u["add"]:
                        dve.wait_ge(S["s_o"], turn * UT + (n + 1))
                        own_steps.link(q.scalar_tensor_tensor(dst, o[:, 0:dv], f, dst, ALU.mult, ALU.add))
                    else:
                        own_steps.link(q.tensor_scalar(dst, o[:, 0:dv], f, None, ALU.mult))
                    q.scalar_tensor_tensor(dst, o[:, dv:2 * dv], f, dst, ALU.mult, ALU.add).then_inc(S["s_o"], 1)

                for b in range(1, S["prep"], 2):
                    at = 4 + S["uses"].index(("stack", 0, b)) % 2
                    dve.wait_ge(S["s_ftr"], turn * NF + (b + 2))
                    q.tensor_copy(stack_dst(0, b), ps[0:width, at, :]).then_inc(S["s_fevd"], 1)
                maxima(0)
                maxima(1)
                for n in range(UT):
                    if n + 2 < UT:
                        maxima(n + 2)
                    take_p(n)
                    if n >= 1:
                        take_o(n - 1)
                take_o(UT - 1)

            for par in range(2):
                v = actT[:, par * 8192 + 4096:par * 8192 + 4096 + T * VW["mla"]].rearrange("p (t n) -> p t n", t=T)
                q.memset(v[:, :, 2 * MLA_V:].bitcast(F32), 1.0).then_inc(s_ones, 1)
            steps = Count(dve, ATT["mla"]["s_own"])
            with dve.Fori(0, TURNS) as turn:
                steps.enter(turn, TURN * 16)
                attend("mla", turn, steps, lambda i: bass.ds((turn * TURN + i) * DH, DH), MLA_V, lambda u: [],
                       stack_slots["mla"], MLA_DH)
            steps.leave(TURN * 16, TURNS)
            barrier(dve, q, "nsa")
            for b in range(2):
                v = actT[:, NSA_V[b]:NSA_V[b] + T * VW["nsa"]].rearrange("p (t n) -> p t n", t=T)
                q.memset(v[:, :, 2 * DH:].bitcast(F32), 1.0).then_inc(s_ones, 1)
            steps = Count(dve, ATT["nsa"]["s_own"])
            with dve.Fori(0, GROUPS) as g:
                for n in range(4):
                    dve.wait_ge(nsag["s_ftr"], g * 9 + (2 * n + 3))
                    q.tensor_copy(actT[:, n * 1024 + 512:(n + 1) * 1024], ps[:, 2 * n + 1, :]).then_inc(nsag["s_fevd"], 1)
                steps.enter(g, PER_GROUP * 73)

                def factor(u):
                    by = [gate3[:, u["t"], bass.ds(g * PER_GROUP + (u["head"] + 8 * u["factor"]), 1)]]
                    return by + ([valid[:, :]] if u["kind"] == "cmp" and u["t"] == 0 else [])

                attend("nsa", g, steps, lambda i: bass.ds((g * PER_GROUP + i) * DH + 512, DH), DH, factor,
                       stack_slots["nsa"], P)
            steps.leave(PER_GROUP * 73, GROUPS)
            barrier(dve, q, "otr0")

            def otr(name):
                for idx, (k, half) in enumerate(ORDER):
                    take_lo(name, idx, k, half, ps[:, idx % 8, :])

            def residual(name, loads):
                dve.wait_ge(s_x, loads)
                for j in range(2):
                    for t in range(T):
                        if t == T - 1:
                            dve.wait_ge(s_wused, FIRST[name] + 2 * j + 2)
                        else:
                            dve.wait_ge(s_mm, MM[name] + 7 * j + t + 1)
                        dst = xr[:, t, j * 512:(j + 1) * 512]
                        q.tensor_tensor(dst, dst, ps[:, t, :], ALU.add).then_inc(s_raw, 1)

            def mlp(layer):
                first = FIRST[f"mlp{layer}"]
                with dve.Fori(0, FF_GROUPS) as g:
                    for idx, (half, f) in enumerate(((0, 0), (0, 1), (1, 0), (1, 1))):
                        dve.wait_ge(s_gr, g * 4 + (layer * 64 + idx + 1))
                        dve.wait_ge(s_gh, g * 4 + (layer * 64 + max(idx - 1, 0) + 1))
                        dve.wait_ge(s_gl, g * 4 + (layer * 64 + max(idx - 1, 0) + 1))
                        q.scalar_tensor_tensor(sq[:, idx % 2, :], ps[:, idx, :], 0.0, relu[:, idx % 2, :],
                                               ALU.max, ALU.mult).then_inc(s_gt, 1)
                        dve.wait_ge(s_gh, g * 4 + (layer * 64 + idx + 2))
                        cols = slice(half * 512, (half + 1) * 512)
                        q.tensor_tensor(gT[:, 1, f, cols], sq[:, idx % 2, :], gT[:, 0, f, cols].bitcast(F32),
                                        ALU.subtract).then_inc(s_gl, 1)
                    for idx in range(16):
                        if idx == 15:
                            dve.wait_ge(s_wused, g * 2 + (first + 2))
                        else:
                            dve.wait_ge(s_y, g * 15 + (layer * 240 + idx + 2))
                        t, n = idx // 2, idx % 2
                        dve.wait_ge(s_ya, g * 16 + (layer * 256 + 1))
                        dst = xr[:, t, n * 512:(n + 1) * 512]
                        q.tensor_tensor(dst, dst, ps[:, 4 + idx % 4, :], ALU.add).then_inc(s_ya, 1)

            otr("otr0")
            barrier(dve, q, "out0")
            residual("out0", 32)
            barrier(dve, q, "norm1")
            norm("norm1", 1)
            barrier(dve, q, "mlp0")
            mlp(0)
            barrier(dve, q, "ada1")
            ada(1)
            barrier(dve, q, "norm2")
            dve.wait_ge(s_xs, 16)
            norm("norm2", 2)
            barrier(dve, q, "proj1")
            for j in range(4):
                dve.wait_ge(s_raw, RAW["proj1"] + 8 * (j + 1))
                norm_rope(raw[:, j % 2, :, :].rearrange("p t (h n) -> p t h n", h=HEADS), HEADS, DH,
                          gainh[:, 4 + j // 2, :], 8, slice(16, 24), alltiles, arena, s_proc)
            barrier(dve, q, "dif")
            steps = Count(dve, ATT["dif"]["s_own"])
            with dve.Fori(0, TURNS) as turn:
                steps.enter(turn, TURN * 40)
                attend("dif", turn, steps, lambda i: bass.ds((turn * TURN + i) * 2 * DH, 2 * DH), 2 * DH,
                       lambda u: [lams[:, 6:7]] if u["factor"] else [], stack_slots["dif"], P)
            steps.leave(TURN * 40, TURNS)
            barrier(dve, q, "sub")
            norm_rope(xr[:, :, :].rearrange("p t (h n) -> p t h n", h=HEADS), HEADS, 2 * DH, gsub[:, :], 0,
                      None, alltiles, arena, s_proc)
            barrier(dve, q, "otr1")
            otr("otr1")
            barrier(dve, q, "out1")
            residual("out1", 48)
            barrier(dve, q, "norm3")
            norm("norm3", 3)
            barrier(dve, q, "mlp1")
            mlp(1)
            barrier(dve, q, "end")


_INS = ['x', 'c', 'positions', 'ada_w', 'ada_b', 'norm_mix', 'norm_mlp', 'mlp_w1', 'mlp_w2', 'hy_w_in', 'hy_w_out',
        'mla_q_norm', 'mla_w_uq', 'mla_kv_norm', 'mla_w_ukv', 'mla_q_gain', 'mla_k_gain', 'nsa_q_gain',
        'nsa_k_gain', 'nsa_cmp_pos', 'nsa_cmp_w1', 'nsa_cmp_w2', 'diff_w_qkv', 'diff_w_out', 'diff_q_gain',
        'diff_k_gain', 'diff_lambda', 'diff_sub_gain']


def kernel(**inputs):
    import numpy as _np
    import concourse.bacc as _bacc
    from concourse import mybir as _mybir
    from concourse.bass_utils import run_bass_kernel_spmd as _run

    nc = _bacc.Bacc("TRN2", target_bir_lowering=False, num_devices=1, dynamic_dma_scratch_size=512)
    arrays, args = {}, []
    for name in _INS:
        a = _np.ascontiguousarray(inputs[name])
        arrays[f"in_{name}"] = a
        args.append(nc.dram_tensor(f"in_{name}", a.shape, _mybir.dt.from_np(a.dtype), kind="ExternalInput").ap())
    o = nc.dram_tensor("out_0", inputs["x"].shape, _mybir.dt.float32, kind="ExternalOutput").ap()
    trunk(nc, *args, o)
    r = _run(nc, [arrays], core_ids=[0])
    return r.results[0]["out_0"]
```

```python
import math
from contextlib import ExitStack

import numpy as np

import concourse.bass as bass
from concourse import mybir

F32 = mybir.dt.float32
F32R = mybir.dt.float32r
I32 = mybir.dt.int32
ACT = mybir.ActivationFunctionType
ALU = mybir.AluOpType
AX = mybir.AxisListType

P = 128
SEQ = 1024
T = SEQ // P
D = 1024
KD = D // P
DFF = 4096
NEG = -1e30
EPS = 1e-6
THETA = 500000.0

HEADS = 8
DH = 64
MLA_DH, MLA_ROPE, MLA_NOPE, MLA_V, RANK = 96, 32, 64, 64, 256
GROUPS, PER_GROUP = 2, 4
WINDOW_TILES = 512 // P
CMP = 64
LATENT_W = 2 * RANK
NQ0 = LATENT_W + MLA_ROPE
NKV0 = NQ0 + HEADS * DH
GATE0 = NKV0 + 768
HY_IN = GATE0 + 24

WCH = 2048
FFG = 256
FF_GROUPS = DFF // FFG
TURN = 4
TURNS = HEADS // TURN

LAM_INIT = 0.8 - 0.6 * math.exp(-0.3)


class Count:

    def __init__(self, eng, sem):
        self.eng, self.sem, self.base, self.k, self.off = eng, sem, 0, 0, 0

    def enter(self, turn, per):
        self.base, self.k, self.off = self.base + self.k, 0, turn * per

    def leave(self, per, times):
        assert self.k == per, (self.k, per)
        self.base, self.k, self.off = self.base + per * times, 0, 0

    def mark(self, ins):
        self.k += 1
        ins.then_inc(self.sem, 1)

    def sync(self):
        self.eng.wait_ge(self.sem, self.off + (self.base + self.k))

    def link(self, ins):
        self.mark(ins)
        self.sync()


def trunk(nc, x, c, positions, ada_w, ada_b, norm_mix, norm_mlp, mlp_w1, mlp_w2, hy_w_in, hy_w_out,
          mla_q_norm, mla_w_uq, mla_kv_norm, mla_w_ukv, mla_q_gain, mla_k_gain, nsa_q_gain,
          nsa_k_gain, nsa_cmp_pos, nsa_cmp_w1, nsa_cmp_w2, diff_w_qkv, diff_w_out, diff_q_gain,
          diff_k_gain, diff_lambda, diff_sub_gain, out):
    ctx = ExitStack()
    with ctx:
        ctx.enter_context(nc.allow_non_contiguous_dma(reason="small vectors are loaded transposed"))

        def sb(name, shape, dt=F32):
            return ctx.enter_context(nc.sbuf_tensor(name, shape, dt))

        def sem(name):
            return ctx.enter_context(nc.semaphore(name))

        actT = sb("actT", [P, 2 * KD * SEQ], F32R)
        wts = sb("wts", [P, 2, 2, WCH], F32R)
        gT = sb("gT", [P, 2, FFG // P, SEQ], F32R)
        xres = sb("xres", [P, T * D])
        stage = sb("stage", [P, 2, WCH])
        arena = sb("arena", [P, 11264])
        gates = sb("gates", [P, 2, D])
        ident = sb("ident", [P, P])
        identr = sb("identr", [P, P], F32R)
        masks = sb("masks", [P, 3 * P], F32R)
        cmask = sb("cmask", [P, 184], F32R)
        ones = sb("ones", [P, P])
        rope = sb("rope", [P, 2, T + 1, 24])
        post = sb("post", [P, T + 1])
        posi = sb("posi", [P, T + 1], I32)
        cond = sb("cond", [P, 2, KD])
        normv = sb("normv", [P, 4, KD])
        latv = sb("latv", [P, 4])
        modv = sb("modv", [P, 4, KD])
        gainq = sb("gainq", [P, 2, 96])
        gainh = sb("gainh", [P, 6, DH])
        gsub = sb("gsub", [P, 1])
        lams = sb("lams", [P, 8])
        small = sb("small", [P, 3, T * 8])
        rows = sb("rows", [P, 3, 8])
        gate3 = sb("gate3", [P, T, 24])
        kpe = sb("kpe", [P, T, MLA_ROPE])
        lamt = kpe[:, :, :].rearrange("p t n -> p (t n)").rearrange("p (a n) -> p a n", a=4)
        kcv = arena[:, 8960:9216].rearrange("p (a n) -> p a n", a=4)
        xtra = gates[:, 1, :]
        valid = sb("valid", [P, 1])
        ps = ctx.enter_context(nc.psum_tensor("ps", [P, 8, 512], F32))
        psf = ps[:, :, :].rearrange("p b n -> p (b n)")

        xsave = nc.dram_tensor("xsave", (SEQ, D), F32).ap()
        nsad = nc.dram_tensor("nsad", (SEQ, 1280), F32).ap()
        mlad = nc.dram_tensor("mlad", (SEQ, 2048), F32).ap()
        difd = nc.dram_tensor("difd", (SEQ, 3072), F32).ap()

        aT = actT[:, :].rearrange("p (s k t) -> p s k t", s=2, k=KD)
        xr = xres[:, :].rearrange("p (t d) -> p t d", t=T)
        raw = xres[:, :].rearrange("p (s t n) -> p s t n", s=2, t=T)
        x_in = x.rearrange("b (t p) d -> p (b t) d", p=P)
        x_sv = xsave.rearrange("(t p) d -> p t d", p=P)
        x_out = out.rearrange("b (t p) d -> p (b t) d", p=P)
        nsav = nsad.rearrange("(t p) n -> p t n", p=P)
        mlav = mlad.rearrange("(t p) n -> p t n", p=P)
        difv = difd.rearrange("(t p) n -> p t n", p=P)

        s_const = sem("s_const")
        s_posz = sem("s_posz")
        s_made = sem("s_made")
        s_stage = [sem("s_stage0"), sem("s_stage1")]
        s_wready = sem("s_wready")
        s_wused = sem("s_wused")
        s_tick = sem("s_tick")
        s_pool = sem("s_pool")
        s_dve = sem("s_dve")
        s_act = sem("s_act")
        s_bar = sem("s_bar")
        s_adal = [sem("s_adal0"), sem("s_adal1")]
        s_adau = sem("s_adau")
        s_adaacc = sem("s_adaacc")
        s_adamm = sem("s_adamm")
        s_adaev = sem("s_adaev")
        s_adap = sem("s_adap")
        s_adad = sem("s_adad")
        s_x = sem("s_x")
        s_ss = sem("s_ss")
        s_var = sem("s_var")
        s_std = sem("s_std")
        s_xn = sem("s_xn")
        s_tr = sem("s_tr")
        s_trh = sem("s_trh")
        s_trl = sem("s_trl")
        s_mm = sem("s_mm")
        s_raw = sem("s_raw")
        s_proc = sem("s_proc")
        s_spill = [sem("s_spill0"), sem("s_spill1")]
        s_cmp = sem("s_cmp")
        s_cmpw = sem("s_cmpw")
        s_cmpx = sem("s_cmpx")
        s_cpe = sem("s_cpe")
        s_cact = sem("s_cact")
        s_cdve = sem("s_cdve")
        s_out = sem("s_out")
        s_xs = sem("s_xs")
        s_sq = sem("s_sq")
        s_kpe = sem("s_kpe")
        s_ones = sem("s_ones")

        s_cond = sem("s_cond")
        s_lam = sem("s_lam")
        s_ang = sem("s_ang")
        s_sin = sem("s_sin")
        s_g1 = sem("s_g1")
        s_gr = sem("s_gr")
        s_gt = sem("s_gt")
        s_gh = sem("s_gh")
        s_gl = sem("s_gl")
        s_y = sem("s_y")
        s_ya = sem("s_ya")

        pexp = arena[:, 9216:11264].rearrange("p (u n) -> p u n", u=2)
        pT = gT
        relu = arena[:, 0:1024].rearrange("p (s n) -> p s n", s=2)
        sq = arena[:, 1024:2048].rearrange("p (s n) -> p s n", s=2)
        upq = [xres[:, 0:3072].rearrange("p (t n) -> p t n", t=4),
               arena[:, 0:3072].rearrange("p (t n) -> p t n", t=4)]
        upk = [xres[:, 3072:8192].rearrange("p (t h n) -> p t h n", t=4, h=HEADS),
               arena[:, 3072:8192].rearrange("p (t h n) -> p t h n", t=4, h=HEADS)]
        ang = xtra[:, 0:216].rearrange("p (t n) -> p t n", t=T + 1)
        turns = xtra[:, 216:432].rearrange("p (t n) -> p t n", t=T + 1)
        half_ang = xtra[:, 432:648].rearrange("p (t n) -> p t n", t=T + 1)
        invf = xtra[:, 648:672]
        NCONST = 22
        ADA_COLS = 6 * D // FF_GROUPS
        ada_piece = arena[:, 2048:2048 + KD * ADA_COLS].rearrange("p (k n) -> p k n", k=KD)
        ada_acc = arena[:, 5120:5120 + 6 * D]
        ada_bias = gates[0:1, 0, 0:ADA_COLS]
        ADA_BANKS = [0, 1, 2, 4, 5, 6]
        ORDER = [(k, half) for half in range(2) for k in range(KD)]

        block = ctx.enter_context(nc.Block())

        STAGES = ["proj0", "latent", "up", "cmp", "mla", "nsa", "otr0", "out0", "mlp0",
                  "ada1", "proj1", "dif", "sub", "out1", "mlp1", "end"]
        BAR = {name: n + 1 for n, name in enumerate(STAGES)}

        def barrier(eng, q, stage, wait=True):
            q.drain().then_inc(s_bar, 1)
            if wait:
                eng.wait_ge(s_bar, 3 * BAR[stage])

        TR = {"norm0": 0, "latent": 16, "otr0": 24, "norm1": 40, "norm2": 56, "otr1": 72, "norm3": 88}
        MM = {"proj0": 0, "up": 28, "out0": 42, "proj1": 56, "out1": 98}
        RAW = {"proj0": 0, "up": 32, "out0": 48, "proj1": 64, "out1": 112}

        def unit(t, kind, k0, nblk, add, factor):
            return dict(t=t, kind=kind, k0=k0, n=nblk, add=add, factor=factor, halves=(nblk + 3) // 4)


        UNITS = {"mla": [unit(t, "full", 0, t + 1, False, None) for t in range(T)],
                 "nsa": [u for t in range(T) for u in (
                     unit(t, "slc", 0, t + 1, False, 1),
                     unit(t, "win", max(0, t - WINDOW_TILES), min(t, WINDOW_TILES) + 1, True, 2),
                     unit(t, "cmp", 0, 1, True, 0))],
                 "dif": [unit(t, f"map{m}", 0, t + 1, m == 1, m) for t in range(T) for m in range(2)]}
        ATT = {}
        for name, prep, steps in (("mla", 8, [3, 3, 3, 4, 4, 4, 5, 5]), ("nsa", 2, [3, 4]),
                                  ("dif", 12, [6, 7, 8, 8, 9, 9, 10, 10, 11, 11, 12, 12])):
            S = {k: sem(f"{name}_{k}") for k in (
                "s_load",
                "s_fhi",
                "s_fmt",
                "s_ftr",
                "s_feva",
                "s_fevd",
                "s_qk",
                "s_mx",
                "s_ex",
                "s_t",
                "s_ph",
                "s_pl",
                "s_pv",
                "s_o",
                "s_own",
                )}
            U = len(UNITS[name])
            S["U"], S["UT"], S["prep"] = U, U * TURN, prep
            S["units"] = [dict(u, head=i) for i in range(TURN) for u in UNITS[name]]
            S["before"] = [sum(u["halves"] for u in S["units"][:n]) for n in range(S["UT"] + 1)]
            S["HT"] = S["before"][-1]
            S["at"] = [[] for _ in S["units"]]
            for i in range(1, TURN):
                for b, step in enumerate(steps):
                    S["at"][(i - 1) * U + step].append((i, b))
            S["uses"] = [("stack", 0, b) for b in range(prep)]
            for n, u in enumerate(S["units"]):
                S["uses"] += [("half", n, half) for half in range(u["halves"])]
                S["uses"] += [("stack", i, b) for i, b in S["at"][n]]
            ATT[name] = S
        VW = {"mla": 2 * MLA_V + 2, "nsa": 2 * DH + 2, "dif": 4 * DH}
        NSA_V = [5120, 5120 + T * VW["nsa"]]
        NSA_CK = NSA_V[1] + T * VW["nsa"]
        NSA_CV = NSA_CK + 2 * P
        nsag = {k: sem(f"nsag_{k}") for k in ("s_load", "s_fhi", "s_fmt", "s_ftr", "s_feva", "s_fevd")}
        for name in ATT:
            ATT[name]["pv0"] = ATT[name]["U"] + 1

        def dve_takes(i, b):
            return i == 0 and b % 2 == 1

        def stacks_taken(S, i, b, eng):
            order = [(0, c) for c in range(S["prep"])] + [x for step in S["at"] for x in step]
            upto = order[:order.index((i, b)) + 1]
            return sum(dve_takes(*x) == bool(eng) for x in upto)

        def stacks_done(S, i, b):
            return ([(0, c) for c in range(S["prep"])] + [x for step in S["at"] for x in step]).index((i, b)) + 1

        stack_slots = {
            "mla": lambda i, b: actT[0:MLA_DH, (i % 2) * 8192 + b * 512:(i % 2) * 8192 + (b + 1) * 512],
            "nsa": lambda i, b: actT[:, 8192 + (i % 2) * 1024 + b * 512:8192 + (i % 2) * 1024 + (b + 1) * 512],
            "dif": lambda i, b: actT[:, (i % 2) * 8192 + b * 512:(i % 2) * 8192 + (b + 1) * 512]}
        ATT["mla"]["nfmt"], ATT["nsa"]["nfmt"], ATT["dif"]["nfmt"] = 3, 1, 5
        ATT["mla"]["laid"], ATT["nsa"]["laid"], ATT["dif"]["laid"] = [1, 1, 2, 2], [1], [1, 2, 2, 3, 4, 4]

        def wview(a, row0, nk, c0, n):
            return a[row0:row0 + nk * P, c0:c0 + n].rearrange("(k p) n -> p k n", p=P)

        HYC = [[(NQ0, 512)], [(NKV0, 512)], [(NKV0 + 512, 280), (LATENT_W, 32)], [(0, 512)]]
        PROJ0 = []
        for cols in HYC:
            for kh in range(2):
                PROJ0.append(("cols", hy_w_in[0], kh * 512, 4, cols, None))
        PROJ0.append(("cols", mla_w_uq[0], 0, 2, [(0, 768)], None))
        PROJ0.append(("cols", mla_w_ukv[0], 0, 2, [(0, 1024)], None))
        OUT0 = [("cols", hy_w_out[0], kh * 512, 4, [(n * 512, 512)], (0, n * 512, 512))
                for n in range(2) for kh in range(2)]
        PROJ1 = [("cols", diff_w_qkv[0], kh * 512, 4, [(n * 512, 512)], None)
                 for n in range(6) for kh in range(2)]
        OUT1 = [("cols", diff_w_out[0], kh * 512, 4, [(n * 512, 512)], (0, n * 512, 512))
                for n in range(2) for kh in range(2)]
        FIRST = {"proj0": 0}
        FIRST["out0"] = len(PROJ0)
        FIRST["mlp0"] = FIRST["out0"] + len(OUT0)
        FIRST["proj1"] = FIRST["mlp0"] + 2 * FF_GROUPS
        FIRST["out1"] = FIRST["proj1"] + len(PROJ1)
        FIRST["mlp1"] = FIRST["out1"] + len(OUT1)
        assert all(v % 2 == 0 for v in FIRST.values())

        def mlp_views(layer, g):
            w1 = mlp_w1[layer].rearrange("(k p) n -> p k n", p=P)[:, :, bass.ds(g * FFG, FFG)]
            w2 = mlp_w2[layer].rearrange("(q p) n -> p q n", p=P)[:, bass.ds(g * 2, 2), :]
            return w1, w2

        @block.sync
        def _(sp):
            def load(dst, src, s):
                sp.dma_start(dst, src).then_inc(s, 16)

            sp.wait_ge(s_posz, 1)
            load(posi[:, 0:T], positions.rearrange("b (t p) -> p (b t)", p=P), s_const)
            load(posi[0:CMP - 1, T:T + 1], positions[0:1, 31:SEQ:16].rearrange("b c -> c b"), s_const)
            load(cond[:, 0, :], c.rearrange("b (p k) -> p (b k)", p=P), s_const)
            for i in range(2):
                load(normv[:, 2 * i, :], norm_mix[i:i + 1, :].rearrange("b (k p) -> p (b k)", p=P), s_const)
                load(normv[:, 2 * i + 1, :], norm_mlp[i:i + 1, :].rearrange("b (k p) -> p (b k)", p=P), s_const)
            load(latv[:, 0:2], mla_q_norm.rearrange("b (k p) -> p (b k)", p=P), s_const)
            load(latv[:, 2:4], mla_kv_norm.rearrange("b (k p) -> p (b k)", p=P), s_const)
            load(gainq[:, 0, :], mla_q_gain.broadcast_to([P, 96]), s_const)
            load(gainq[:, 1, :], mla_k_gain.broadcast_to([P, 96]), s_const)
            load(gainh[:, 0, :], nsa_q_gain.broadcast_to([P, DH]), s_const)
            for b in range(3):
                load(gainh[:, 1 + b, :], nsa_k_gain[0, b:b + 1, :].broadcast_to([P, DH]), s_const)
            load(gainh[:, 4, :], diff_q_gain.broadcast_to([P, DH]), s_const)
            load(gainh[:, 5, :], diff_k_gain.broadcast_to([P, DH]), s_const)
            load(gsub[:, :], diff_sub_gain.rearrange("b p -> p b"), s_const)
            for b in range(4):
                load(lamt[:, b, :], diff_lambda[0, b:b + 1, :].broadcast_to([P, DH]), s_const)

            def chunk(n, kind):
                _, w, row0, nk, cols, _ = kind
                if n >= 2:
                    sp.wait_ge(s_wready, n - 1)
                width = sum(m for _, m in cols)
                dst = stage[:, n % 2, 0:nk * width].rearrange("p (k n) -> p k n", k=nk)
                at = 0
                for c0, m in cols:
                    load(dst[:, :, at:at + m], wview(w, row0, nk, c0, m), s_stage[n % 2])
                    at += m

            def ada(g, half):
                w = ada_w[0].rearrange("(p k) n -> p k n", k=KD)
                slot = half if g < 2 else 1
                if g >= 2 and half == 0:
                    sp.wait_ge(s_adaacc, g)
                elif g >= 2:
                    sp.wait_ge(s_adau, g + 1)
                elif g == 1:
                    sp.wait_ge(s_adaacc if half else s_adau, 1)
                dst = arena[:, slot * 4096:slot * 4096 + 4096].rearrange("p (k n) -> p k n", k=4)
                load(dst, w[:, 4 * half:4 * half + 4, g * 1024:(g + 1) * 1024], s_adal[slot])
                if half == 0:
                    load(arena[0:1, 9216 + (g % 2) * 1024:10240 + (g % 2) * 1024],
                         ada_b[0:1, g * 1024:(g + 1) * 1024], s_adal[slot])

            def mlp(layer):
                with sp.Fori(0, FF_GROUPS) as g:
                    w1, w2 = mlp_views(layer, g)
                    first = FIRST[f"mlp{layer}"]
                    sp.wait_ge(s_wready, g * 2 + first - 1)
                    load(stage[:, 0, :].rearrange("p (k n) -> p k n", k=KD), w1, s_stage[0])
                    sp.wait_ge(s_wready, g * 2 + first)
                    load(stage[:, 1, :].rearrange("p (k n) -> p k n", k=2), w2, s_stage[1])
                    if layer == 0:
                        sp.wait_ge(s_bar, 3 * BAR["mlp0"])
                        sp.wait_ge(s_adad, g + 1)
                        load(ada_piece, ada_w[1].rearrange("(p k) n -> p k n", k=KD)[:, :, bass.ds(g * ADA_COLS, ADA_COLS)],
                             s_adap)
                        load(ada_bias, ada_b[1:2, bass.ds(g * ADA_COLS, ADA_COLS)], s_adap)

            ada(0, 0)
            ada(0, 1)
            load(xr, x_in, s_x)
            ada(1, 0)
            ada(1, 1)
            chunk(0, PROJ0[0])
            chunk(1, PROJ0[1])
            chunk(2, PROJ0[2])
            chunk(3, PROJ0[3])
            sp.wait_ge(s_bar, 3 * BAR["proj0"])
            ada(2, 0)
            ada(2, 1)
            for n in range(4, len(PROJ0)):
                chunk(n, PROJ0[n])
                ada(3 + (n - 4) // 2, (n - 4) % 2)
            sp.wait_ge(s_wready, len(PROJ0))
            for j in range(2):
                load(stage[:, j, :].rearrange("p (i n) -> p i n", i=16),
                     nsa_cmp_w1[0, j].rearrange("(i q) n -> q i n", q=P), s_cmpw)
            sp.wait_ge(s_spill[1], 16)
            sp.wait_ge(s_spill[0], 16 * 4)
            for a in range(4):
                load(xres[0:CMP, a * 1024:(a + 1) * 1024].rearrange("p (l n) -> p l n", l=16),
                     nsad[:, 512 + a * DH:512 + (a + 1) * DH].rearrange("(m l) n -> m l n", l=16), s_cmpx)
            sp.wait_ge(s_bar, 3 * BAR["cmp"])
            for j in range(2):
                load(arena[:, 10240 + j * 64:10304 + j * 64], nsa_cmp_w2[0, j], s_cmp)
                for par in range(2):
                    load(arena[64 * par:64 * par + 64, 10368 + j * 16:10384 + j * 16],
                         nsa_cmp_pos[0, j].rearrange("(i r) d -> r d i", r=2)[par], s_cmp)
            sp.wait_ge(s_bar, 3 * BAR["mla"])
            mla = ATT["mla"]
            with sp.Fori(0, HEADS) as h:
                sp.wait_ge(mla["s_fmt"], h * 3 + 1)
                hb = arena[:, 0:T * 256].rearrange("p (t n) -> p t n", t=T)
                load(hb[:, :, 0:96], mlav[:, :, bass.ds(h * 96, 96)], mla["s_load"])
                load(hb[:, :, 96:256], mlav[:, :, bass.ds(h * 160 + 768, 160)], mla["s_load"])
            chunk(FIRST["out0"], OUT0[0])
            chunk(FIRST["out0"] + 1, OUT0[1])
            nsa = ATT["nsa"]
            with sp.Fori(0, GROUPS) as g:
                sp.wait_ge(nsag["s_fmt"], g * 6 + 1)
                kb = arena[:, 6144:6144 + T * 256].rearrange("p (t n) -> p t n", t=T)
                for m, col in enumerate([768, 768 + 128, 1024, 1024 + 128]):
                    load(kb[:, :, m * 64:(m + 1) * 64], nsav[:, :, bass.ds(g * 64 + col, 64)], nsag["s_load"])
                with sp.Fori(0, PER_GROUP) as hh:
                    sp.wait_ge(nsa["s_fmt"], g * PER_GROUP + hh + 1)
                    sp.sem_inc(s_tick, 1)
                    load(arena[:, 8192:8704].rearrange("p (t n) -> p t n", t=T),
                         nsav[:, :, bass.ds((g * PER_GROUP + hh) * 64, 64)], nsa["s_load"])
            chunk(FIRST["out0"] + 2, OUT0[2])
            chunk(FIRST["out0"] + 3, OUT0[3])
            sp.wait_ge(s_bar, 3 * BAR["out0"])
            load(xr, x_in, s_x)
            mlp(0)
            sp.wait_ge(s_bar, 3 * BAR["ada1"])
            load(x_sv, xr, s_xs)
            n0 = FIRST["proj1"]
            chunk(n0, PROJ1[0])
            chunk(n0 + 1, PROJ1[1])
            for n in range(2, len(PROJ1)):
                chunk(n0 + n, PROJ1[n])

            sp.wait_ge(s_spill[0], 16 * 7)
            dif = ATT["dif"]
            with sp.Fori(0, HEADS) as h:
                sp.wait_ge(dif["s_fmt"], h * 5 + 1)
                hb = arena[:, 6144:6144 + T * 384].rearrange("p (t n) -> p t n", t=T)
                for m in range(3):
                    load(hb[:, :, m * 128:(m + 1) * 128], difv[:, :, bass.ds(h * 128 + m * 1024, 128)],
                         dif["s_load"])
            for n, kind in enumerate(OUT1):
                chunk(FIRST["out1"] + n, kind)
            sp.wait_ge(s_bar, 3 * BAR["out1"])
            load(xr, x_sv, s_x)
            mlp(1)
            for t in range(T):
                sp.wait_ge(s_ya, 1 + 32 * FF_GROUPS - 16 + 2 * (t + 1))
                load(x_out[:, t, :], xr[:, t, :], s_out)
            sp.wait_ge(s_out, 16 * T)
            sp.wait_ge(s_xs, 16)

        @block.gpsimd
        def _(pool):
            own = Count(pool, s_pool)
            q = nc.gpsimd
            for name in ATT:
                pool.sem_inc(ATT[name]["s_fmt"], 1)
            pool.sem_inc(nsag["s_fmt"], 1)
            own.mark(q.memset(ones[:, :], 1.0))
            own.mark(q.memset(gates[:, 0, 0:184], 0.0))
            q.memset(posi[:, :], 0).then_inc(s_posz, 1)
            own.sync()
            own.link(q.affine_select(out=ident[:, :], in_=gates[:, 0, 0:P], compare_op=ALU.not_equal, fill=1.0,
                                     base=0, pattern=[[-1, P]], channel_multiplier=1))
            own.mark(q.affine_select(out=masks[:, 2 * P:3 * P], in_=gates[:, 0, 0:P], compare_op=ALU.is_ge, fill=NEG,
                                     base=0, pattern=[[-1, P]], channel_multiplier=1))
            own.mark(q.memset(masks[:, P:2 * P].bitcast(F32), 0.0))
            own.mark(q.affine_select(out=masks[:, 0:P], in_=gates[:, 0, 0:P], compare_op=ALU.is_gt, fill=NEG,
                                     base=0, pattern=[[1, P]], channel_multiplier=-1))
            own.mark(q.affine_select(out=cmask[:, :], in_=gates[:, 0, 0:184], compare_op=ALU.is_ge,
                                     fill=NEG, base=16 * 56 - 31, pattern=[[-16, 184]], channel_multiplier=1))
            own.mark(q.affine_select(out=valid[:, :], in_=ones[:, 0:1], compare_op=ALU.is_ge, fill=0.0,
                                     base=-31, pattern=[[0, 1]], channel_multiplier=1))
            own.mark(q.tensor_copy(identr[:, :], ident[:, :]))
            own.sync()
            q.drain().then_inc(s_made, 1)

            def split(n, slot, length, staged, gate):
                w = stage[:, slot, 0:length]
                pool.wait_ge(s_stage[slot], staged)
                if gate is not None:
                    nk, g, c0, m = gate
                    v = w.rearrange("p (k n) -> p k n", k=nk)
                    own.link(q.tensor_tensor(v, v, gates[:, g:g + 1, c0:c0 + m].broadcast_to([P, nk, m]), ALU.mult))
                hi, lo = wts[:, slot, 0, 0:length], wts[:, slot, 1, 0:length]
                if not (isinstance(n, int) and n < 2):
                    pool.wait_ge(s_wused, n - 1)
                own.link(q.tensor_tensor(hi, w, ones[:, 0:1].broadcast_to([P, length]), ALU.mult))
                q.tensor_tensor(lo, w, hi.bitcast(F32), ALU.subtract).then_inc(s_wready, 1)

            def hi_of(dst, src, done):
                shape = list(dst.shape)
                one = ones[0:shape[0], 0:1]
                for _ in shape[2:]:
                    one = one.unsqueeze(1)
                q.tensor_tensor(dst, src, one.broadcast_to(shape), ALU.mult).then_inc(done, 1)

            def lo_of(dst, src, hi, done):
                q.tensor_tensor(dst, src, hi.bitcast(F32), ALU.subtract).then_inc(done, 1)

            def format_heads_mla():
                S = ATT["mla"]
                hb = arena[:, 0:2048].rearrange("p (t n) -> p t n", t=T)
                fm = arena[:, 2048:6144].rearrange("p (a t n) -> p a t n", a=4, t=T)
                with pool.Fori(0, HEADS // 2) as pair:
                    for par in range(2):
                        h = pair * 2 + par
                        v = actT[:, par * 8192 + 4096:par * 8192 + 4096 + T * VW["mla"]].rearrange("p (t n) -> p t n", t=T)
                        pool.wait_ge(S["s_load"], h * 32 + 32)
                        pool.wait_ge(S["s_ftr"], h * 8 + 1)
                        hi_of(fm[:, 0, :, 0:96].bitcast(F32R), hb[:, :, 0:96], S["s_fhi"])
                        hi_of(fm[:, 2, :, 0:96].bitcast(F32R), hb[:, :, 96:192], S["s_fhi"])
                        pool.wait_ge(S["s_fhi"], h * 3 + 2)
                        lo_of(fm[:, 1, :, 0:96], hb[:, :, 0:96], fm[:, 0, :, 0:96], S["s_fmt"])
                        lo_of(fm[:, 3, :, 0:96], hb[:, :, 96:192], fm[:, 2, :, 0:96], S["s_fmt"])
                        pool.wait_ge(S["s_pv"], h * S["U"] + 1)
                        hi_of(v[:, :, 0:64], hb[:, :, 192:256], S["s_fhi"])
                        pool.wait_ge(S["s_fhi"], h * 3 + 3)
                        lo_of(v[:, :, 64:128], hb[:, :, 192:256], v[:, :, 0:64], S["s_fmt"])

            def format_heads_nsa():
                S = ATT["nsa"]
                kb = arena[:, 6144:8192].rearrange("p (t b n) -> p t b n", t=T, b=4)
                fm = arena[:, 0:4096].rearrange("p (a t r n) -> p a t r n", a=4, t=T, r=2)
                fc = arena[:, 5120:5376].rearrange("p (s r n) -> p s r n", s=2, r=2)
                hb = arena[:, 8192:8704].rearrange("p (t n) -> p t n", t=T)
                fq = arena[:, 4096:5120].rearrange("p (t r n) -> p t r n", t=T, r=2)
                vs = [actT[:, NSA_V[b]:NSA_V[b] + T * VW["nsa"]].rearrange("p (t n) -> p t n", t=T) for b in range(2)]
                cv = actT[0:CMP, NSA_CV:NSA_CV + P].rearrange("p (s n) -> p s n", s=2)
                with pool.Fori(0, GROUPS) as g:
                    kc = kcv[0:CMP, bass.ds(g, 1), :]
                    vc = kcv[0:CMP, bass.ds(g + 2, 1), :]
                    pool.wait_ge(nsag["s_load"], g * 64 + 64)
                    pool.wait_ge(nsag["s_ftr"], g * 9 + 1)
                    srcs = [kb[:, :, 2 * b:2 * b + 1, :].broadcast_to([P, T, 2, DH]) for b in range(2)]
                    for b in range(2):
                        hi_of(fm[:, 2 * b, :, :, :].bitcast(F32R), srcs[b], nsag["s_fhi"])
                    pool.wait_ge(s_ones, 5)
                    hi_of(fc[0:CMP, 0, :, :].bitcast(F32R), kc.broadcast_to([CMP, 2, DH]), nsag["s_fhi"])
                    pool.wait_ge(nsag["s_fhi"], g * 6 + 3)
                    for b in range(2):
                        lo_of(fm[:, 2 * b + 1, :, :, :], srcs[b], fm[:, 2 * b, :, :, :], nsag["s_fmt"])
                    lo_of(fc[0:CMP, 1, :, :], kc.broadcast_to([CMP, 2, DH]), fc[0:CMP, 0, :, :], nsag["s_fmt"])
                    pool.wait_ge(S["s_pv"], g * S["UT"] + S["pv0"])
                    for b in range(2):
                        hi_of(vs[b][:, :, 0:64], kb[:, :, 2 * b + 1, :], nsag["s_fhi"])
                    hi_of(cv[:, 0:1, :], vc, nsag["s_fhi"])
                    pool.wait_ge(nsag["s_fhi"], g * 6 + 6)
                    for b in range(2):
                        lo_of(vs[b][:, :, 64:128], kb[:, :, 2 * b + 1, :], vs[b][:, :, 0:64], nsag["s_fmt"])
                    lo_of(cv[:, 1:2, :], vc, cv[:, 0:1, :], nsag["s_fmt"])
                    with pool.Fori(0, PER_GROUP) as hh:
                        h = g * PER_GROUP + hh
                        pool.wait_ge(S["s_load"], h * 16 + 16)
                        pool.wait_ge(S["s_ftr"], h * 2 + 1)
                        hi_of(fq[:, :, 0, :].bitcast(F32R), hb, S["s_fhi"])
                        pool.wait_ge(S["s_fhi"], h + 1)
                        lo_of(fq[:, :, 1, :], hb, fq[:, :, 0, :], S["s_fmt"])

            def format_heads_dif():
                S = ATT["dif"]
                hb = arena[:, 6144:9216].rearrange("p (t w m n) -> p t w m n", t=T, w=3, m=2)
                hv = arena[:, 6144:9216].rearrange("p (t n) -> p t n", t=T)[:, :, 256:384]
                fm = arena[:, 0:6144].rearrange("p (m a t r n) -> p m a t r n", m=2, a=3, t=T, r=2)
                with pool.Fori(0, HEADS // 2) as pair:
                    for par in range(2):
                        h = pair * 2 + par
                        v = actT[:, par * 8192 + 6144:par * 8192 + 8192].rearrange("p (t s n) -> p t s n", t=T, s=2)
                        k_src = [hb[:, :, 1, m, :].unsqueeze(2).broadcast_to([P, T, 2, DH]) for m in range(2)]
                        pool.wait_ge(S["s_load"], h * 48 + 48)
                        pool.wait_ge(S["s_ftr"], h * 12 + 1)
                        for m in range(2):
                            hi_of(fm[:, m, 0, :, 0, :].bitcast(F32R), hb[:, :, 0, m, :], S["s_fhi"])
                            hi_of(fm[:, m, 1, :, :, :].bitcast(F32R), k_src[m], S["s_fhi"])
                            pool.wait_ge(S["s_fhi"], h * 5 + (2 * m + 2))
                            lo_of(fm[:, m, 0, :, 1, :], hb[:, :, 0, m, :], fm[:, m, 0, :, 0, :], S["s_fmt"])
                            lo_of(fm[:, m, 2, :, :, :], k_src[m], fm[:, m, 1, :, :, :], S["s_fmt"])
                        pool.wait_ge(S["s_pv"], h * S["U"] + 1)
                        hi_of(v[:, :, 0, :], hv, S["s_fhi"])
                        pool.wait_ge(S["s_fhi"], h * 5 + 5)
                        lo_of(v[:, :, 1, :], hv, v[:, :, 0, :], S["s_fmt"])

            staged = [0, 0]

            def straight(first, kinds):
                for m, (_, _, _, nk, cols, gate) in enumerate(kinds):
                    n = first + m
                    staged[n % 2] += 16 * len(cols)
                    width = sum(w for _, w in cols)
                    split(n, n % 2, nk * width, staged[n % 2], None if gate is None else (nk, *gate))

            def mlp(layer):
                first = FIRST[f"mlp{layer}"]
                with pool.Fori(0, FF_GROUPS) as g:
                    own.enter(g, 3)
                    split(g * 2 + first, 0, WCH, g * 16 + (staged[0] + 16), None)
                    split(g * 2 + (first + 1), 1, WCH, g * 16 + (staged[1] + 16), (2, 1, 0, D))
                own.leave(3, FF_GROUPS)
                staged[0] += 16 * FF_GROUPS
                staged[1] += 16 * FF_GROUPS

            straight(FIRST["proj0"], PROJ0)
            pool.wait_ge(s_adaev, 6)
            pool.wait_ge(s_bar, 3 * BAR["mla"])
            format_heads_mla()
            straight(FIRST["out0"], OUT0[:2])
            pool.wait_ge(s_bar, 3 * BAR["nsa"])
            format_heads_nsa()
            straight(FIRST["out0"] + 2, OUT0[2:])
            mlp(0)
            straight(FIRST["proj1"], PROJ1)
            pool.wait_ge(s_adaev, 12)
            pool.wait_ge(s_bar, 3 * BAR["dif"])
            format_heads_dif()
            straight(FIRST["out1"], OUT1)
            mlp(1)


        @block.tensor
        def _(pe):
            q = nc.tensor

            def product(dst, passes, last):
                ins = None
                for n, (a, b) in enumerate(passes):
                    ins = q.matmul(dst, a, b, start=(n == 0), stop=(n == len(passes) - 1 and last))
                return ins

            def ada(g):
                pe.wait_ge(s_adaacc, g + 1)
                if g == 1:
                    pe.wait_ge(s_adaev, g)
                if g >= 2:
                    pe.wait_ge(s_raw, 8 * (g - 2) + 2)
                acc = arena[:, 8192:9216]
                bias = arena[0:1, 9216 + (g % 2) * 1024:10240 + (g % 2) * 1024]
                if g in (2, 5):
                    for h in range(2):
                        q.matmul(ps[:, h, :], ones[:, :], acc[:, h * 512:(h + 1) * 512], start=True, stop=False)
                        ins = q.matmul(ps[:, h, :], ones[0:1, :], bias[:, h * 512:(h + 1) * 512],
                                       start=False, stop=True)
                else:
                    for k in range(KD):
                        q.matmul(ps[:, 0, k:k + 1], acc[:, k * P:(k + 1) * P], ones[:, 0:1], start=True, stop=False)
                        ins = q.matmul(ps[:, 0, k:k + 1], bias[:, k * P:(k + 1) * P], ones[0:1, 0:1],
                                       start=False, stop=True)
                ins.then_inc(s_adamm, 1)
                if g >= 2:
                    pe.wait_ge(s_adaev, g + 1)

            def ada1():
                for g, b in enumerate(ADA_BANKS):
                    acc = ada_acc[:, g * 1024:(g + 1) * 1024]
                    if g in (2, 5):
                        for h in range(2):
                            ins = q.matmul(ps[:, b + h, :], ones[:, :], acc[:, h * 512:(h + 1) * 512],
                                           start=True, stop=True)
                    else:
                        for k in range(KD):
                            ins = q.matmul(ps[:, b, k:k + 1], acc[:, k * P:(k + 1) * P], ones[:, 0:1],
                                           start=True, stop=True)
                    ins.then_inc(s_adamm, 1)

            def transposes(name, src, order, only):
                for idx, (k, half) in enumerate(order):
                    if only not in (None, half):
                        continue
                    if idx >= 8:
                        pe.wait_ge(s_trl, TR[name] + idx - 7)
                    for m in range(4):
                        ins = q.transpose(ps[:, idx % 8, m * P:(m + 1) * P], src(4 * half + m, k), ident[:, :])
                    ins.then_inc(s_tr, 1)

            def norm_banks(name, n):
                for idx, (k, half) in enumerate(ORDER):
                    pe.wait_ge(s_xn, 8 * n + 4 * half + 4)
                    if idx >= 8:
                        pe.wait_ge(s_trl, TR[name] + idx - 7)
                    for m in range(4):
                        t = 4 * half + m
                        ins = q.transpose(ps[:, idx % 8, m * P:(m + 1) * P],
                                          arena[:, t * D + k * P:t * D + (k + 1) * P], ident[:, :])
                    ins.then_inc(s_tr, 1)

            def splits(a, b):
                return [(a[0], b[0]), (a[0], b[1]), (a[1], b[0])]

            def project(chunk, width, raw_free, norm=None):
                for kh in range(2):
                    pe.wait_ge(s_wready, chunk + (kh + 1))
                    w = [wts[:, kh, s, 0:4 * width].rearrange("p (k n) -> p k n", k=4) for s in range(2)]
                    for t in range(T):
                        if kh == 0 and raw_free is not None:
                            pe.wait_ge(s_raw, raw_free + (t + 1))
                        if kh == 0 and norm is not None and t <= 4:
                            pe.wait_ge(s_trl, TR[norm] + min(9 + t + 3 * (t == 4), 16))
                        passes = []
                        for k in range(4):
                            a = [aT[:, s, kh * 4 + k, t * P:(t + 1) * P] for s in range(2)]
                            passes += splits(a, [w[s][:, k, :] for s in range(2)])
                        for n, (a, b) in enumerate(passes):
                            ins = q.matmul(ps[:, t, 0:width], a, b, start=(kh == 0 and n == 0),
                                           stop=(kh == 1 and n == len(passes) - 1))
                        if t == T - 1:
                            ins.then_inc(s_wused, 1)
                        elif kh == 1:
                            ins.then_inc(s_mm, 1)

            def up():
                for which, (k0, halfw) in enumerate(((0, 384), (2, 512))):
                    n = FIRST["proj0"] + 8 + which
                    pe.wait_ge(s_wready, n + 1)
                    w = [wts[:, which, s, 0:4 * halfw].rearrange("p (k n) -> p k n", k=2) for s in range(2)]
                    for t in range(T):
                        u = which * T + t
                        if u >= 4:
                            pe.wait_ge(s_raw, RAW["up"] + u - 3)
                        for h in range(2):
                            passes = []
                            for k in range(2):
                                a = [aT[:, s, k0 + k, t * P:(t + 1) * P] for s in range(2)]
                                passes += splits(a, [w[s][:, k, h * halfw:(h + 1) * halfw] for s in range(2)])
                            ins = product(ps[:, (u % 4) * 2 + h, 0:halfw], passes, True)
                        ins.then_inc(s_wused if t == T - 1 else s_mm, 1)

            def compress():
                pe.wait_ge(s_cmpx, 16 * 4)
                cb = xres[0:CMP, 0:4096].rearrange("p (a n) -> p a n", a=4)
                for a in range(4):
                    for i in range(8):
                        ins = q.transpose(ps[:, a, i * CMP:(i + 1) * CMP],
                                          cb[:, a, i * P:(i + 1) * P], ident[0:CMP, 0:CMP])
                    ins.then_inc(s_cpe, 1)
                pe.wait_ge(s_cmpw, 16 * 2)
                pe.wait_ge(s_cmp, 16 * 6)
                w1 = stage[:, :, :].rearrange("p j (i n) -> p j i n", i=16)
                blk = arena[:, 4096:8192].rearrange("p (i a m) -> p i a m", i=16, a=4)
                pe.wait_ge(s_cdve, 2)
                for j in range(2):
                    ins = product(ps[:, 4 + j, 0:P], [(w1[:, j, i, :], blk[:, i, 2 * j:2 * j + 2, :])
                                                      for i in range(16)], True)
                    ins.then_inc(s_cpe, 1)
                hid = arena[:, 8192:8448].rearrange("p (j g m) -> p j g m", j=2, g=2)
                w2 = arena[:, 10240:10368].rearrange("p (j n) -> p j n", j=2)
                pe.wait_ge(s_cact, 2)
                for j in range(2):
                    for g in range(2):
                        ins = q.matmul(ps[0:CMP, 6, (2 * j + g) * DH:(2 * j + g + 1) * DH], hid[:, j, g, :],
                                       w2[:, j, :], start=True, stop=True)
                ins.then_inc(s_cpe, 1)

            def attend(name, turn, stack_src, width, scores, values, more_scores):
                S = ATT[name]
                U, UT, HT, units, before = S["U"], S["UT"], S["HT"], S["units"], S["before"]
                NA = stacks_taken(S, TURN - 1, S["prep"] - 1, 0)
                ND = stacks_taken(S, TURN - 1, S["prep"] - 1, 1)

                def bank(use):
                    k = S["uses"].index(use)
                    if k >= 2:
                        kind, a, b = S["uses"][k - 2]
                        if kind == "half":
                            pe.wait_ge(S["s_pl"], turn * HT + (before[a] + b + 2))
                        elif dve_takes(a, b):
                            pe.wait_ge(S["s_fevd"], turn * ND + (stacks_taken(S, a, b, 1) + 1))
                        else:
                            pe.wait_ge(S["s_feva"], turn * NA + (stacks_taken(S, a, b, 0) + 1))
                    return 4 + k % 2

                def stack(i, b):
                    at = bank(("stack", i, b))
                    laid = S["laid"]
                    if b % 2 == 0 and (b == 0 or laid[b // 2] > laid[b // 2 - 1]):
                        pe.wait_ge(S["s_fmt"], turn * (TURN * S["nfmt"]) + (i * S["nfmt"] + laid[b // 2] + 1))
                    for m in range(4):
                        ins = q.transpose(ps[0:width, at, m * P:(m + 1) * P],
                                          stack_src[b // 2][:, 4 * (b % 2) + m, 0:width], ident[:, :])
                    ins.then_inc(S["s_ftr"], 1)

                def qk(n):
                    u = units[n]
                    if n % U == 0:
                        i = u["head"]

                        pe.wait_ge(S["s_feva"], turn * NA + (stacks_taken(S, i, S["prep"] - 1, 0) + 1))
                        if i == 0:
                            pe.wait_ge(S["s_fevd"], turn * ND + (stacks_taken(S, i, S["prep"] - 1, 1) + 1))
                            more_scores()
                    if n >= 2:
                        pe.wait_ge(S["s_ex"], turn * UT + n)
                    base = (n % 2) * 1024
                    for b in range(0, u["n"], 4):
                        w = min(4, u["n"] - b) * P
                        dst = psf[:, base + b * P:base + b * P + w]
                        for m, (a, c2) in enumerate(scores(u, (u["k0"] + b) * P, w)):
                            ins = q.matmul(dst, a, c2, start=(m == 0), stop=False, skip_group_check=True)
                        if u["kind"] == "cmp":
                            wanted = [(0, 0, 1, cmask[:, 56 - 8 * u["t"]:184 - 8 * u["t"]])]
                        else:
                            at = u["t"] - u["k0"]
                            two = 1 if at > b else 0
                            wanted = [(at, at - two, 1 + two, masks[:, (2 - two) * P:3 * P])]
                            if u["kind"] == "win" and u["t"] >= WINDOW_TILES:
                                wanted.append((0, 0, 2, masks[:, 0:2 * P]))
                        for at, first, tiles, mask in wanted:
                            if b <= at < b + 4:
                                ins = q.matmul(psf[:, base + first * P:base + (first + tiles) * P], identr[:, :],
                                               mask, start=False, stop=False, skip_group_check=True)
                    ins.then_inc(S["s_qk"], 1)

                def tr(n):
                    u = units[n]
                    pe.wait_ge(S["s_ex"], turn * UT + (n + 2))
                    for half in range(u["halves"]):
                        at = bank(("half", n, half))
                        for m in range(4 * half, min(4 * half + 4, u["n"])):
                            ins = q.transpose(ps[:, at, (m % 4) * P:(m % 4 + 1) * P],
                                              pexp[:, n % 2, m * P:(m + 1) * P], ident[:, :])
                        ins.then_inc(S["s_t"], 1)

                def pv(n):
                    u = units[n]
                    if n % U == 0:
                        pe.wait_ge(S["s_fmt"], turn * (TURN * S["nfmt"]) + ((u["head"] + 1) * S["nfmt"] + 1))
                    pe.wait_ge(S["s_pl"], turn * HT + (before[n + 1] + 1))
                    pe.wait_ge(S["s_o"], turn * UT + (max(n - 1, 0) + 1))
                    passes = []
                    for m in range(u["n"]):
                        passes += [(pT[:, s, n % 2, m * P:(m + 1) * P], values(u, u["k0"] + m)) for s in range(2)]
                    product(ps[:, 6 + n % 2, 0:VW[name]], passes, True).then_inc(S["s_pv"], 1)

                pe.wait_ge(S["s_o"], turn * UT + 1)
                pe.wait_ge(S["s_pl"], turn * HT + 1)
                pe.wait_ge(S["s_ex"], turn * UT + 1)
                for b in range(S["prep"]):
                    stack(0, b)
                qk(0)
                qk(1)
                for n in range(UT):
                    if n + 2 < UT:
                        qk(n + 2)
                    tr(n)
                    if n >= 1:
                        pv(n - 1)
                    for i, b in S["at"][n]:
                        stack(i, b)
                pv(UT - 1)

            def mla():
                pe.wait_ge(s_ones, 2)
                fm = arena[:, 2048:6144].rearrange("p (a t n) -> p a t n", a=4, t=T)
                with pe.Fori(0, TURNS) as turn:
                    def scores(u, c0, w):
                        o = (u["head"] % 2) * 8192
                        st = [actT[0:MLA_DH, o + n * 1024:o + (n + 1) * 1024] for n in range(4)]
                        qt = [st[s][:, u["t"] * P:(u["t"] + 1) * P] for s in range(2)]
                        return splits(qt, [st[2 + s][:, c0:c0 + w] for s in range(2)])

                    def values(u, kb):
                        o = (u["head"] % 2) * 8192 + 4096 + kb * VW["mla"]
                        return actT[:, o:o + VW["mla"]]

                    attend("mla", turn, [fm[:, n, :, :] for n in range(4)], MLA_DH, scores, values, lambda: None)

            def nsa():
                st = {"slc": [actT[:, 0:1024], actT[:, 1024:2048]], "win": [actT[:, 2048:3072], actT[:, 3072:4096]],
                      "cmp": [actT[:, NSA_CK + s * P:NSA_CK + (s + 1) * P] for s in range(2)]}
                v = {"slc": NSA_V[0], "win": NSA_V[1], "cmp": NSA_CV}
                fm = arena[:, 0:4096].rearrange("p (a t n) -> p a t n", a=4, t=T)
                fq = arena[:, 4096:5120].rearrange("p (t n) -> p t n", t=T)
                fc = arena[:, 5120:5376].rearrange("p (s n) -> p s n", s=2)
                S = ATT["nsa"]
                pe.wait_ge(s_ones, 4)
                with pe.Fori(0, GROUPS) as g:
                    pe.wait_ge(S["s_o"], g * S["UT"] + 1)
                    pe.wait_ge(S["s_pl"], g * S["HT"] + 1)
                    pe.wait_ge(S["s_ex"], g * S["UT"] + 1)
                    pe.wait_ge(nsag["s_fmt"], g * 6 + 4)
                    for n in range(4):
                        for half in range(2):
                            for m in range(4):
                                ins = q.transpose(ps[:, 2 * n + half, m * P:(m + 1) * P],
                                                  fm[:, n, 4 * half + m, :], ident[:, :])
                            ins.then_inc(nsag["s_ftr"], 1)
                    pe.wait_ge(nsag["s_feva"], g * 5 + 1)
                    for s in range(2):
                        ins = q.transpose(ps[:, 0, s * P:(s + 1) * P], fc[:, s, :], ident[:, :])
                    ins.then_inc(nsag["s_ftr"], 1)
                    pe.wait_ge(nsag["s_feva"], g * 5 + 5)
                    pe.wait_ge(nsag["s_fevd"], g * 4 + 4)

                    def values_ready():
                        pe.wait_ge(nsag["s_fmt"], g * 6 + 7)

                    def scores(u, c0, w):
                        o = 8192 + (u["head"] % 2) * 1024 + u["t"] * P
                        return [(actT[:, o:o + P], st[u["kind"]][s][:, c0:c0 + w]) for s in range(2)]

                    def values(u, kb):
                        o = v[u["kind"]] + kb * VW["nsa"]
                        return actT[:, o:o + VW["nsa"]]

                    attend("nsa", g, [fq], P, scores, values, values_ready)

            def dif():
                fm = arena[:, 0:6144].rearrange("p (a t n) -> p a t n", a=6, t=T)
                with pe.Fori(0, TURNS) as turn:
                    def scores(u, c0, w):
                        o = (u["head"] % 2) * 8192 + 3072 * u["factor"]
                        qt = actT[:, o + u["t"] * P:o + (u["t"] + 1) * P]
                        return [(qt, actT[:, o + (1 + s) * 1024 + c0:o + (1 + s) * 1024 + c0 + w]) for s in range(2)]

                    def values(u, kb):
                        o = (u["head"] % 2) * 8192 + 6144 + kb * VW["dif"]
                        return actT[:, o:o + VW["dif"]]

                    attend("dif", turn, [fm[:, n, :, :] for n in range(6)], P, scores, values, lambda: None)

            def mlp(layer):
                first = FIRST[f"mlp{layer}"]
                norm = ("norm1", "norm3")[layer]
                w1 = [wts[:, 0, s, :].rearrange("p (k n) -> p k n", k=KD) for s in range(2)]
                w2 = [wts[:, 1, s, :].rearrange("p (k n) -> p k n", k=2) for s in range(2)]
                with pe.Fori(0, FF_GROUPS) as g:
                    pe.wait_ge(s_wready, g * 2 + (first + 1))
                    for idx, (half, f) in enumerate(((0, 0), (0, 1), (1, 0), (1, 1))):
                        if idx % 2 == 0:
                            pe.wait_ge(s_trl, TR[norm] + (16 if half else 10))
                        pe.wait_ge(s_gl, g * 4 + (layer * 64 + max(idx - 3, 0) + 1))
                        passes = []
                        for k in range(KD):
                            passes += splits([w1[s][:, k, f * P:(f + 1) * P] for s in range(2)],
                                             [aT[:, s, k, half * 512:(half + 1) * 512] for s in range(2)])
                        product(ps[:, idx, :], passes, True).then_inc(s_wused if idx == 3 else s_g1, 1)
                    pe.wait_ge(s_wready, g * 2 + (first + 2))
                    for idx in range(16):
                        t, n = idx // 2, idx % 2
                        if idx == 0:
                            pe.wait_ge(s_gl, g * 4 + (layer * 64 + 3))
                        if idx == 8:
                            pe.wait_ge(s_gl, g * 4 + (layer * 64 + 5))
                        pe.wait_ge(s_ya, g * 16 + (layer * 256 + max(idx - 3, 0) + 1))
                        passes = []
                        for f in range(2):
                            passes += splits([gT[:, s, f, t * P:(t + 1) * P] for s in range(2)],
                                             [w2[s][:, f, n * 512:(n + 1) * 512] for s in range(2)])
                        product(ps[:, 4 + idx % 4, :], passes, True).then_inc(s_wused if idx == 15 else s_y, 1)

            for name in ATT:
                for key in ("s_t", "s_ftr"):
                    pe.sem_inc(ATT[name][key], 1)
                pe.sem_inc(ATT[name]["s_pv"], ATT[name]["pv0"])
            pe.sem_inc(nsag["s_ftr"], 1)
            pe.sem_inc(s_y, 1)
            pe.wait_ge(s_made, 1)
            ada(0)
            ada(1)
            norm_banks("norm0", 0)
            barrier(pe, q, "proj0", wait=False)
            for j, cols in enumerate(HYC):
                project(2 * j, sum(w for _, w in cols), None if j == 0 else 8 * (j - 1), None if j else "norm0")
                ada(2 + j)
            barrier(pe, q, "latent")
            latents = xres[:, 4096:8192].rearrange("p (t n) -> p t n", t=T)
            pe.wait_ge(s_proc, 3)
            transposes("latent", lambda t, k: latents[:, t, k * P:(k + 1) * P],
                       [(k, h) for h in range(2) for k in range(4)], None)
            barrier(pe, q, "up")
            up()
            barrier(pe, q, "cmp")
            compress()
            barrier(pe, q, "mla")
            mla()
            barrier(pe, q, "nsa")
            nsa()
            barrier(pe, q, "otr0")
            for half in range(2):
                transposes("otr0", lambda t, k: xr[:, t, k * P:(k + 1) * P], ORDER, half)
            barrier(pe, q, "out0")
            for j in range(2):
                project(FIRST["out0"] + 2 * j, 512, None if j == 0 else RAW["out0"])

            norm_banks("norm1", 1)
            barrier(pe, q, "mlp0", wait=False)
            mlp(0)
            barrier(pe, q, "ada1")
            ada1()
            norm_banks("norm2", 2)
            barrier(pe, q, "proj1", wait=False)
            project(FIRST["proj1"], 512, None, "norm2")
            with pe.Fori(0, 5) as j:
                project(j * 2 + (FIRST["proj1"] + 2), 512, j * 8 + RAW["proj1"])
            barrier(pe, q, "dif")
            dif()
            barrier(pe, q, "sub")
            for half in range(2):
                pe.wait_ge(s_proc, 14 + half)
                transposes("otr1", lambda t, k: xr[:, t, k * P:(k + 1) * P], ORDER, half)
            barrier(pe, q, "out1")
            for j in range(2):
                project(FIRST["out1"] + 2 * j, 512, None if j == 0 else RAW["out1"])

            norm_banks("norm3", 3)
            barrier(pe, q, "mlp1", wait=False)
            mlp(1)
            barrier(pe, q, "end")

        @block.scalar
        def _(act):
            q = nc.scalar
            own = Count(act, s_act)
            std = [0]
            spills = [0, 0]

            def sqrt(n):
                std[0] += 1
                act.wait_ge(s_var, std[0])
                q.activation(small[:, 2, 0:n], small[:, 1, 0:n], ACT.Sqrt).then_inc(s_std, 1)

            def sumsq(n, added):
                for t in range(T):
                    if t >= 1:
                        act.wait_ge(s_ss, 8 * n + t)
                    if added is not None:
                        act.wait_ge(s_raw, added + t)
                    q.activation(gT[:, 0, 0, :], xr[:, t, :], ACT.Square,
                                 accum_out=small[:, 0, t:t + 1]).then_inc(s_ss, 1)

            def take_hi(name, order, scale, shift, only=None):
                for idx, (k, half) in enumerate(order):
                    if only not in (None, half):
                        continue
                    act.wait_ge(s_tr, TR[name] + idx + 1)
                    dst = aT[:, 0, k, half * 512:(half + 1) * 512]
                    src = ps[:, idx % 8, :]
                    if shift is not None:
                        act.wait_ge(s_trl, TR[name] + max(idx - 1, 0))
                        tmp = arena[:, 8192 + (idx % 2) * 512:8704 + (idx % 2) * 512]
                        own.link(q.activation(tmp, src, ACT.Identity, bias=shift(k), scale=scale(k)))
                        q.activation(dst, tmp, ACT.Copy).then_inc(s_trh, 1)
                    elif scale is not None:
                        q.activation(dst, src, ACT.Copy, scale=scale(k)).then_inc(s_trh, 1)
                    else:
                        q.activation(dst, src, ACT.Copy).then_inc(s_trh, 1)

            def norm(name, n):
                sqrt(T)
                w = n % 2
                take_hi(name, ORDER, lambda k: modv[:, 2 * w, k:k + 1], lambda k: modv[:, 2 * w + 1, k:k + 1])

            def spill(slot, ready, pairs):
                if ready is not None:
                    act.wait_ge(s_proc, ready)
                for dst, src in pairs:
                    act.dma_start(dst, src).then_inc(s_spill[slot], 16)
                    spills[slot] += 16

            def stored(*slots):
                for slot in slots:
                    act.wait_ge(s_spill[slot], spills[slot])

            def take(mm, wused, name, t, dst, src):
                if t == T - 1:
                    act.wait_ge(s_wused, wused)
                else:
                    act.wait_ge(s_mm, mm + t + 1)
                q.activation(dst, src, ACT.Copy).then_inc(s_raw, 1)

            for name in ATT:
                for key in ("s_ex", "s_feva"):
                    act.sem_inc(ATT[name][key], 1)
            act.sem_inc(s_gh, 1)
            act.wait_ge(s_const, 16 * NCONST)
            q.activation(cond[:, 1, :], cond[:, 0, :], ACT.Exp, scale=-1.0).then_inc(s_cond, 1)
            act.wait_ge(s_ang, 1)
            q.activation(rope[:, 1, :, :], ang, ACT.Sin).then_inc(s_sin, 1)
            q.activation(half_ang, ang, ACT.Sin, scale=0.5).then_inc(s_sin, 1)
            act.wait_ge(s_lam, 1)
            q.activation(lams[:, 2:4], lams[:, 0:2], ACT.Exp).then_inc(s_cond, 1)
            act.wait_ge(s_x, 16)
            sumsq(0, None)
            norm("norm0", 0)
            barrier(act, q, "proj0")
            for j in range(4):
                width = sum(w for _, w in HYC[j])
                stored(j % 2)
                for t in range(T):
                    take(7 * j, 2 * j + 2, "proj0", t, raw[:, j % 2, t, 0:width], ps[:, t, 0:width])
                if j != 2:
                    sqrt({0: 64, 1: 16, 3: 16}[j])
                else:
                    sqrt(16)
                    act.wait_ge(s_raw, 24)
                    q.activation(gate3[:, :, :], raw[:, 0, :, 256:280], ACT.Exp, scale=-1.0).then_inc(s_cond, 1)
                    q.activation(kpe[:, :, :], raw[:, 0, :, 280:312], ACT.Copy).then_inc(s_cond, 1)
                if j == 0:
                    spill(0, 1, [(nsav[:, :, 0:512], raw[:, 0, :, :])])
                if j == 1:
                    spill(1, 2, [(nsav[:, :, 512:1024], raw[:, 1, :, :])])
                if j == 2:
                    spill(0, 3, [(nsav[:, :, 1024:1280], raw[:, 0, :, 0:256])])
            stored(0, 1)
            barrier(act, q, "latent")
            take_hi("latent", [(k, h) for h in range(2) for k in range(4)], lambda k: latv[:, k:k + 1], None)
            barrier(act, q, "up")
            squares_of = arena[:, 8192:11264].rearrange("p (t h n) -> p t h n", t=4, h=HEADS)

            def square(n, v, taken):
                act.wait_ge(s_raw, RAW["up"] + taken)
                act.wait_ge(s_proc, 4 + n)
                if n >= 2:
                    act.wait_ge(s_kpe, n - 1)
                q.activation(squares_of, v, ACT.Square).then_inc(s_sq, 1)
                sqrt(32)

            for hf in range(2):
                for t in range(4 * hf, 4 * hf + 4):
                    take(MM["up"], 9, "up", t, upq[hf][:, t % 4, :].rearrange("p (h n) -> p h n", h=2),
                         ps[:, (t % 4) * 2:(t % 4) * 2 + 2, 0:384])
            square(0, upq[0].rearrange("p t (h n) -> p t h n", h=HEADS), 4)
            for hf in range(2):
                for t in range(4 * hf, 4 * hf + 4):
                    take(MM["up"] + 7, 10, "up", t, upk[hf][:, t % 4, :, 32:160],
                         psf[:, (t % 4) * 1024:(t % 4) * 1024 + 1024].rearrange("p (h n) -> p h n", h=HEADS))
                if hf == 0:
                    square(1, upq[1].rearrange("p t (h n) -> p t h n", h=HEADS), 8)
                    spill(0, 5, [(mlav[:, 0:4, 0:768], upq[0])])
            for hf in range(2):
                square(2 + hf, upk[hf][:, :, :, 0:96], 12 + 4 * hf)
                rowsd = mlav[:, 4 * hf:4 * hf + 4, :]
                if hf == 0:
                    spill(1, 6, [(mlav[:, 4:8, 0:768], upq[1])])
                spill(hf, 7 + hf, [(rowsd[:, :, 768:2048], upk[hf].rearrange("p t h n -> p t (h n)"))])
            stored(0, 1)
            barrier(act, q, "cmp")
            for j in range(2):
                act.wait_ge(s_cpe, 5 + j)
                q.activation(arena[:, 8192 + j * P:8320 + j * P], ps[:, 4 + j, 0:P],
                             ACT.Gelu_apprx_tanh).then_inc(s_cact, 1)
            sqrt(2)
            barrier(act, q, "mla")

            def attend(name, turn, stack_dst, width):
                S = ATT[name]
                U, UT, HT, units, before = S["U"], S["UT"], S["HT"], S["units"], S["before"]
                NF = S["prep"] * TURN

                def exps(n):
                    u = units[n]
                    act.wait_ge(S["s_mx"], turn * UT + (n + 1))
                    act.wait_ge(S["s_t"], turn * HT + (before[max(n - 1, 0)] + 1))
                    base = (n % 2) * 1024
                    sums = dict(accum_out=rows[:, 1, n % 8:n % 8 + 1]) if name == "dif" else {}
                    q.activation(pexp[:, n % 2, 0:u["n"] * P], psf[:, base:base + u["n"] * P], ACT.Exp,
                                 bias=rows[:, 0, n % 8:n % 8 + 1], **sums).then_inc(S["s_ex"], 1)

                def take_p(n):
                    u = units[n]
                    for half in range(u["halves"]):
                        at = 4 + S["uses"].index(("half", n, half)) % 2
                        w = min(4, u["n"] - 4 * half) * P
                        act.wait_ge(S["s_t"], turn * HT + (before[n] + half + 2))
                        act.wait_ge(S["s_pv"], turn * UT + (max(n - 1, 0) + S["pv0"]))
                        q.activation(pT[:, 0, n % 2, 512 * half:512 * half + w], ps[:, at, 0:w],
                                     ACT.Copy).then_inc(S["s_ph"], 1)

                def take_stack(i, b):
                    at = 4 + S["uses"].index(("stack", i, b)) % 2
                    act.wait_ge(S["s_ftr"], turn * NF + (stacks_done(S, i, b) + 1))
                    q.activation(stack_dst(i, b), ps[0:width, at, :], ACT.Copy).then_inc(S["s_feva"], 1)

                for b in range(0, S["prep"], 2):
                    take_stack(0, b)
                exps(0)
                exps(1)
                for n in range(UT):
                    take_p(n)
                    for i, b in S["at"][n]:
                        take_stack(i, b)
                    if n + 2 < UT:
                        exps(n + 2)

            with act.Fori(0, TURNS) as turn:
                attend("mla", turn, stack_slots["mla"], MLA_DH)
            barrier(act, q, "nsa")
            with act.Fori(0, GROUPS) as g:
                for n in range(4):
                    act.wait_ge(nsag["s_ftr"], g * 9 + (2 * n + 2))
                    q.activation(actT[:, n * 1024:n * 1024 + 512], ps[:, 2 * n, :], ACT.Copy).then_inc(nsag["s_feva"], 1)
                act.wait_ge(nsag["s_ftr"], g * 9 + 10)
                q.activation(actT[:, NSA_CK:NSA_CV], ps[:, 0, 0:256], ACT.Copy).then_inc(nsag["s_feva"], 1)
                attend("nsa", g, stack_slots["nsa"], P)
            barrier(act, q, "otr0")
            take_hi("otr0", ORDER, None, None)
            barrier(act, q, "out0")
            sumsq(1, RAW["out0"] + 9)
            norm("norm1", 1)

            def mlp(layer):
                first = FIRST[f"mlp{layer}"]
                with act.Fori(0, FF_GROUPS) as g:
                    for idx, (half, f) in enumerate(((0, 0), (0, 1), (1, 0), (1, 1))):
                        if idx == 3:
                            act.wait_ge(s_wused, g * 2 + (first + 1))
                        else:
                            act.wait_ge(s_g1, g * 3 + (layer * 48 + idx + 1))
                        act.wait_ge(s_gt, g * 4 + (layer * 64 + max(idx - 1, 0) + 1))
                        q.activation(relu[:, idx % 2, :], ps[:, idx, :], ACT.Relu).then_inc(s_gr, 1)
                        act.wait_ge(s_gt, g * 4 + (layer * 64 + idx + 2))
                        act.wait_ge(s_y, g * 15 + (layer * 240 + 1))
                        q.activation(gT[:, 0, f, half * 512:(half + 1) * 512], sq[:, idx % 2, :],
                                     ACT.Copy).then_inc(s_gh, 1)

            barrier(act, q, "mlp0")
            mlp(0)
            barrier(act, q, "ada1")
            sumsq(2, None)
            norm("norm2", 2)
            barrier(act, q, "proj1")
            for j in range(6):
                stored(j % 2)
                for t in range(T):
                    take(MM["proj1"] + 7 * j, FIRST["proj1"] + 2 * j + 2, "proj1", t, raw[:, j % 2, t, :], ps[:, t, :])
                if j < 4:
                    sqrt(64)
                    spill(j % 2, 10 + j, [(difv[:, :, j * 512:(j + 1) * 512], raw[:, j % 2, :, :])])
                else:
                    act.wait_ge(s_raw, RAW["proj1"] + 8 * (j + 1))
                    spill(j % 2, None, [(difv[:, :, j * 512:(j + 1) * 512], raw[:, j % 2, :, :])])
            stored(0, 1)
            barrier(act, q, "dif")
            with act.Fori(0, TURNS) as turn:
                attend("dif", turn, stack_slots["dif"], P)
            barrier(act, q, "sub")
            for half in range(2):
                q.activation(arena[:, half * 4096:(half + 1) * 4096].rearrange("p (t n) -> p t n", t=4),
                             xr[:, 4 * half:4 * half + 4, :], ACT.Square).then_inc(s_sq, 1)
            for half in range(2):
                sqrt(32)
                take_hi("otr1", ORDER, lambda k: gsub[:, 0:1], None, half)
            barrier(act, q, "out1")
            sumsq(3, RAW["out1"] + 9)
            norm("norm3", 3)
            barrier(act, q, "mlp1")
            mlp(1)
            barrier(act, q, "end")

        @block.vector
        def _(dve):
            q = nc.vector
            own = Count(dve, s_dve)
            std = [0]
            procs = [0]

            for name in ATT:
                for key in ("s_pl", "s_o", "s_fevd"):
                    dve.sem_inc(ATT[name][key], 1)
            for primed in (s_gt, s_gl, s_ya, s_adad):
                dve.sem_inc(primed, 1)
            dve.wait_ge(s_const, 16 * NCONST)
            dve.wait_ge(s_made, 1)
            for n in range(16):
                own.mark(q.memset(invf[:, n:n + 1], float(np.float32(THETA ** (-n / 16)))))
            for n in range(8):
                own.mark(q.memset(invf[:, 16 + n:17 + n], float(np.float32(THETA ** (-n / 8)))))
            own.mark(q.tensor_copy(post[:, :], posi[:, :]))
            own.mark(q.tensor_scalar(gainq[:, 0, :], gainq[:, 0, :], MLA_DH ** -0.5, None, ALU.mult))
            own.mark(q.tensor_scalar(gainh[:, 0, :], gainh[:, 0, :], DH ** -0.5, None, ALU.mult))
            own.mark(q.tensor_scalar(gainh[:, 4, :], gainh[:, 4, :], DH ** -0.5, None, ALU.mult))
            own.mark(q.tensor_scalar(gsub[:, :], gsub[:, :], 1.0 - LAM_INIT, None, ALU.mult))
            own.mark(q.tensor_tensor(lamt[:, 0, :], lamt[:, 0, :], lamt[:, 1, :], ALU.mult))
            own.mark(q.tensor_tensor(lamt[:, 2, :], lamt[:, 2, :], lamt[:, 3, :], ALU.mult))
            dve.wait_ge(s_cond, 1)
            own.mark(q.tensor_scalar(cond[:, 1, :], cond[:, 1, :], 1.0, None, ALU.add))
            own.sync()
            own.mark(q.reciprocal(cond[:, 1, :], cond[:, 1, :]))
            own.mark(q.tensor_reduce(lams[:, 0:1], lamt[:, 0, :], AX.X, ALU.add))
            own.mark(q.tensor_reduce(lams[:, 1:2], lamt[:, 2, :], AX.X, ALU.add))
            own.link(q.tensor_tensor(ang, post[:, :].unsqueeze(2).broadcast_to([P, T + 1, 24]),
                                     invf[:, :].unsqueeze(1).broadcast_to([P, T + 1, 24]), ALU.mult))
            q.tensor_copy(lams[:, 4:5], lams[:, 0:1]).then_inc(s_lam, 1)
            own.mark(q.tensor_tensor(cond[:, 0, :], cond[:, 0, :], cond[:, 1, :], ALU.mult))
            own.link(q.tensor_scalar(turns, ang, 1.0 / (2 * math.pi), 12582912.0, ALU.mult, ALU.add))
            own.link(q.tensor_scalar(turns, turns, -12582912.0, None, ALU.add))
            C1 = 6.28125
            C2 = float(np.float32(np.round((2 * math.pi - C1) * 2 ** 21) / 2 ** 21))
            C3 = 2 * math.pi - C1 - C2
            for cc in (C1, C2, C3):
                own.link(q.scalar_tensor_tensor(ang, turns, -cc, ang, ALU.mult, ALU.add))
            q.tensor_scalar(ang, ang, 3.1415925, -3.1415925, ALU.min, ALU.max).then_inc(s_ang, 1)
            dve.wait_ge(s_sin, 2)
            own.link(q.scalar_tensor_tensor(rope[:, 0, :, :], half_ang, -2.0, half_ang, ALU.mult, ALU.mult))
            own.mark(q.tensor_scalar(rope[:, 0, :, :], rope[:, 0, :, :], 1.0, None, ALU.add))
            dve.wait_ge(s_cond, 2)
            own.link(q.tensor_tensor(lams[:, 5:6], lams[:, 3:4], lams[:, 2:3], ALU.subtract))
            own.link(q.tensor_scalar(lams[:, 6:7], lams[:, 5:6], -LAM_INIT, None, ALU.add))

            def ada_out(layer, g, bank):
                dve.wait_ge(s_adamm, 6 * layer + g + 1)
                if g in (2, 5):
                    q.tensor_copy(gates[:, g // 3, :], psf[:, bank * 512:bank * 512 + 1024]).then_inc(s_adaev, 1)
                elif g in (1, 4):
                    w = g // 3
                    q.scalar_tensor_tensor(modv[:, 2 * w, :], ps[:, bank, 0:KD], 1.0, normv[:, 2 * layer + w, :],
                                           ALU.add, ALU.mult).then_inc(s_adaev, 1)
                else:
                    q.tensor_copy(modv[:, 2 * (g // 3) + 1, :], ps[:, bank, 0:KD]).then_inc(s_adaev, 1)

            landed = [0, 0]

            def ada(g):
                acc = arena[:, 8192:9216]
                if g >= 1:
                    dve.wait_ge(s_adamm, g)
                for half in range(2):
                    slot = half if g < 2 else 1
                    landed[slot] += 32 if half == 0 else 16
                    dve.wait_ge(s_adal[slot], landed[slot])
                    piece = arena[:, slot * 4096:slot * 4096 + 4096].rearrange("p (k n) -> p k n", k=4)
                    for k in range(4):
                        s = cond[:, 0, 4 * half + k:4 * half + k + 1]
                        last = half == 1 and k == 3
                        if half == 0 and k == 0:
                            ins = q.tensor_scalar(acc, piece[:, k, :], s, None, ALU.mult)
                        else:
                            ins = q.scalar_tensor_tensor(acc, piece[:, k, :], s, acc, ALU.mult, ALU.add)
                        if last:
                            ins.then_inc(s_adaacc, 1)
                        elif k == 3:
                            ins.then_inc(s_adau, 1)
                            dve.wait_ge(s_adau, g + 1)
                        else:
                            own.link(ins)
                ada_out(0, g, 0)

            def rstd(n, width, src):
                q.tensor_scalar(small[:, 1, 0:n], src, 1.0 / width, EPS, ALU.mult, ALU.add).then_inc(s_var, 1)
                std[0] += 1
                dve.wait_ge(s_std, std[0])
                own.link(q.reciprocal(small[:, 0, 0:n], small[:, 2, 0:n]))

            def norm(name, n):
                dve.wait_ge(s_ss, 8 * n + 8)
                rstd(T, D, small[:, 0, 0:T])
                for t in range(T):
                    q.tensor_scalar(arena[:, t * D:(t + 1) * D], xr[:, t, :], small[:, 0, t:t + 1], None,
                                    ALU.mult).then_inc(s_xn, 1)
                for idx, (k, half) in enumerate(ORDER):
                    take_lo(name, idx, k, half, arena[:, 8192 + (idx % 2) * 512:8704 + (idx % 2) * 512])

            def take_lo(name, idx, k, half, src, scale=None):
                dve.wait_ge(s_trh, TR[name] + idx + 1)
                cols = slice(half * 512, (half + 1) * 512)
                if scale is None:
                    ins = q.tensor_tensor(aT[:, 1, k, cols], src, aT[:, 0, k, cols].bitcast(F32), ALU.subtract)
                else:
                    ins = q.scalar_tensor_tensor(aT[:, 1, k, cols], src, scale, aT[:, 0, k, cols].bitcast(F32),
                                                 ALU.mult, ALU.subtract)
                ins.then_inc(s_trl, 1)

            def norm_rope(v, heads, width, gain, half, cols, tiles, scratch, done, squared=None):
                pn, tn = v.shape[0], v.shape[1]
                n = tn * heads
                sqs = scratch[0:pn, 0:n * width].rearrange("p (t h n) -> p t h n", t=tn, h=heads)
                if procs[0]:
                    dve.wait_ge(done, procs[0])
                procs[0] += 1
                if squared is None:
                    own.link(q.tensor_tensor(sqs, v, v, ALU.mult))
                else:
                    dve.wait_ge(s_sq, squared)
                own.link(q.tensor_reduce(small[0:pn, 0, 0:n], sqs, AX.X, ALU.add))
                q.tensor_scalar(small[0:pn, 1, 0:n], small[0:pn, 0, 0:n], 1.0 / width, EPS, ALU.mult,
                                ALU.add).then_inc(s_var, 1)
                std[0] += 1
                dve.wait_ge(s_std, std[0])
                own.link(q.reciprocal(small[0:pn, 0, 0:n], small[0:pn, 2, 0:n]))
                r = small[0:pn, 0, 0:n].rearrange("p (t h) -> p t h", t=tn)
                ins = q.tensor_tensor(v, v, r.unsqueeze(3).broadcast_to([pn, tn, heads, width]), ALU.mult)
                if gain is None:
                    ins.then_inc(done, 1)
                    return
                own.link(ins)
                own_gain = gain[0:pn].unsqueeze(1).unsqueeze(1).broadcast_to([pn, tn, heads, width])
                ins = q.tensor_tensor(v, v, own_gain, ALU.mult)
                if not half:
                    ins.then_inc(done, 1)
                    return
                own.link(ins)
                cos, sin = [rope[0:pn, m, tiles, cols].unsqueeze(2).broadcast_to([pn, tn, heads, half])
                            for m in range(2)]
                x1, x2 = v[:, :, :, 0:half], v[:, :, :, half:2 * half]
                tmp = [scratch[0:pn, m * n * half:(m + 1) * n * half].rearrange("p (t h n) -> p t h n", t=tn, h=heads)
                       for m in range(4)]
                for m, (a, b) in enumerate(((x1, cos), (x2, sin), (x1, sin), (x2, cos))):
                    own.mark(q.tensor_tensor(tmp[m], a, b, ALU.mult))
                own.sync()
                own.link(q.tensor_tensor(x1, tmp[0], tmp[1], ALU.subtract))
                q.tensor_tensor(x2, tmp[2], tmp[3], ALU.add).then_inc(done, 1)

            ada(0)
            ada(1)
            dve.wait_ge(s_x, 16)
            norm("norm0", 0)
            barrier(dve, q, "proj0")
            alltiles = slice(0, T)
            ada(2)
            dve.wait_ge(s_raw, 8)
            norm_rope(raw[:, 0, :, :].rearrange("p t (h n) -> p t h n", h=HEADS), HEADS, DH, gainh[:, 0, :], 8,
                      slice(16, 24), alltiles, arena, s_proc)
            ada(3)
            dve.wait_ge(s_raw, 16)
            norm_rope(raw[:, 1, :, 256:384].rearrange("p t (h n) -> p t h n", h=2), 2, DH, gainh[:, 2, :], 8,
                      slice(16, 24), alltiles, arena, s_proc)
            ada(4)
            dve.wait_ge(s_raw, 24)
            norm_rope(raw[:, 0, :, 0:128].rearrange("p t (h n) -> p t h n", h=2), 2, DH, gainh[:, 3, :], 8,
                      slice(16, 24), alltiles, arena, s_proc)
            dve.wait_ge(s_cond, 3)
            own.link(q.tensor_scalar(gate3[:, :, :], gate3[:, :, :], 1.0, None, ALU.add))
            own.mark(q.reciprocal(gate3[:, :, :], gate3[:, :, :]))
            ada(5)
            dve.wait_ge(s_raw, 32)
            norm_rope(raw[:, 1, :, :].rearrange("p t (h n) -> p t h n", h=2), 2, RANK, None, 0,
                      None, alltiles, arena, s_proc)
            barrier(dve, q, "latent")
            for idx, (k, half) in enumerate([(k, h) for h in range(2) for k in range(4)]):
                take_lo("latent", idx, k, half, ps[:, idx % 8, :], latv[:, k:k + 1])
            barrier(dve, q, "up")
            for hf in range(2):
                q.tensor_copy(upk[hf][:, :, :, 0:32], kpe[:, 4 * hf:4 * hf + 4, :].unsqueeze(2)
                              .broadcast_to([P, 4, HEADS, 32])).then_inc(s_kpe, 1)
            for hf in range(2):
                dve.wait_ge(s_raw, RAW["up"] + 4 * hf + 4)
                norm_rope(upq[hf].rearrange("p t (h n) -> p t h n", h=HEADS), HEADS, MLA_DH, gainq[:, 0, :], 16,
                          slice(0, 16), slice(4 * hf, 4 * hf + 4), arena[:, 8192:11264], s_proc, hf + 1)
            for hf in range(2):
                norm_rope(upk[hf][:, :, :, 0:96], HEADS, MLA_DH, gainq[:, 1, :], 16,
                          slice(0, 16), slice(4 * hf, 4 * hf + 4), arena[:, 8192:11264], s_proc, hf + 3)
            barrier(dve, q, "cmp")
            tt = xres[:, 4096:6144].rearrange("p (a i m) -> p a i m", a=4, i=8)
            blk = arena[:, 4096:8192].rearrange("p (i a m) -> p i a m", i=16, a=4)
            own.mark(q.memset(blk[:, :, :, CMP - 1:CMP], 0.0))
            for a in range(4):
                dve.wait_ge(s_cpe, a + 1)
                own.mark(q.tensor_copy(tt[:, a, :, :], ps[:, a, :].rearrange("p (i m) -> p i m", i=8)))
            own.sync()
            dve.wait_ge(s_cmp, 16 * 6)
            for j in range(2):
                for i in range(16):
                    o = i // 8
                    ins = q.tensor_scalar(blk[:, i, 2 * j:2 * j + 2, 0:CMP - 1], tt[:, 2 * j:2 * j + 2, i % 8, o:o + CMP - 1],
                                          arena[:, 10368 + j * 16 + i:10369 + j * 16 + i], None, ALU.add)
                    if i == 15:
                        ins.then_inc(s_cdve, 1)
            dve.wait_ge(s_cpe, 7)
            own.link(q.tensor_copy(kcv[0:CMP, :, :], ps[0:CMP, 6, 0:256].rearrange("p (a n) -> p a n", a=4)))
            norm_rope(kcv[0:CMP, 0:2, :].unsqueeze(1), 2, DH, gainh[:, 1, :], 8, slice(16, 24), slice(T, T + 1),
                      arena[:, 8448:10240], s_proc)

            own.mark(q.memset(actT[:, NSA_CV:NSA_CV + P].bitcast(F32), 0.0))
            own.mark(q.memset(actT[:, NSA_CV + P:NSA_CV + VW["nsa"]].bitcast(F32), 1.0))
            barrier(dve, q, "mla")

            def attend(name, turn, own_steps, cols, dv, factor, stack_dst, width):
                S = ATT[name]
                U, UT, HT, units, before = S["U"], S["UT"], S["HT"], S["units"], S["before"]
                NF = S["prep"] * TURN

                def maxima(n):
                    u = units[n]
                    dve.wait_ge(S["s_qk"], turn * UT + (n + 1))
                    base = (n % 2) * 1024
                    q.tensor_reduce(rows[:, 0, n % 8:n % 8 + 1], psf[:, base:base + u["n"] * P], AX.X, ALU.max,
                                    negate=True).then_inc(S["s_mx"], 1)

                def take_p(n, half):
                    u = units[n]
                    at = 4 + S["uses"].index(("half", n, half)) % 2
                    w = min(4, u["n"] - 4 * half) * P
                    dve.wait_ge(S["s_ph"], turn * HT + (before[n] + half + 1))
                    at2 = slice(512 * half, 512 * half + w)
                    q.tensor_tensor(pT[:, 1, n % 2, at2], ps[:, at, 0:w], pT[:, 0, n % 2, at2].bitcast(F32),
                                    ALU.subtract).then_inc(S["s_pl"], 1)

                def o_sums(n):
                    total = rows[:, 1, n % 8:n % 8 + 1] if name == "dif" else ps[:, 6 + n % 2, 2 * dv:2 * dv + 1]
                    dve.wait_ge(S["s_pv"], turn * UT + (n + 1 + S["pv0"]))
                    own_steps.mark(q.reciprocal(rows[:, 2, n % 8:n % 8 + 1], total))

                def o_factor(n):
                    f = rows[:, 2, n % 8:n % 8 + 1]
                    for by in factor(units[n]):
                        own_steps.sync()
                        own_steps.mark(q.tensor_tensor(f, f, by, ALU.mult))

                def o_first(n):
                    u = units[n]
                    f, part = rows[:, 2, n % 8:n % 8 + 1], ps[:, 6 + n % 2, 0:dv]
                    dst = xr[:, u["t"], cols(u["head"])]
                    own_steps.sync()
                    if u["add"]:
                        dve.wait_ge(S["s_o"], turn * UT + (n + 1))
                        own_steps.mark(q.scalar_tensor_tensor(dst, part, f, dst, ALU.mult, ALU.add))
                    else:
                        own_steps.mark(q.tensor_scalar(dst, part, f, None, ALU.mult))

                def o_second(n):
                    u = units[n]
                    f, part = rows[:, 2, n % 8:n % 8 + 1], ps[:, 6 + n % 2, dv:2 * dv]
                    dst = xr[:, u["t"], cols(u["head"])]
                    own_steps.sync()
                    q.scalar_tensor_tensor(dst, part, f, dst, ALU.mult, ALU.add).then_inc(S["s_o"], 1)

                for b in range(1, S["prep"], 2):
                    at = 4 + S["uses"].index(("stack", 0, b)) % 2
                    dve.wait_ge(S["s_ftr"], turn * NF + (b + 2))
                    q.tensor_copy(stack_dst(0, b), ps[0:width, at, :]).then_inc(S["s_fevd"], 1)
                maxima(0)
                maxima(1)
                for n in range(UT):
                    if n >= 2:
                        o_sums(n - 2)
                    if n + 2 < UT:
                        maxima(n + 2)
                    if n >= 2:
                        o_factor(n - 2)
                        o_first(n - 2)
                    take_p(n, 0)
                    if units[n]["halves"] == 2:
                        take_p(n, 1)
                    if n >= 2:
                        o_second(n - 2)
                for m in (UT - 2, UT - 1):
                    o_sums(m)
                    o_factor(m)
                    o_first(m)
                    o_second(m)

            for par in range(2):
                v = actT[:, par * 8192 + 4096:par * 8192 + 4096 + T * VW["mla"]].rearrange("p (t n) -> p t n", t=T)
                q.memset(v[:, :, 2 * MLA_V:].bitcast(F32), 1.0).then_inc(s_ones, 1)
            steps = Count(dve, ATT["mla"]["s_own"])
            with dve.Fori(0, TURNS) as turn:
                steps.enter(turn, TURN * 16)
                attend("mla", turn, steps, lambda i: bass.ds((turn * TURN + i) * DH, DH), MLA_V, lambda u: [],
                       stack_slots["mla"], MLA_DH)
            steps.leave(TURN * 16, TURNS)
            barrier(dve, q, "nsa")
            for b in range(2):
                v = actT[:, NSA_V[b]:NSA_V[b] + T * VW["nsa"]].rearrange("p (t n) -> p t n", t=T)
                q.memset(v[:, :, 2 * DH:].bitcast(F32), 1.0).then_inc(s_ones, 1)
            q.memset(arena[:, 5120:5376], 0.0).then_inc(s_ones, 1)
            steps = Count(dve, ATT["nsa"]["s_own"])
            with dve.Fori(0, GROUPS) as g:
                for n in range(4):
                    dve.wait_ge(nsag["s_ftr"], g * 9 + (2 * n + 3))
                    q.tensor_copy(actT[:, n * 1024 + 512:(n + 1) * 1024], ps[:, 2 * n + 1, :]).then_inc(nsag["s_fevd"], 1)
                steps.enter(g, PER_GROUP * 73)

                def factor(u):
                    by = [gate3[:, u["t"], bass.ds(g * PER_GROUP + (u["head"] + 8 * u["factor"]), 1)]]
                    return by + ([valid[:, :]] if u["kind"] == "cmp" and u["t"] == 0 else [])

                attend("nsa", g, steps, lambda i: bass.ds((g * PER_GROUP + i) * DH + 512, DH), DH, factor,
                       stack_slots["nsa"], P)
            steps.leave(PER_GROUP * 73, GROUPS)
            barrier(dve, q, "otr0")


            def residual(name, loads):
                dve.wait_ge(s_x, loads)
                for j in range(2):
                    for t in range(T):
                        if t == T - 1:
                            dve.wait_ge(s_wused, FIRST[name] + 2 * j + 2)
                        else:
                            dve.wait_ge(s_mm, MM[name] + 7 * j + t + 1)
                        dst = xr[:, t, j * 512:(j + 1) * 512]
                        q.tensor_tensor(dst, dst, ps[:, t, :], ALU.add).then_inc(s_raw, 1)

            def mlp(layer):
                first = FIRST[f"mlp{layer}"]
                with dve.Fori(0, FF_GROUPS) as g:
                    if layer == 0:
                        own.enter(g, KD)
                    for idx, (half, f) in enumerate(((0, 0), (0, 1), (1, 0), (1, 1))):
                        dve.wait_ge(s_gr, g * 4 + (layer * 64 + idx + 1))
                        dve.wait_ge(s_gh, g * 4 + (layer * 64 + max(idx - 1, 0) + 1))
                        dve.wait_ge(s_gl, g * 4 + (layer * 64 + max(idx - 1, 0) + 1))
                        q.scalar_tensor_tensor(sq[:, idx % 2, :], ps[:, idx, :], 0.0, relu[:, idx % 2, :],
                                               ALU.max, ALU.mult).then_inc(s_gt, 1)
                        dve.wait_ge(s_gh, g * 4 + (layer * 64 + idx + 2))
                        cols = slice(half * 512, (half + 1) * 512)
                        q.tensor_tensor(gT[:, 1, f, cols], sq[:, idx % 2, :], gT[:, 0, f, cols].bitcast(F32),
                                        ALU.subtract).then_inc(s_gl, 1)
                    for idx in range(16):
                        if idx == 15:
                            dve.wait_ge(s_wused, g * 2 + (first + 2))
                        else:
                            dve.wait_ge(s_y, g * 15 + (layer * 240 + idx + 2))
                        t, n = idx // 2, idx % 2
                        dve.wait_ge(s_ya, g * 16 + (layer * 256 + 1))
                        dst = xr[:, t, n * 512:(n + 1) * 512]
                        q.tensor_tensor(dst, dst, ps[:, 4 + idx % 4, :], ALU.add).then_inc(s_ya, 1)
                        if layer == 0 and idx % 2 == 1:
                            k = idx // 2
                            s = cond[:, 0, k:k + 1]
                            acc = ada_acc[:, bass.ds(g * ADA_COLS, ADA_COLS)]
                            if k == 0:
                                dve.wait_ge(s_adap, g * 32 + 32)
                                own.mark(q.tensor_scalar(acc, ada_piece[:, k, :], s, None, ALU.mult))
                            else:
                                own.sync()
                                own.mark(q.scalar_tensor_tensor(acc, ada_piece[:, k, :], s, acc, ALU.mult, ALU.add))
                    if layer == 0:
                        own.sync()
                        acc = ada_acc[0:1, bass.ds(g * ADA_COLS, ADA_COLS)]
                        q.tensor_tensor(acc, acc, ada_bias, ALU.add).then_inc(s_adad, 1)
                if layer == 0:
                    own.leave(KD, FF_GROUPS)

            for idx, (k, half) in enumerate(ORDER):
                take_lo("otr0", idx, k, half, ps[:, idx % 8, :])
            barrier(dve, q, "out0")
            residual("out0", 32)
            norm("norm1", 1)
            barrier(dve, q, "mlp0")
            mlp(0)
            barrier(dve, q, "ada1")
            for g, bank in enumerate(ADA_BANKS):
                ada_out(1, g, bank)
            dve.wait_ge(s_xs, 16)
            norm("norm2", 2)
            barrier(dve, q, "proj1")
            for j in range(4):
                dve.wait_ge(s_raw, RAW["proj1"] + 8 * (j + 1))
                norm_rope(raw[:, j % 2, :, :].rearrange("p t (h n) -> p t h n", h=HEADS), HEADS, DH,
                          gainh[:, 4 + j // 2, :], 8, slice(16, 24), alltiles, arena, s_proc)
            barrier(dve, q, "dif")
            steps = Count(dve, ATT["dif"]["s_own"])
            with dve.Fori(0, TURNS) as turn:
                steps.enter(turn, TURN * 40)
                attend("dif", turn, steps, lambda i: bass.ds((turn * TURN + i) * 2 * DH, 2 * DH), 2 * DH,
                       lambda u: [lams[:, 6:7]] if u["factor"] else [], stack_slots["dif"], P)
            steps.leave(TURN * 40, TURNS)
            barrier(dve, q, "sub")
            for half in range(2):
                norm_rope(xr[:, 4 * half:4 * half + 4, :].rearrange("p t (h n) -> p t h n", h=HEADS), HEADS, 2 * DH,
                          None, 0, None, None, arena[:, 4096 * half:4096 * half + 4096], s_proc, 5 + half)
                for idx, (k, h) in enumerate(ORDER):
                    if h == half:
                        take_lo("otr1", idx, k, h, ps[:, idx % 8, :], gsub[:, 0:1])
            barrier(dve, q, "out1")
            residual("out1", 48)
            norm("norm3", 3)
            barrier(dve, q, "mlp1")
            mlp(1)
            barrier(dve, q, "end")


_INS = ['x', 'c', 'positions', 'ada_w', 'ada_b', 'norm_mix', 'norm_mlp', 'mlp_w1', 'mlp_w2', 'hy_w_in', 'hy_w_out',
        'mla_q_norm', 'mla_w_uq', 'mla_kv_norm', 'mla_w_ukv', 'mla_q_gain', 'mla_k_gain', 'nsa_q_gain',
        'nsa_k_gain', 'nsa_cmp_pos', 'nsa_cmp_w1', 'nsa_cmp_w2', 'diff_w_qkv', 'diff_w_out', 'diff_q_gain',
        'diff_k_gain', 'diff_lambda', 'diff_sub_gain']


def kernel(**inputs):
    import numpy as _np
    import concourse.bacc as _bacc
    from concourse import mybir as _mybir
    from concourse.bass_utils import run_bass_kernel_spmd as _run

    nc = _bacc.Bacc("TRN2", target_bir_lowering=False, num_devices=1, dynamic_dma_scratch_size=512)
    arrays, args = {}, []
    for name in _INS:
        a = _np.ascontiguousarray(inputs[name])
        arrays[f"in_{name}"] = a
        args.append(nc.dram_tensor(f"in_{name}", a.shape, _mybir.dt.from_np(a.dtype), kind="ExternalInput").ap())
    o = nc.dram_tensor("out_0", inputs["x"].shape, _mybir.dt.float32, kind="ExternalOutput").ap()
    trunk(nc, *args, o)
    r = _run(nc, [arrays], core_ids=[0])
    return r.results[0]["out_0"]
```
